# Optimizing a Trainium2 kernel written in Bass

```python
import jax
import jax.numpy as jnp
from jax import lax
import numpy as np

D_MODEL = 1024
BATCH = 1
SEQ = 256
DEPTH = 2

HEAD_DIM = 64
ROPE_THETA = 10000.0
EPS = 1e-6
Q_BLOCK = 128

A_HEADS = 4
IDX_HEADS = 8
IDX_DIM = 32
TOPK_MAX = 256

B_HEADS = 4
B_NOPE = 64
B_ROPE = 32
B_V = 64
B_Q_RANK = 256
B_KV_RANK = 128

C_HEADS = 8
C_KV_HEADS = 2
WINDOW = 128

D_FF = 2816
N_EXPERTS = 8
TOP_K = 2
EXPERT_FF = 3584
MOE_BLOCK = 256

N_DENSE = (DEPTH + 1) // 2
N_MOE = DEPTH // 2

IN_SIZES = (A_HEADS * HEAD_DIM, HEAD_DIM, HEAD_DIM,
            IDX_HEADS * IDX_DIM, IDX_DIM, IDX_HEADS,
            B_Q_RANK, B_KV_RANK, B_ROPE,
            C_HEADS * HEAD_DIM, C_KV_HEADS * HEAD_DIM, C_KV_HEADS * HEAD_DIM,
            3 * D_MODEL)
D_IN = sum(IN_SIZES)

kernel_name = 'hybrid_dsa_mla_swa_gated_moe'

def rms_norm(x, g):
    xf = x.astype(jnp.float32)
    y = xf * lax.rsqrt(jnp.mean(xf * xf, axis=-1, keepdims=True) + EPS)
    return (y * g.astype(jnp.float32)).astype(x.dtype)

def rope(x, pos):
    half = x.shape[-1] // 2
    inv_freq = ROPE_THETA ** (-jnp.arange(half, dtype=jnp.float32) / half)
    ang = pos.astype(jnp.float32)[:, :, None] * inv_freq
    cos = jnp.cos(ang)[:, :, None, :]
    sin = jnp.sin(ang)[:, :, None, :]
    xf = x.astype(jnp.float32)
    x1, x2 = xf[..., :half], xf[..., half:]
    return jnp.concatenate([x1 * cos - x2 * sin, x2 * cos + x1 * sin], axis=-1).astype(x.dtype)

def to_blocks(x, blk=Q_BLOCK):
    b, s = x.shape[0], x.shape[1]
    return jnp.moveaxis(x.reshape((b, s // blk, blk) + x.shape[2:]), 1, 0)

def from_blocks(y):
    n, b, blk = y.shape[0], y.shape[1], y.shape[2]
    return jnp.moveaxis(y, 0, 1).reshape((b, n * blk) + y.shape[3:])

def split_columns(p):
    cuts = np.cumsum(IN_SIZES)[:-1].tolist()
    return jnp.split(p, cuts, axis=-1)

def dsa_attention(q, k, v, iq, ik, iw):
    s = q.shape[1]
    n_sel = min(TOPK_MAX, s // 4)
    key_pos = jnp.arange(s)

    def block(args):
        qb, iqb, iwb, t = args
        sc = jnp.einsum('bqhd,bsd->bqhs', iqb, ik, preferred_element_type=jnp.float32) * IDX_DIM ** -0.5
        score = jnp.einsum('bqhs,bqh->bqs', jax.nn.relu(sc), iwb.astype(jnp.float32))
        score = jnp.where((key_pos[None, :] <= t[:, None])[None], score, -jnp.inf)
        _, sel = lax.top_k(score, n_sel)
        valid = sel <= t[None, :, None]
        k_g = jax.vmap(lambda kk, ii: kk[ii])(k, sel)
        v_g = jax.vmap(lambda vv, ii: vv[ii])(v, sel)
        logits = jnp.einsum('bqhd,bqkd->bqhk', qb, k_g, preferred_element_type=jnp.float32) * HEAD_DIM ** -0.5
        logits = jnp.where(valid[:, :, None, :], logits, -jnp.inf)
        p = jax.nn.softmax(logits, axis=-1)
        return jnp.einsum('bqhk,bqkd->bqhd', p.astype(v.dtype), v_g)

    t_blocks = jnp.arange(s).reshape(s // Q_BLOCK, Q_BLOCK)
    out = lax.map(block, (to_blocks(q), to_blocks(iq), to_blocks(iw), t_blocks))
    return from_blocks(out)

def mla_attention(q_nope, q_rope, k_nope, k_rope, v):
    s = q_nope.shape[1]
    key_pos = jnp.arange(s)
    scale = (B_NOPE + B_ROPE) ** -0.5

    def block(args):
        qn, qr, t = args
        logits = (jnp.einsum('bqhd,bshd->bhqs', qn, k_nope, preferred_element_type=jnp.float32)
                  + jnp.einsum('bqhr,bsr->bhqs', qr, k_rope, preferred_element_type=jnp.float32)) * scale
        logits = jnp.where(key_pos[None, :] <= t[:, None], logits, -jnp.inf)
        p = jax.nn.softmax(logits, axis=-1)
        return jnp.einsum('bhqs,bshd->bqhd', p.astype(v.dtype), v)

    t_blocks = jnp.arange(s).reshape(s // Q_BLOCK, Q_BLOCK)
    out = lax.map(block, (to_blocks(q_nope), to_blocks(q_rope), t_blocks))
    return from_blocks(out)

def swa_attention(q, k, v, sinks):
    b, s, _, d = q.shape
    g = C_HEADS // C_KV_HEADS
    n = s // WINDOW
    qb = q.reshape(b, n, WINDOW, C_KV_HEADS, g, d)

    def band(x):
        xb = x.reshape(b, n, WINDOW, C_KV_HEADS, d)
        prev = jnp.concatenate([jnp.zeros_like(xb[:, :1]), xb[:, :-1]], axis=1)
        return jnp.concatenate([prev, xb], axis=2)

    kb, vb = band(k), band(v)
    i = jnp.arange(WINDOW)[:, None]
    j = jnp.arange(2 * WINDOW)[None, :]
    in_window = (j > i) & (j <= i + WINDOW)
    sink = sinks.reshape(C_KV_HEADS, g).astype(jnp.float32)[None, :, :, None, None]

    def block(args):
        qn, kn, vn, blk = args
        mask = in_window & (blk * WINDOW - WINDOW + j >= 0)
        logits = jnp.einsum('bqkgd,bskd->bkgqs', qn, kn, preferred_element_type=jnp.float32) * d ** -0.5
        logits = jnp.where(mask, logits, -jnp.inf)
        m = jnp.maximum(jnp.max(logits, axis=-1, keepdims=True), sink)
        p = jnp.exp(logits - m)
        denom = jnp.sum(p, axis=-1, keepdims=True) + jnp.exp(sink - m)
        return jnp.einsum('bkgqs,bskd->bqkgd', (p / denom).astype(v.dtype), vn)

    out = lax.map(block, (jnp.moveaxis(qb, 1, 0), jnp.moveaxis(kb, 1, 0), jnp.moveaxis(vb, 1, 0), jnp.arange(n)))
    return jnp.moveaxis(out, 0, 1).reshape(b, s, C_HEADS, d)

def swiglu(h, w1, w3, w2):
    return (jax.nn.silu(h @ w1) * (h @ w3)) @ w2

def moe_ffn(h, w_router, w1, w3, w2):
    b, s, d = h.shape
    n_tok = b * s
    hf = h.reshape(n_tok, d)
    logits = jnp.matmul(hf, w_router, preferred_element_type=jnp.float32)
    top_logits, top_e = lax.top_k(logits, TOP_K)
    gates = jax.nn.softmax(top_logits, axis=-1)
    n_asg = n_tok * TOP_K
    e_flat = top_e.reshape(n_asg)
    tok_flat = jnp.repeat(jnp.arange(n_tok), TOP_K)
    order = jnp.argsort(e_flat)
    e_s, tok_s = e_flat[order], tok_flat[order]
    gate_s = gates.reshape(n_asg)[order]
    counts = jnp.bincount(e_flat, length=N_EXPERTS)
    padded = (counts + MOE_BLOCK - 1) // MOE_BLOCK * MOE_BLOCK
    start = jnp.cumsum(counts) - counts
    pend = jnp.cumsum(padded)
    pstart = pend - padded
    dest = pstart[e_s] + (jnp.arange(n_asg) - start[e_s])
    n_blocks = -(-n_asg // MOE_BLOCK) + N_EXPERTS
    rows = n_blocks * MOE_BLOCK
    xbuf = jnp.zeros((rows, d), h.dtype).at[dest].set(hf[tok_s])
    block_e = jnp.minimum(jnp.searchsorted(pend, jnp.arange(n_blocks) * MOE_BLOCK, side='right'), N_EXPERTS - 1)

    def expert_block(args):
        xb, e = args
        return swiglu(xb, w1[e], w3[e], w2[e])

    ybuf = lax.map(expert_block, (xbuf.reshape(n_blocks, MOE_BLOCK, d), block_e)).reshape(rows, d)
    y_s = ybuf[dest] * gate_s[:, None].astype(h.dtype)
    out = jax.ops.segment_sum(y_s, tok_s, num_segments=n_tok)
    return out.reshape(b, s, d)

def setup_inputs(seed: int = 0) -> dict:
    key = jax.random.key(seed)
    ks = jax.random.split(key, 29)

    def w(k, shape, fan_in):
        return jax.random.normal(k, shape, jnp.float32) * fan_in ** -0.5

    def gain(k, shape):
        return 1.0 + 0.1 * jax.random.normal(k, shape, jnp.float32)

    b_qk = B_HEADS * (B_NOPE + B_ROPE)
    b_kv = B_HEADS * (B_NOPE + B_V)
    return {
        'x': jax.random.normal(ks[0], (BATCH, SEQ, D_MODEL), jnp.float32),
        'positions': (jnp.arange(SEQ, dtype=jnp.int32)[None, :]
                      + jax.random.randint(ks[1], (BATCH, 1), 0, 4096, dtype=jnp.int32)),
        'attn_norm_g': gain(ks[2], (DEPTH, D_MODEL)),
        'w_in': w(ks[3], (DEPTH, D_MODEL, D_IN), D_MODEL),
        'a_q_norm_g': gain(ks[4], (DEPTH, HEAD_DIM)),
        'a_k_norm_g': gain(ks[5], (DEPTH, HEAD_DIM)),
        'b_cq_norm_g': gain(ks[6], (DEPTH, B_Q_RANK)),
        'b_ckv_norm_g': gain(ks[7], (DEPTH, B_KV_RANK)),
        'b_w_uq': w(ks[8], (DEPTH, B_Q_RANK, b_qk), B_Q_RANK),
        'b_w_ukv': w(ks[9], (DEPTH, B_KV_RANK, b_kv), B_KV_RANK),
        'b_qn_g': gain(ks[10], (DEPTH, B_NOPE)),
        'b_qr_g': gain(ks[11], (DEPTH, B_ROPE)),
        'b_kn_g': gain(ks[12], (DEPTH, B_NOPE)),
        'b_kr_g': gain(ks[13], (DEPTH, B_ROPE)),
        'c_q_norm_g': gain(ks[14], (DEPTH, HEAD_DIM)),
        'c_k_norm_g': gain(ks[15], (DEPTH, HEAD_DIM)),
        'c_sinks': 0.5 * jax.random.normal(ks[16], (DEPTH, C_HEADS), jnp.float32),
        'w_a_out': w(ks[17], (DEPTH, A_HEADS * HEAD_DIM, D_MODEL), A_HEADS * HEAD_DIM),
        'w_b_out': w(ks[18], (DEPTH, B_HEADS * B_V, D_MODEL), B_HEADS * B_V),
        'w_c_out': w(ks[19], (DEPTH, C_HEADS * HEAD_DIM, D_MODEL), C_HEADS * HEAD_DIM),
        'w_o': w(ks[20], (DEPTH, D_MODEL, D_MODEL), D_MODEL),
        'ffn_norm_g': gain(ks[21], (DEPTH, D_MODEL)),
        'ffn_w1': w(ks[22], (N_DENSE, D_MODEL, D_FF), D_MODEL),
        'ffn_w3': w(ks[23], (N_DENSE, D_MODEL, D_FF), D_MODEL),
        'ffn_w2': w(ks[24], (N_DENSE, D_FF, D_MODEL), D_FF),
        'router_w': w(ks[25], (N_MOE, D_MODEL, N_EXPERTS), D_MODEL),
        'moe_w1': w(ks[26], (N_MOE, N_EXPERTS, D_MODEL, EXPERT_FF), D_MODEL),
        'moe_w3': w(ks[27], (N_MOE, N_EXPERTS, D_MODEL, EXPERT_FF), D_MODEL),
        'moe_w2': w(ks[28], (N_MOE, N_EXPERTS, EXPERT_FF, D_MODEL), EXPERT_FF),
    }

def reference(x, positions, attn_norm_g, w_in, a_q_norm_g, a_k_norm_g, b_cq_norm_g, b_ckv_norm_g,
              b_w_uq, b_w_ukv, b_qn_g, b_qr_g, b_kn_g, b_kr_g, c_q_norm_g, c_k_norm_g, c_sinks,
              w_a_out, w_b_out, w_c_out, w_o, ffn_norm_g, ffn_w1, ffn_w3, ffn_w2,
              router_w, moe_w1, moe_w3, moe_w2):
    b, s, _ = x.shape
    for l in range(DEPTH):
        h = rms_norm(x, attn_norm_g[l])
        proj = h @ w_in[l]
        qa, ka, va, iq, ik, iw, cq, ckv, kr, qc, kc, vc, gates = split_columns(proj)

        qa = rope(rms_norm(qa.reshape(b, s, A_HEADS, HEAD_DIM), a_q_norm_g[l]), positions)
        ka = rope(rms_norm(ka[:, :, None, :], a_k_norm_g[l]), positions)[:, :, 0]
        iq = rope(iq.reshape(b, s, IDX_HEADS, IDX_DIM), positions)
        ik = rope(ik[:, :, None, :], positions)[:, :, 0]
        ya = dsa_attention(qa, ka, va, iq, ik, iw * IDX_HEADS ** -0.5)

        q_b = (rms_norm(cq, b_cq_norm_g[l]) @ b_w_uq[l]).reshape(b, s, B_HEADS, B_NOPE + B_ROPE)
        kv_b = (rms_norm(ckv, b_ckv_norm_g[l]) @ b_w_ukv[l]).reshape(b, s, B_HEADS, B_NOPE + B_V)
        q_nope = rms_norm(q_b[..., :B_NOPE], b_qn_g[l])
        q_rope = rope(rms_norm(q_b[..., B_NOPE:], b_qr_g[l]), positions)
        k_nope = rms_norm(kv_b[..., :B_NOPE], b_kn_g[l])
        v_b = kv_b[..., B_NOPE:]
        k_rope = rope(rms_norm(kr[:, :, None, :], b_kr_g[l]), positions)[:, :, 0]
        yb = mla_attention(q_nope, q_rope, k_nope, k_rope, v_b)

        qc = rope(rms_norm(qc.reshape(b, s, C_HEADS, HEAD_DIM), c_q_norm_g[l]), positions)
        kc = rope(rms_norm(kc.reshape(b, s, C_KV_HEADS, HEAD_DIM), c_k_norm_g[l]), positions)
        vc = vc.reshape(b, s, C_KV_HEADS, HEAD_DIM)
        yc = swa_attention(qc, kc, vc, c_sinks[l])

        ga, gb, gc = jnp.split(jax.nn.sigmoid(gates), 3, axis=-1)
        merged = (ga * (ya.reshape(b, s, -1) @ w_a_out[l])
                  + gb * (yb.reshape(b, s, -1) @ w_b_out[l])
                  + gc * (yc.reshape(b, s, -1) @ w_c_out[l]))
        x = x + merged @ w_o[l]

        h2 = rms_norm(x, ffn_norm_g[l])
        if l % 2 == 0:
            x = x + swiglu(h2, ffn_w1[l // 2], ffn_w3[l // 2], ffn_w2[l // 2])
        else:
            x = x + moe_ffn(h2, router_w[l // 2], moe_w1[l // 2], moe_w3[l // 2], moe_w2[l // 2])
    return x


_drawn_inputs = setup_inputs


def setup_inputs(seed=0):
    import zlib

    import numpy as np

    out = dict(_drawn_inputs(seed))
    spreads = {}
    factors = {'b_kr_g': 2.945, 'c_sinks': 4.923}
    for name, (base, spread) in spreads.items():
        noise = np.random.default_rng([zlib.crc32(name.encode()), seed]).standard_normal(out[name].shape)
        drawn = base * np.exp(spread * noise) if base else spread * noise
        out[name] = jnp.asarray(drawn.astype(out[name].dtype))
    for name, factor in factors.items():
        out[name] = (out[name] * factor).astype(out[name].dtype)
    return out
```

```python
from contextlib import ExitStack

import numpy as np

import concourse.bass as bass
from concourse import mybir

F32 = mybir.dt.float32
I32 = mybir.dt.int32
U32 = mybir.dt.uint32
ALU = mybir.AluOpType
ACT = mybir.ActivationFunctionType
AX_X = mybir.AxisListType.X

P = 128
D_MODEL, SEQ, DEPTH = 1024, 256, 2
T = SEQ // P
KC = D_MODEL // P
HEAD, IDX_DIM, IDX_HEADS = 64, 32, 8
TOPK = min(256, SEQ // 4)
A_HEADS, B_HEADS, C_HEADS, C_KV = 4, 4, 8, 2
B_NOPE, B_ROPE, B_V, B_QR, B_KVR = 64, 32, 64, 256, 128
D_FF, N_EXP, E_FF = 2816, 8, 3584
EPS = 1e-6

SIZES = dict(qa=256, ka=64, va=64, iq=256, ik=32, iw=8, cq=256, ckv=128, kr=32, qc=512, kc=128, vc=128)
COL, ATT = {}, 0
for _name, _size in SIZES.items():
    COL[_name] = ATT
    ATT += _size
W = 512
ATT_GROUPS = [(g * W, min(W, ATT - g * W)) for g in range(-(-ATT // W))]
GATE_GROUPS = 3 * D_MODEL // W

MASKED, REMOVED = -1e30, -3e38

UNIT, SLOTS = 2048, 7
E_GROUPS = E_FF // W
E_CHUNKS = E_FF // P
E_UNITS = 4 * E_GROUPS + E_CHUNKS // 2
FF_GROUPS = [(j * W, min(W, D_FF - j * W)) for j in range(-(-D_FF // W))]
FF_CHUNKS = D_FF // P

MIXERS = ["c0", "c1", "b", "a"]
JOBS = [(m, t) for m in MIXERS for t in range(T)]
Y_COL = dict(a=0, b=256, c0=512, c1=768)
SCALE = dict(a=HEAD ** -0.5, b=(B_NOPE + B_ROPE) ** -0.5, c0=HEAD ** -0.5, c1=HEAD ** -0.5)


class BankRing:

    def __init__(self, taken_by):
        self.taken_by, self.order, self.index = taken_by, [], {}

    def add(self, name, reader):
        self.index[name] = len(self.order)
        self.order.append(reader)

    def no(self, name):
        return self.index[name] + 1

    def bank(self, name):
        return self.index[name] % 4

    def count(self, i):
        reader = self.order[i]
        return self.taken_by[reader], self.order[:i + 1].count(reader)

    def taken(self, name):
        return self.count(self.index[name])

    def free(self, name):
        i = self.index[name]
        return self.count(i - 4) if i >= 4 else None


def plan_units(w):
    units = []

    def columns(name, src, c0, n, chunks):
        v = src.rearrange("(c p) n -> p c n", p=P)
        per = UNIT // n if n >= 256 else chunks
        per = min(per, chunks)
        if n > 256:
            per = 4
        for h in range(chunks // per):
            units.append((name + (h,), v[:, h * per:(h + 1) * per, c0:c0 + n], (per, n)))

    def rows(name, src, chunks):
        v = src.rearrange("(c p) n -> p c n", p=P)
        for h in range(chunks // 2):
            units.append((name + (h,), v[:, 2 * h:2 * h + 2, :], (2, D_MODEL)))

    for l in range(DEPTH):
        for g, (c0, n) in enumerate(ATT_GROUPS):
            columns(("p", l, g), w["w_in"][l], c0, n, KC)
        for g in range(GATE_GROUPS):
            columns(("g", l, g), w["w_in"][l], ATT + g * W, W, KC)
        rows(("wa", l), w["w_a_out"][l], 2)
        rows(("wb", l), w["w_b_out"][l], 2)
        rows(("wc", l), w["w_c_out"][l], 4)
        rows(("wo", l), w["w_o"][l], KC)
        if l == 0:
            for j, (c0, n) in enumerate(FF_GROUPS):
                columns(("w1", j), w["ffn_w1"][0], c0, n, KC)
                columns(("w3", j), w["ffn_w3"][0], c0, n, KC)
            rows(("w2",), w["ffn_w2"][0], FF_CHUNKS)
    return units


def hybrid_layers(nc, w, out, stop=None):
    with ExitStack() as ctx:
        def sb(name, shape, dt=F32):
            return ctx.enter_context(nc.sbuf_tensor(name, shape, dt))

        def sem(name):
            return ctx.enter_context(nc.semaphore(name))

        consts_loaded = sem("consts_loaded")
        mla_loaded = sem("mla_loaded")
        unit_loaded = [sem(f"unit_loaded{i}") for i in range(SLOTS)]
        unit_used = sem("unit_used")
        acc_ready, aux_ready = sem("acc_ready"), sem("aux_ready")
        acc_taken = dict(act=sem("acc_taken_by_act"), dve=sem("acc_taken_by_dve"))
        aux_taken = dict(act=sem("aux_taken_by_act"), dve=sem("aux_taken_by_dve"))
        pool_step = sem("pool_step")
        masks_ready = sem("masks_ready")
        mean_ready = sem("mean_ready")
        rstd_ready = sem("rstd_ready")
        dve_step = sem("dve_step")
        act_step = sem("act_step")
        angles_ready = sem("angles_ready")
        trig_ready = sem("trig_ready")
        normed = sem("normed")
        lowrank_ready = sem("lowrank_ready")
        roped_a = sem("roped_a")
        roped_c = sem("roped_c")
        mla_heads_ready = sem("mla_heads_ready")
        relu_used = sem("relu_used")
        relu_ready = sem("relu_ready")
        logits_ready = sem("logits_ready")
        probs_ready = sem("probs_ready")
        merged_ready = sem("merged_ready")
        silu_ready = sem("silu_ready")
        hidden_ready = sem("hidden_ready")
        routed = sem("routed")
        passes_ready = sem("passes_ready")
        onehot_ready = sem("onehot_ready")
        e_silu, e_hidden = sem("expert_silu"), sem("expert_hidden")
        x_done = sem("x_done")
        stored = sem("stored")

        acc_bank = [ctx.enter_context(nc.psum_tensor(f"acc{i}", [P, W], F32)) for i in range(4)]
        aux_bank = [ctx.enter_context(nc.psum_tensor(f"aux{i}", [P, W], F32)) for i in range(4)]

        ring = sb("ring", [P, SLOTS, UNIT])
        x_sb = sb("x_sb", [P, T, D_MODEL])
        xn = sb("xn", [P, T, D_MODEL])
        hT = sb("hT", [P, KC, SEQ])
        yT = sb("yT", [P, KC, SEQ])
        proj = sb("proj", [P, T, ATT])
        gates = sb("gates", [P, T, 3 * D_MODEL])
        swing = sb("swing", [P, 1280])
        logit = sb("logit", [P, 2, 4, SEQ])
        probT = sb("probT", [P, 2, 8, P])
        qcT, kcz = sb("qcT", [P, 4, SEQ]), sb("kcz", [P, C_KV, 2, SEQ])
        cqT, iqT = qcT[:, 0:2, :], qcT[:, 2:4, :]
        qaT, kaz = sb("qaT", [P, 2, SEQ]), sb("kaz", [P, 2, SEQ])
        ikz = sb("ikz", [P, 4, SEQ])
        qbT, kbT = sb("qbT", [P, B_HEADS, SEQ]), sb("kbT", [P, B_HEADS, SEQ])
        ckvT = sb("ckvT", [P, SEQ])
        kc2, ka2, ik4 = sb("kc2", [P, T, C_KV, P]), sb("ka2", [P, T, P]), sb("ik4", [P, T, P])
        qb, kvb = sb("qb", [P, T, 384]), sb("kvb", [P, T, 512])
        kcat = sb("kcat", [P, T, B_HEADS, 96])
        uq, ukv = sb("uq", [P, 2, 384]), sb("ukv", [P, 512])
        selmask = sb("selmask", [P, T, SEQ])
        ident = sb("ident", [P, P])
        cmask, wmask = sb("cmask", [P, SEQ]), sb("wmask", [P, SEQ])
        gain_rows, gainT = sb("gain_rows", [64, P]), sb("gainT", [P, 64])
        GAINS = dict(aq=(0, 64), ak=(64, 64), qn=(128, 64), qr=(192, 32), kn=(224, 64), kr=(288, 32),
                     cq=(320, 64), ck=(384, 64), sink=(448, 8))
        gains = sb("gains", [P, DEPTH, 456])
        pos_i, pos_f = sb("pos_i", [P, T], I32), sb("pos_f", [P, T])
        freq = sb("freq", [P, 32])
        ang = sb("ang", [P, 4, T, 32])
        score = ang[:, :, :, :].rearrange("p a t d -> p (a t d)")
        trig = sb("trig", [P, 2, T, 32])
        cos64, sin64 = sb("cos64", [P, T, 64]), sb("sin64", [P, T, 64])
        cos32, sin32 = sb("cos32", [P, T, 32]), sb("sin32", [P, T, 32])
        NST = 18 + 12
        invn = sb("invn", [P, NST])
        stat, rstd = sb("stat", [P, T, NST]), sb("rstd", [P, T, NST])
        minus_half = sb("minus_half", [P, T * NST])
        xstat, xrstd = sb("xstat", [P, T]), sb("xrstd", [P, T])
        iws = sb("iws", [P, T, IDX_HEADS])
        top8 = sb("top8", [P, 8])
        nmax, denom = sb("nmax", [P, 2, 4]), sb("denom", [P, 4, 4])
        sinkx, rden = sb("sinkx", [P, 4, 2, 4]), sb("rden", [P, 4, 4])
        wr = sb("wr", [P, KC, N_EXP])
        rl, rtop, ridx = sb("rl", [P, T, 8]), sb("rtop", [P, T, 8]), sb("ridx", [P, T, 8], U32)
        ridxf, iota8 = sb("ridxf", [P, T, 8]), sb("iota8", [P, 8])
        gate2, onehot = sb("gate2", [P, T, 2]), sb("onehot", [P, T, 2, 8])
        chosen, gated = sb("chosen", [P, T, 8]), sb("gated", [P, T, 8])
        lower, ones = sb("lower", [P, P]), sb("ones", [P, P])
        slot_of = sb("slot_of", [P, T, 2, 8])
        n_pass = sb("n_pass", [P, 1], I32)
        cnt = sb("cnt", [P, 4])
        iota_slot = sb("iota_slot", [P, P])
        pick, pickg = (qbT[:, i, :].rearrange("p (t n) -> p t n", n=P) for i in range(2))

        flat = lambda b, k: b[:, :, :].rearrange("p a b -> p (a b)")[:, 0:k]
        ffT = flat(gates, FF_CHUNKS * SEQ).rearrange("p (c n) -> p c n", n=SEQ)
        hidT = flat(gates, E_CHUNKS * P).rearrange("p (c n) -> p c n", n=P)
        ysb = flat(gates, E_CHUNKS * P + D_MODEL)[:, E_CHUNKS * P:]
        pickT = flat(gates, E_CHUNKS * P + D_MODEL + SEQ)[:, E_CHUNKS * P + D_MODEL:]\
            .rearrange("p (t n) -> p t n", n=P)
        silu = logit[:, :, :, :].rearrange("p a b c -> p a (b c)")
        hidden = probT[:, :, :, :].rearrange("p a b c -> p a (b c)")
        xgT = yT[:, 0:4, :].rearrange("p a b -> p (a b)").rearrange("p (c n) -> p c n", n=P)
        sq = yT[:, :, :].rearrange("p a b -> p (a b)")

        acc, aux = BankRing(acc_taken), BankRing(aux_taken)
        for l in range(DEPTH):
            for g in range(len(ATT_GROUPS)):
                for t in range(T):
                    acc.add(("p", l, g, t), "act")
            for g in range(GATE_GROUPS):
                for t in range(T):
                    acc.add(("g", l, g, t), "act")
            for m in "abc":
                for t in range(T):
                    for h in range(2):
                        acc.add(("m", l, m, t, h), "dve")
            for t in range(T):
                for h in range(2):
                    acc.add(("o", l, t, h), "dve")
            if l == 0:
                for j in range(len(FF_GROUPS)):
                    for t in range(T):
                        acc.add(("h1", j, t), "act")
                    for t in range(T):
                        acc.add(("h3", j, t), "dve")
                for t in range(T):
                    for h in range(2):
                        acc.add(("y", t, h), "dve")
        aux.add(("gains",), "act")
        for l in range(DEPTH):
            for i in range(4):
                aux.add(("h", l, i), "act")
            for n in ("cq", "ckv", "ika", "iq", "qa"):
                aux.add((n, l), "act")
            for n in ("uq", "ukv"):
                for t in range(T):
                    aux.add((n, l, t), "act")
            for t in range(T):
                for i in range(2 * (t + 1)):
                    aux.add(("ix", l, t, i), "act")
            for n in ("kc", "qc0", "qc1", "qb0", "qb1", "kb0", "kb1"):
                aux.add((n, l), "act")
            for s in range(len(JOBS) + 2):
                if s < len(JOBS):
                    for i in range(JOBS[s][1] + 1):
                        aux.add(("lg", l, s, i), "dve")
                if 1 <= s <= len(JOBS):
                    for i in range(JOBS[s - 1][1] + 1):
                        aux.add(("pt", l, s - 1, i), "act")
                if s >= 2:
                    aux.add(("pv", l, s - 2), "dve")
            for i in range(4):
                aux.add(("yt", l, i), "act")
            for i in range(4):
                aux.add(("mt", l, i), "act")
            for i in range(4):
                aux.add(("f", l, i), "act")
            if l == 0:
                for j in range(len(FF_GROUPS)):
                    for t in range(T):
                        aux.add(("ht", j, t), "act")
        aux.add(("router", 0), "act")
        aux.add(("router", 1), "act")
        aux.add(("slots",), "dve")
        ACC0, AUX0 = len(acc.order), len(aux.order)
        E_ACC = ["act", "dve"] * E_GROUPS + ["act", "act"]
        E_AUX = ["act"] * 5 + ["act"] * E_GROUPS + ["dve"] * 4
        assert len(E_ACC) % 4 == 0 and len(E_AUX) % 4 == 0

        units = plan_units(w)
        UNITS0 = len(units)
        unit_no = {name: n for n, (name, _, _) in enumerate(units)}
        shape_of = {name: s for name, _, s in units}

        def slot(n, shape):
            return ring[:, n % SLOTS, 0:shape[0] * shape[1]].rearrange("p (c n) -> p c n", n=shape[1])

        def unit(name):
            return slot(unit_no[name], shape_of[name])

        def arrived(name):
            n = unit_no[name]
            return unit_loaded[n % SLOTS], 16 * (n // SLOTS + 1)

        ends_fill = {}
        for l in range(DEPTH):
            for g in range(len(ATT_GROUPS)):
                ends_fill["p", l, g, 1] = ("p", l, g, 1)
            for g in range(GATE_GROUPS):
                ends_fill["g", l, g, 1] = ("g", l, g, 1)
            ends_fill["wa", l, 0] = ("m", l, "a", 1, 1)
            ends_fill["wb", l, 0] = ("m", l, "b", 1, 1)
            ends_fill["wc", l, 1] = ("m", l, "c", 1, 1)
            ends_fill["wo", l, 3] = ("o", l, 1, 1)
        for j, (_, n) in enumerate(FF_GROUPS):
            last = 1 if n > 256 else 0
            ends_fill["w1", j, last] = ("h1", j, 1)
            ends_fill["w3", j, last] = ("h3", j, 1)
        ends_fill["w2", FF_CHUNKS // 2 - 1] = ("y", 1, 1)
        own = [n for n, (name, _, _) in enumerate(units) if name not in ends_fill]
        assert all(name in unit_no for name in ends_fill)
        OWN0 = len(own)

        def released(n):
            name = units[n][0]
            if name in ends_fill:
                return acc_ready, acc.no(ends_fill[name])
            return unit_used, own.index(n) + 1

        E_OWN = [u for u in range(E_UNITS) if not ((u < 4 * E_GROUPS and u % 2) or u == E_UNITS - 1)]

        def e_released(u, it):
            if u in E_OWN:
                return unit_used, it * len(E_OWN) + (OWN0 + E_OWN.index(u) + 1)
            fill = u // 2 + 1 if u < 4 * E_GROUPS else len(E_ACC)
            return acc_ready, it * len(E_ACC) + (ACC0 + fill)

        def e_arrived(u, it):
            n = UNITS0 + u
            return unit_loaded[n % SLOTS], it * (16 * (E_UNITS // SLOTS)) + 16 * (n // SLOTS + 1)

        def e_free(ring0, order, i, it):
            base = {r: ring0[1].order.count(r) for r in ("act", "dve")}
            if i >= 4:
                r = order[i - 4]
                return ring0[1].taken_by[r], it * order.count(r) + (base[r] + order[:i - 3].count(r))
            r = order[i - 4]
            return ring0[1].taken_by[r], it * order.count(r) + (base[r] - order[len(order) + i - 3:].count(r))

        def e_taken(ring0, order, i, it):
            r = order[i]
            base = ring0[1].order.count(r)
            return ring0[1].taken_by[r], it * order.count(r) + (base + order[:i + 1].count(r))

        ACCR, AUXR = (ACC0, acc), (AUX0, aux)
        X0, PG, HT0, CB0 = 0, 4, 5, 5 + E_GROUPS

        def rows_of(name, l, n):
            return w[name][l].rearrange("(c p) -> c p", p=P), n // P
        small = []
        r = 0
        GROW = {}
        for name, n in (("attn_norm_g", D_MODEL), ("ffn_norm_g", D_MODEL), ("b_cq_norm_g", B_QR), ("b_ckv_norm_g", B_KVR)):
            k = DEPTH * n // P
            small.append((gain_rows[r:r + k, :], w[name].rearrange("l (c p) -> (l c) p", p=P)))
            for l in range(DEPTH):
                GROW[name, l] = r + l * n // P
            r += k
        NROWS = r
        for key, name in (("aq", "a_q_norm_g"), ("ak", "a_k_norm_g"), ("qn", "b_qn_g"), ("qr", "b_qr_g"), ("kn", "b_kn_g"),
                          ("kr", "b_kr_g"), ("cq", "c_q_norm_g"), ("ck", "c_k_norm_g"), ("sink", "c_sinks")):
            o, n = GAINS[key]
            small.append((gains[:, :, o:o + n], w[name].partition_broadcast(P)))
        small.append((pos_i[:, :], w["positions"].rearrange("b (t p) -> p (b t)", p=P)))
        small.append((wr[:, :, :], w["router_w"][0].rearrange("(c p) e -> p c e", p=P)))
        x_view = w["x"].rearrange("b (t p) d -> p (b t) d", p=P)
        out_view = out.rearrange("b (t p) d -> p (b t) d", p=P)
        small.append((x_sb[:, :, :], x_view))
        CONSTS = 16 * len(small)

        def gain(key, l, heads):
            o, n = GAINS[key]
            return gains[:, l:l + 1, o:o + n].unsqueeze(1).to_broadcast([P, T, heads, n])

        def heads_of(buf, c0, heads, d):
            return buf[:, :, c0:c0 + heads * d].rearrange("p t (h d) -> p t h d", d=d)

        block = ctx.enter_context(nc.Block())

        @block.scalar
        def _(act):
            steps = [0]

            def link(ins):
                steps[0] += 1
                ins.then_inc(act_step, 1)
                act.wait_ge(act_step, steps[0])

            for dst, src in small:
                act.dma_start(dst, src, allow_slow_non_contiguous=(dst.dtype == I32)).then_inc(consts_loaded, 16)

            def take_aux(name, dst, src=None, func=ACT.Copy, **kw):
                act.wait_ge(aux_ready, aux.no(name))
                b = aux_bank[aux.bank(name)]
                return act.activation(dst, b[:, :] if src is None else src(b), func, **kw).then_inc(aux_taken["act"], 1)

            take_aux(("gains",), gainT[:, 0:NROWS], lambda b: b[:, 0:NROWS])
            act.wait_ge(angles_ready, 1)
            act.activation(trig[:, :, :, :], ang[:, 2:4, :, :], ACT.Sin).then_inc(trig_ready, 1)

            def take_transposed(kind, l, row):
                for i in range(4):
                    act.wait_ge(aux_ready, aux.no((kind, l, i)))
                    b = aux_bank[aux.bank((kind, l, i))]
                    for c in range(2):
                        ins = act.activation(hT[:, 2 * i + c, :], b[:, c * SEQ:(c + 1) * SEQ], ACT.Copy,
                                             scale=gainT[:, row + 2 * i + c:row + 2 * i + c + 1])
                    ins.then_inc(aux_taken["act"], 1)

            for l in range(DEPTH):
                act.wait_ge(*aux.taken(("gains",)))
                take_transposed("h", l, GROW["attn_norm_g", l])
                for g, (c0, n) in enumerate(ATT_GROUPS):
                    for t in range(T):
                        act.wait_ge(acc_ready, acc.no(("p", l, g, t)))
                        act.activation(proj[:, t, c0:c0 + n], acc_bank[acc.bank(("p", l, g, t))][:, 0:n], ACT.Copy)\
                           .then_inc(acc_taken["act"], 1)

                def take_gate(i):
                    g, t = i // 2, i % 2
                    act.wait_ge(acc_ready, acc.no(("g", l, g, t)))
                    act.activation(gates[:, t, g * W:(g + 1) * W], acc_bank[acc.bank(("g", l, g, t))][:, :],
                                   ACT.Exp, scale=-1.0).then_inc(acc_taken["act"], 1)

                take_gate(0)
                take_gate(1)
                act.wait_ge(aux_ready, aux.no(("cq", l)))
                b, r = aux_bank[aux.bank(("cq", l))], GROW["b_cq_norm_g", l]
                for c in range(2):
                    ins = act.activation(cqT[:, c, :], b[:, c * SEQ:(c + 1) * SEQ], ACT.Copy, scale=gainT[:, r + c:r + c + 1])
                ins.then_inc(aux_taken["act"], 1)
                r = GROW["b_ckv_norm_g", l]
                take_aux(("ckv", l), ckvT[:, :], lambda b: b[:, 0:SEQ], scale=gainT[:, r:r + 1])
                act.wait_ge(aux_ready, aux.no(("ika", l)))
                b = aux_bank[aux.bank(("ika", l))]
                for v in range(2):
                    act.activation(kaz[64 * v:64 * v + 64, v, :], b[64 * v:64 * v + 64, 0:SEQ], ACT.Copy)
                for v in range(4):
                    ins = act.activation(ikz[32 * v:32 * v + 32, v, :], b[32 * v:32 * v + 32, SEQ:2 * SEQ], ACT.Copy)
                ins.then_inc(aux_taken["act"], 1)
                take_aux(("iq", l), iqT[:, :, :].rearrange("p a b -> p (a b)"))
                take_aux(("qa", l), qaT[:, :, :].rearrange("p a b -> p (a b)"))
                take_gate(2)
                for t in range(T):
                    take_aux(("uq", l, t), qb[:, t, :], lambda b: b[:, 0:384])
                for t in range(T):
                    take_aux(("ukv", l, t), kvb[:, t, :])
                n = 0
                act.wait_ge(roped_c, l + 1)
                for t in range(T):
                    for i in range(2 * (t + 1)):
                        k = 6 * l + n
                        if n >= 2:
                            act.wait_ge(relu_used, k - 1)
                        act.wait_ge(aux_ready, aux.no(("ix", l, t, i)))
                        act.activation(swing[:, (n % 2) * W:(n % 2 + 1) * W], aux_bank[aux.bank(("ix", l, t, i))][:, :],
                                       ACT.Relu).then_inc(aux_taken["act"], 1)
                        n += 1
                take_gate(3)
                act.wait_ge(aux_ready, aux.no(("kc", l)))
                b = aux_bank[aux.bank(("kc", l))]
                for kv in range(C_KV):
                    for v in range(2):
                        ins = act.activation(kcz[64 * v:64 * v + 64, kv, v, :],
                                             b[64 * v:64 * v + 64, kv * SEQ:(kv + 1) * SEQ], ACT.Copy)
                ins.then_inc(aux_taken["act"], 1)
                for i in range(2):
                    take_aux((f"qc{i}", l), qcT[:, 2 * i:2 * i + 2, :].rearrange("p a b -> p (a b)"))
                for nm, dst in (("qb", qbT), ("kb", kbT)):
                    for i in range(2):
                        take_aux((f"{nm}{i}", l), dst[0:96, 2 * i:2 * i + 2, :].rearrange("p a b -> p (a b)"),
                                 lambda b: b[0:96, :])
                take_gate(4)
                take_gate(5)
                for s in range(len(JOBS) + 2):
                    if s < len(JOBS):
                        m, t = JOBS[s]
                        nk, job = P * (t + 1), len(JOBS) * l + s
                        act.wait_ge(logits_ready, job + 1)
                        if m[0] == "c":
                            act.activation(sinkx[:, s % 4, 1, :], sinkx[:, s % 4, 0, :], ACT.Exp)
                        for h in range(4):
                            row = logit[:, s % 2, h, 0:nk]
                            ins = act.activation(row, row, ACT.Exp, bias=nmax[:, s % 2, h:h + 1],
                                                 accum_out=denom[:, s % 4, h:h + 1])
                        ins.then_inc(probs_ready, 1)
                    if s < 6:
                        take_gate(6 + s)
                    if 1 <= s <= len(JOBS):
                        q, tq = s - 1, JOBS[s - 1][1]
                        if q >= 2:
                            act.wait_ge(aux_ready, aux.no(("pv", l, q - 2)))
                        for i in range(tq + 1):
                            take_aux(("pt", l, q, i), probT[:, q % 2, 4 * i:4 * i + 4, :].rearrange("p a b -> p (a b)"))
                for i in range(4):
                    take_aux(("yt", l, i), yT[:, 2 * i:2 * i + 2, :].rearrange("p a b -> p (a b)"))
                act.wait_ge(acc_ready, acc.no(("g", l, GATE_GROUPS - 1, T - 1)))
                for i in range(4):
                    take_aux(("mt", l, i), hT[:, 2 * i:2 * i + 2, :].rearrange("p a b -> p (a b)"))
                act.wait_ge(acc_ready, acc.no(("o", l, 1, 1)))
                take_transposed("f", l, GROW["ffn_norm_g", l])
                if l == 0:
                    def take_hidden(j):
                        n = FF_GROUPS[j][1]
                        for t in range(T):
                            act.wait_ge(aux_ready, aux.no(("ht", j, t)))
                            b = aux_bank[aux.bank(("ht", j, t))]
                            act.activation(ffT[:, 4 * j:4 * j + n // P, t * P:(t + 1) * P],
                                           b[:, 0:n].rearrange("p (c n) -> p c n", n=P), ACT.Copy)\
                               .then_inc(aux_taken["act"], 1)

                    for j, (_, n) in enumerate(FF_GROUPS):
                        for t in range(T):
                            act.wait_ge(acc_ready, acc.no(("h1", j, t)))
                            if j:
                                act.wait_ge(hidden_ready, 2 * j - 1 + t)
                            act.activation(silu[:, t, 0:n], acc_bank[acc.bank(("h1", j, t))][:, 0:n], ACT.Silu)\
                               .then_inc(acc_taken["act"], 1)
                        if j:
                            take_hidden(j - 1)
                    take_hidden(len(FF_GROUPS) - 1)

            for t in range(T):
                take_aux(("router", t), rl[:, t, :], lambda b: b[:, 0:N_EXP])
            act.wait_ge(routed, 1)
            act.activation(gate2[:, :, 1:2], gate2[:, :, 0:1], ACT.Exp).then_inc(routed, 1)

            act.wait_ge(passes_ready, 1)
            passes = act.value_load(n_pass[0:1, 0:1], min_val=1, max_val=2)
            with act.Fori(0, passes) as ps:
                with act.Fori(0, N_EXP) as e:
                    it = ps * N_EXP + e

                    def take(i, dst, src):
                        act.wait_ge(aux_ready, it * len(E_AUX) + (AUX0 + i + 1))
                        act.activation(dst, src, ACT.Copy).then_inc(aux_taken["act"], 1)

                    row = GROW["ffn_norm_g", 1]
                    for i in range(4):
                        act.wait_ge(aux_ready, it * len(E_AUX) + (AUX0 + X0 + i + 1))
                        for c in range(2):
                            k = 2 * i + c
                            ins = act.activation(xgT[:, k, :], aux_bank[(AUX0 + i) % 4][:, c * P:(c + 1) * P], ACT.Copy,
                                                 scale=gainT[:, row + k:row + k + 1])
                        ins.then_inc(aux_taken["act"], 1)
                    take(PG, pickT.rearrange("p a b -> p (a b)"), aux_bank[(AUX0 + PG) % 4][:, 0:T * P])

                    def take_expert_hidden(j):
                        take(HT0 + j, hidT[:, 4 * j:4 * j + 4, :].rearrange("p a b -> p (a b)"),
                             aux_bank[(AUX0 + HT0 + j) % 4][:, :])

                    for j in range(E_GROUPS):
                        act.wait_ge(acc_ready, it * len(E_ACC) + (ACC0 + 2 * j + 1))
                        if j >= 2:
                            act.wait_ge(*e_taken(ACCR, E_ACC, 2 * j - 3, it))
                        act.activation(silu[:, j % 2, 0:W], acc_bank[(ACC0 + 2 * j) % 4][:, :], ACT.Silu)\
                           .then_inc(acc_taken["act"], 1)
                        if j:
                            take_expert_hidden(j - 1)
                    take_expert_hidden(E_GROUPS - 1)
                    for h in range(2):
                        i = 2 * E_GROUPS + h
                        act.wait_ge(acc_ready, it * len(E_ACC) + (ACC0 + i + 1))
                        act.activation(ysb[:, h * W:(h + 1) * W], acc_bank[(ACC0 + i) % 4][:, :], ACT.Copy)\
                           .then_inc(acc_taken["act"], 1)

        @block.gpsimd
        def _(pool):
            steps = [0]

            def link(ins):
                steps[0] += 1
                ins.then_inc(pool_step, 1)
                pool.wait_ge(pool_step, steps[0])

            pool.memset(minus_half[:, :], -0.5)
            inv_freq = np.float32(10000.0) ** (-np.arange(32, dtype=np.float32) / np.float32(32))
            for i in range(32):
                pool.memset(freq[:, i:i + 1], float(inv_freq[i]))
            for c0, c1, n in ((0, 5, 64), (5, 6, B_QR), (6, 7, B_KVR), (7, 8, B_ROPE), (8, 18, 64),
                              (18, 22, 64), (22, 26, 32), (26, 30, 64)):
                pool.memset(invn[:, c0:c1], 1.0 / n)
            for z in (kcz[:, :, :, :], kaz[:, :, :], ikz[:, :, :], cmask[:, :], wmask[:, :], ident[:, :]):
                pool.memset(z, 0.0)
            pool.memset(ones[:, :], 1.0)
            link(pool.memset(lower[:, :], 1.0))
            pool.affine_select(out=ident[:, :], in_=ident[:, :], compare_op=ALU.not_equal, fill=1.0, base=0,
                               pattern=[[-1, P]], channel_multiplier=1)
            pool.affine_select(out=cmask[:, P:], in_=cmask[:, P:], compare_op=ALU.is_ge, fill=MASKED, base=0,
                               pattern=[[-1, P]], channel_multiplier=1)
            pool.affine_select(out=wmask[:, P:], in_=wmask[:, P:], compare_op=ALU.is_ge, fill=MASKED, base=0,
                               pattern=[[-1, P]], channel_multiplier=1)
            pool.affine_select(out=wmask[:, 0:P], in_=wmask[:, 0:P], compare_op=ALU.is_gt, fill=MASKED, base=0,
                               pattern=[[1, P]], channel_multiplier=-1)
            pool.affine_select(out=lower[:, :], in_=lower[:, :], compare_op=ALU.is_gt, fill=0.0, base=0,
                               pattern=[[1, P]], channel_multiplier=-1)
            pool.iota(iota8[:, :], pattern=[[1, N_EXP]], base=0, channel_multiplier=0, allow_small_or_imprecise_dtypes=True)
            pool.iota(iota_slot[:, :], pattern=[[1, P]], base=0, channel_multiplier=0,
                      allow_small_or_imprecise_dtypes=True).then_inc(masks_ready, 1)
            asks = 0

            def power(dst, src):
                nonlocal asks
                asks += 1
                pool.wait_ge(mean_ready, asks)
                n = dst.shape[-1]
                half = minus_half[:, 0:T * n].rearrange("p (t n) -> p t n", t=T) if len(dst.shape) == 3 else minus_half[:, 0:n]
                pool.tensor_tensor(dst, src, half, ALU.pow).then_inc(rstd_ready, 1)

            for l in range(DEPTH):
                for t in range(T):
                    power(xrstd[:, t:t + 1], xstat[:, t:t + 1])
                power(rstd[:, :, 0:8], stat[:, :, 0:8])
                power(rstd[:, :, 8:18], stat[:, :, 8:18])
                power(rstd[:, :, 18:30], stat[:, :, 18:30])
                for t in range(T):
                    power(xrstd[:, t:t + 1], xstat[:, t:t + 1])

        @block.vector
        def _(dve):
            steps, asks = [0], [0]

            def link(ins):
                steps[0] += 1
                ins.then_inc(dve_step, 1)
                dve.wait_ge(dve_step, steps[0])

            def root(ins):
                ins.then_inc(mean_ready, 1)
                asks[0] += 1
                dve.wait_ge(rstd_ready, asks[0])

            dve.wait_ge(consts_loaded, CONSTS)
            dve.wait_ge(masks_ready, 1)
            TWO_PI, MAGIC = 2.0 * np.pi, 1.5 * 2.0 ** 23
            C1 = 6.28125
            C2 = float(np.round((TWO_PI - C1) * 2 ** 19) / 2 ** 19)
            C3 = float(TWO_PI - C1 - C2)
            link(dve.tensor_copy(pos_f[:, :], pos_i[:, :]))
            link(dve.tensor_tensor(ang[:, 0, :, :], freq[:, :].unsqueeze(1).to_broadcast([P, T, 32]),
                                   pos_f[:, :].unsqueeze(2).to_broadcast([P, T, 32]), ALU.mult))
            for row, turn, shift in ((2, 0.0, 0.0), (3, 0.25, np.pi / 2)):
                r = ang[:, row, :, :]
                k = ang[:, 1, :, :]
                link(dve.tensor_scalar(k, ang[:, 0, :, :], float(1.0 / TWO_PI), turn, ALU.mult, ALU.add))
                link(dve.tensor_scalar(k, k, MAGIC, None, ALU.add))
                link(dve.tensor_scalar(k, k, -MAGIC, None, ALU.add))
                link(dve.scalar_tensor_tensor(out=r, in0=k, scalar=-C1, in1=ang[:, 0, :, :], op0=ALU.mult, op1=ALU.add))
                link(dve.scalar_tensor_tensor(out=r, in0=k, scalar=-C2, in1=r, op0=ALU.mult, op1=ALU.add))
                link(dve.scalar_tensor_tensor(out=r, in0=k, scalar=-C3, in1=r, op0=ALU.mult, op1=ALU.add))
                link(dve.tensor_scalar(r, r, float(shift), 3.1415925, ALU.add, ALU.min))
                ins = dve.tensor_scalar(r, r, -3.1415925, None, ALU.max)
                if row == 2:
                    link(ins)
            ins.then_inc(angles_ready, 1)
            dve.wait_ge(trig_ready, 1)
            sin, cos = trig[:, 0, :, :], trig[:, 1, :, :]
            for h in range(2):
                dve.tensor_copy(cos64[:, :, 32 * h:32 * h + 32], cos)
                dve.tensor_copy(cos32[:, :, 16 * h:16 * h + 16], cos[:, :, 0:32:2])
                dve.tensor_scalar(sin64[:, :, 32 * h:32 * h + 32], sin, 2.0 * h - 1.0, None, ALU.mult)
                ins = dve.tensor_scalar(sin32[:, :, 16 * h:16 * h + 16], sin[:, :, 0:32:2], 2.0 * h - 1.0, None, ALU.mult)
            link(ins)

            def norm_x(k):
                for t in range(T):
                    link(dve.scalar_tensor_tensor(out=swing[:, 0:D_MODEL], in0=x_sb[:, t, :], scalar=1.0, in1=x_sb[:, t, :],
                                                  op0=ALU.mult, op1=ALU.mult, accum_out=xstat[:, t:t + 1]))
                    root(dve.tensor_scalar(xstat[:, t:t + 1], xstat[:, t:t + 1], 1.0 / D_MODEL, EPS, ALU.mult, ALU.add))
                    dve.tensor_scalar(xn[:, t, :], x_sb[:, t, :], xrstd[:, t:t + 1], None, ALU.mult).then_inc(normed, 1)

            def mean_square(dst, view, width):
                link(dve.tensor_reduce(dst, view, AX_X, ALU.add))

            def finish_means(c0, c1):
                link(dve.tensor_tensor(stat[:, :, c0:c1], stat[:, :, c0:c1],
                                       invn[:, c0:c1].unsqueeze(1).to_broadcast([P, T, c1 - c0]), ALU.mult))
                root(dve.tensor_scalar(stat[:, :, c0:c1], stat[:, :, c0:c1], EPS, None, ALU.add))

            def scale_heads(v, c0, heads, d):
                r = rstd[:, :, c0:c0 + heads].unsqueeze(3).to_broadcast([P, T, heads, d])
                link(dve.tensor_tensor(v, v, r, ALU.mult))

            def rotate(v, heads, d, dsts):
                half = d // 2
                cs, sn = (cos64, sin64) if d == 64 else (cos32, sin32)
                tmp = swing[:, 0:T * heads * d].rearrange("p (t h d) -> p t h d", t=T, d=d)

                def over(a):
                    return a.unsqueeze(2).to_broadcast([P, T, heads, a.shape[-1]])
                dve.tensor_tensor(tmp[:, :, :, 0:half], v[:, :, :, half:], over(sn[:, :, 0:half]), ALU.mult)
                link(dve.tensor_tensor(tmp[:, :, :, half:], v[:, :, :, 0:half], over(sn[:, :, half:]), ALU.mult))
                link(dve.tensor_tensor(v, v, over(cs[:, :, :]), ALU.mult))
                for dst in dsts:
                    ins = dve.tensor_tensor(dst, v, tmp, ALU.add)
                return ins

            def squares(c0, n, off):
                v = sq[:, off:off + T * n].rearrange("p (t n) -> p t n", t=T)
                link(dve.tensor_tensor(v, proj[:, :, c0:c0 + n], proj[:, :, c0:c0 + n], ALU.mult))
                return v

            def add_to_x(l_fill, t, h):
                b = acc_bank[acc.bank(l_fill)]
                dve.wait_ge(acc_ready, acc.no(l_fill))
                xs = x_sb[:, t, h * W:(h + 1) * W]
                dve.tensor_tensor(xs, xs, b[:, :], ALU.add).then_inc(acc_taken["dve"], 1)

            for l in range(DEPTH):
                if l:
                    dve.wait_ge(*acc.taken(("y", 1, 1)))
                norm_x(2 * l)
                dve.wait_ge(*acc.taken(("p", l, len(ATT_GROUPS) - 1, 1)))
                v = squares(COL["cq"], 416, 0)
                mean_square(stat[:, :, 5:6], v[:, :, 0:256].unsqueeze(2), 256)
                mean_square(stat[:, :, 6:7], v[:, :, 256:384].unsqueeze(2), 128)
                mean_square(stat[:, :, 7:8], v[:, :, 384:416].unsqueeze(2), 32)
                v = squares(0, 320, 900)
                mean_square(stat[:, :, 0:5], v.rearrange("p t (h d) -> p t h d", d=64), 64)
                finish_means(0, 8)
                scale_heads(heads_of(proj, COL["cq"], 1, 256), 5, 1, 256)
                dve.tensor_tensor(heads_of(proj, COL["ckv"], 1, 128), heads_of(proj, COL["ckv"], 1, 128),
                                  rstd[:, :, 6:7].unsqueeze(3).to_broadcast([P, T, 1, 128]), ALU.mult).then_inc(lowrank_ready, 1)
                link(rotate(heads_of(proj, COL["iq"], 8, 32), 8, 32, [heads_of(proj, COL["iq"], 8, 32)]))
                link(rotate(heads_of(proj, COL["ik"], 1, 32), 1, 32,
                            [ik4[:, :, 32 * v:32 * v + 32].unsqueeze(2) for v in range(4)]))
                qa, ka = heads_of(proj, COL["qa"], 4, 64), heads_of(proj, COL["ka"], 1, 64)
                scale_heads(heads_of(proj, 0, 5, 64), 0, 5, 64)
                dve.tensor_tensor(qa, qa, gain("aq", l, 4), ALU.mult)
                link(dve.tensor_tensor(ka, ka, gain("ak", l, 1), ALU.mult))
                link(rotate(qa, 4, 64, [qa]))
                link(dve.tensor_scalar(iws[:, :, :], proj[:, :, COL["iw"]:COL["iw"] + 8],
                                       float(IDX_HEADS ** -0.5 * IDX_DIM ** -0.5), None, ALU.mult))
                rotate(ka, 1, 64, [ka2[:, :, 64 * v:64 * v + 64].unsqueeze(2) for v in range(2)]).then_inc(roped_a, 1)
                dve.wait_ge(roped_a, l + 1)
                kr = heads_of(proj, COL["kr"], 1, 32)
                scale_heads(kr, 7, 1, 32)
                link(dve.tensor_tensor(kr, kr, gain("kr", l, 1), ALU.mult))
                link(rotate(kr, 1, 32, [kcat[:, :, h:h + 1, 64:96] for h in range(B_HEADS)]))
                v = squares(COL["qc"], 640, 0)
                mean_square(stat[:, :, 8:18], v.rearrange("p t (h d) -> p t h d", d=64), 64)
                finish_means(8, 18)
                qc, kc = heads_of(proj, COL["qc"], 8, 64), heads_of(proj, COL["kc"], 2, 64)
                scale_heads(heads_of(proj, COL["qc"], 10, 64), 8, 10, 64)
                dve.tensor_tensor(qc, qc, gain("cq", l, 8), ALU.mult)
                link(dve.tensor_tensor(kc, kc, gain("ck", l, 2), ALU.mult))
                link(rotate(qc, 8, 64, [qc]))
                rotate(kc, 2, 64, [kc2[:, :, :, 64 * v:64 * v + 64] for v in range(2)]).then_inc(roped_c, 1)

                dve.wait_ge(*aux.taken(("ukv", l, 1)))
                v = sq[:, 0:T * 384].rearrange("p (t h d) -> p t h d", t=T, d=96)
                qbh = qb[:, :, :].rearrange("p t (h d) -> p t h d", d=96)
                kvh = kvb[:, :, :].rearrange("p t (h d) -> p t h d", d=128)
                vk = sq[:, 1024:1024 + T * 256].rearrange("p (t h d) -> p t h d", t=T, d=64)
                dve.tensor_tensor(v, qbh, qbh, ALU.mult)
                link(dve.tensor_tensor(vk, kvh[:, :, :, 0:64], kvh[:, :, :, 0:64], ALU.mult))
                mean_square(stat[:, :, 18:22], v[:, :, :, 0:64], 64)
                mean_square(stat[:, :, 22:26], v[:, :, :, 64:96], 32)
                mean_square(stat[:, :, 26:30], vk, 64)
                finish_means(18, 30)
                scale_heads(qbh[:, :, :, 0:64], 18, 4, 64)
                scale_heads(qbh[:, :, :, 64:96], 22, 4, 32)
                scale_heads(kvh[:, :, :, 0:64], 26, 4, 64)
                dve.tensor_tensor(qbh[:, :, :, 0:64], qbh[:, :, :, 0:64], gain("qn", l, 4), ALU.mult)
                link(dve.tensor_tensor(qbh[:, :, :, 64:96], qbh[:, :, :, 64:96], gain("qr", l, 4), ALU.mult))
                tmp = sq[:, 0:T * 128].rearrange("p (t h d) -> p t h d", t=T, d=32)
                qr = qbh[:, :, :, 64:96]

                def over(a):
                    return a.unsqueeze(2).to_broadcast([P, T, 4, a.shape[-1]])
                dve.tensor_tensor(tmp[:, :, :, 0:16], qr[:, :, :, 16:32], over(sin32[:, :, 0:16]), ALU.mult)
                link(dve.tensor_tensor(tmp[:, :, :, 16:32], qr[:, :, :, 0:16], over(sin32[:, :, 16:32]), ALU.mult))
                link(dve.tensor_tensor(qr, qr, over(cos32[:, :, :]), ALU.mult))
                dve.tensor_tensor(qr, qr, tmp, ALU.add)
                dve.tensor_tensor(kcat[:, :, :, 0:64], kvh[:, :, :, 0:64], gain("kn", l, 4), ALU.mult)\
                   .then_inc(mla_heads_ready, 1)

                n = 0
                for t in range(T):
                    nk = P * (t + 1)
                    per = W // nk
                    for i in range(2 * (t + 1)):
                        dve.wait_ge(*aux.taken(("ix", l, t, i)))
                        for j in range(per):
                            h = i * per + j
                            rel = swing[:, (n % 2) * W + j * nk:(n % 2) * W + (j + 1) * nk]
                            wgt = iws[:, t, h:h + 1]
                            if h == 0:
                                ins = dve.tensor_scalar(score[:, 0:nk], rel, wgt, None, ALU.mult)
                            else:
                                ins = dve.scalar_tensor_tensor(out=score[:, 0:nk], in0=rel, scalar=wgt, in1=score[:, 0:nk],
                                                               op0=ALU.mult, op1=ALU.add)
                            if j < per - 1:
                                link(ins)
                        n += 1
                        ins.then_inc(relu_used, 1)
                        dve.wait_ge(relu_used, 6 * l + n)
                    bias = cmask[:, SEQ - nk:]
                    link(dve.tensor_tensor(score[:, 0:nk], score[:, 0:nk], bias, ALU.add))
                    for r in range(TOPK // 8):
                        link(dve.max(top8[:, :], score[:, 0:nk]))
                        link(dve.match_replace(score[:, 0:nk], top8[:, :], score[:, 0:nk], REMOVED))
                    link(dve.tensor_scalar(selmask[:, t, 0:nk], score[:, 0:nk], REMOVED * 0.5, MASKED, ALU.is_gt, ALU.mult))
                    link(dve.tensor_tensor(selmask[:, t, 0:nk], selmask[:, t, 0:nk], bias, ALU.add))

                def sigmoid(i):
                    g, t = i // 2, i % 2
                    dve.wait_ge(*acc.taken(("g", l, g, t)))
                    v = gates[:, t, g * W:(g + 1) * W]
                    link(dve.tensor_scalar(v, v, 1.0, None, ALU.add))
                    link(dve.reciprocal(v, v))

                for s in range(len(JOBS) + 2):
                    if s < len(JOBS):
                        m, t = JOBS[s]
                        nk = P * (t + 1)
                        per = W // nk
                        mask = dict(a=selmask[:, t, 0:nk], b=cmask[:, SEQ - nk:]).get(m, wmask[:, SEQ - nk:])
                        if s >= 2:
                            dve.wait_ge(aux_ready, aux.no(("pt", l, s - 2, JOBS[s - 2][1])))
                        for i in range(t + 1):
                            dve.wait_ge(aux_ready, aux.no(("lg", l, s, i)))
                            b = aux_bank[aux.bank(("lg", l, s, i))]
                            dve.scalar_tensor_tensor(out=logit[:, s % 2, i * per:(i + 1) * per, 0:nk],
                                                     in0=b[:, :].rearrange("p (h k) -> p h k", k=nk), scalar=SCALE[m],
                                                     in1=mask.unsqueeze(1).to_broadcast([P, per, nk]),
                                                     op0=ALU.mult, op1=ALU.add).then_inc(aux_taken["dve"], 1)
                        dve.wait_ge(*aux.taken(("lg", l, s, t)))
                        red = dve.tensor_reduce(nmax[:, s % 2, :], logit[:, s % 2, :, 0:nk], AX_X, ALU.max, negate=True)
                        if m[0] == "c":
                            link(red)
                            o = GAINS["sink"][0] + 4 * int(m[1])
                            sink = gains[:, l, o:o + 4]
                            link(dve.scalar_tensor_tensor(out=nmax[:, s % 2, :], in0=sink, scalar=-1.0, in1=nmax[:, s % 2, :],
                                                          op0=ALU.mult, op1=ALU.min))
                            red = dve.tensor_tensor(sinkx[:, s % 4, 0, :], sink, nmax[:, s % 2, :], ALU.add)
                        red.then_inc(logits_ready, 1)
                    for i in ((0, 1), (2, 3), (4, 5, 6), (7, 8), (9,), (10,), (11,), (), (), ())[s]:
                        sigmoid(i)
                    if s >= 2:
                        q = s - 2
                        m, t = JOBS[q]
                        dve.wait_ge(probs_ready, len(JOBS) * l + q + 1)
                        if m[0] == "c":
                            link(dve.tensor_tensor(denom[:, q % 4, :], denom[:, q % 4, :], sinkx[:, q % 4, 1, :], ALU.add))
                        link(dve.reciprocal(rden[:, q % 4, :], denom[:, q % 4, :]))
                        dve.wait_ge(aux_ready, aux.no(("pv", l, q)))
                        b = aux_bank[aux.bank(("pv", l, q))]
                        c0 = Y_COL[m]
                        dve.tensor_tensor(xn[:, t, c0:c0 + 256].rearrange("p (h d) -> p h d", d=64),
                                          b[:, 0:256].rearrange("p (h d) -> p h d", d=64),
                                          rden[:, q % 4, :].unsqueeze(2).to_broadcast([P, 4, 64]), ALU.mult)\
                           .then_inc(aux_taken["dve"], 1)

                dve.wait_ge(*acc.taken(("g", l, GATE_GROUPS - 1, 1)))
                dve.wait_ge(*aux.taken(("yt", l, 3)))
                for gi, m in enumerate("abc"):
                    for t in range(T):
                        for h in range(2):
                            name = ("m", l, m, t, h)
                            dve.wait_ge(acc_ready, acc.no(name))
                            b = acc_bank[acc.bank(name)]
                            e = gates[:, t, gi * D_MODEL + h * W:gi * D_MODEL + (h + 1) * W]
                            dst = xn[:, t, h * W:(h + 1) * W]
                            o = dst if m == "a" else swing[:, 0:W]
                            dve.tensor_tensor(o, b[:, :], e, ALU.mult).then_inc(acc_taken["dve"], 1)
                            if m != "a":
                                dve.wait_ge(*acc.taken(name))
                                ins = dve.tensor_tensor(dst, dst, swing[:, 0:W], ALU.add)
                                if m == "c" and h == 1:
                                    ins.then_inc(merged_ready, 1)
                                    dve.wait_ge(merged_ready, 2 * l + t + 1)
                                else:
                                    link(ins)
                for t in range(T):
                    for h in range(2):
                        add_to_x(("o", l, t, h), t, h)
                dve.wait_ge(*acc.taken(("o", l, 1, 1)))
                norm_x(2 * l + 1)
                if l == 0:
                    for j, (_, n) in enumerate(FF_GROUPS):
                        for t in range(T):
                            dve.wait_ge(acc_ready, acc.no(("h3", j, t)))
                            dve.wait_ge(*acc.taken(("h1", j, t)))
                            if j:
                                dve.wait_ge(aux_ready, aux.no(("ht", j - 1, t)))
                            dve.tensor_tensor(hidden[:, t, 0:n], silu[:, t, 0:n],
                                              acc_bank[acc.bank(("h3", j, t))][:, 0:n], ALU.mult).then_inc(acc_taken["dve"], 1)
                            dve.wait_ge(*acc.taken(("h3", j, t)))
                            dve.tensor_copy(top8[:, 0:1], top8[:, 1:2]).then_inc(hidden_ready, 1)
                    for t in range(T):
                        for h in range(2):
                            add_to_x(("y", t, h), t, h)

            for t in range(T):
                dve.wait_ge(*aux.taken(("router", t)))
                link(dve.max(rtop[:, t, :], rl[:, t, :]))
                link(dve.max_index(ridx[:, t, :], rtop[:, t, :], rl[:, t, :]))
            link(dve.tensor_copy(ridxf[:, :, :], ridx[:, :, :]))
            dve.tensor_tensor(gate2[:, :, 0:1], rtop[:, :, 1:2], rtop[:, :, 0:1], ALU.subtract).then_inc(routed, 1)
            for k in range(2):
                dve.tensor_tensor(onehot[:, :, k, :], iota8[:, :].unsqueeze(1).to_broadcast([P, T, 8]),
                                  ridxf[:, :, k:k + 1].to_broadcast([P, T, 8]), ALU.is_equal)
            dve.wait_ge(routed, 2)
            link(dve.tensor_scalar(gate2[:, :, 0:1], gate2[:, :, 1:2], 1.0, None, ALU.add))
            link(dve.reciprocal(gate2[:, :, 0:1], gate2[:, :, 0:1]))
            link(dve.tensor_tensor(gate2[:, :, 1:2], gate2[:, :, 1:2], gate2[:, :, 0:1], ALU.mult))
            link(dve.tensor_tensor(gated[:, :, :], onehot[:, :, 0, :], gate2[:, :, 0:1].to_broadcast([P, T, 8]), ALU.mult))
            link(dve.tensor_tensor(chosen[:, :, :], onehot[:, :, 1, :], gate2[:, :, 1:2].to_broadcast([P, T, 8]), ALU.mult))
            link(dve.tensor_tensor(gated[:, :, :], gated[:, :, :], chosen[:, :, :], ALU.add))
            dve.tensor_tensor(chosen[:, :, :], onehot[:, :, 0, :], onehot[:, :, 1, :], ALU.add).then_inc(routed, 1)
            dve.wait_ge(routed, 3)
            dve.wait_ge(aux_ready, aux.no(("slots",)))
            b = aux_bank[aux.bank(("slots",))]
            link(dve.scalar_tensor_tensor(out=slot_of[:, :, 0, :], in0=b[:, 0:16].rearrange("p (t e) -> p t e", t=T),
                                          scalar=1.0, in1=chosen[:, :, :], op0=ALU.add, op1=ALU.mult))
            link(dve.tensor_scalar(slot_of[:, :, 0, :], slot_of[:, :, 0, :], -1.0, None, ALU.add))
            link(dve.tensor_scalar(slot_of[:, :, 1, :], slot_of[:, :, 0, :], float(-P), None, ALU.add))
            dve.tensor_reduce(cnt[:, 0:1], b[:, 16:24], AX_X, ALU.max).then_inc(aux_taken["dve"], 1)
            dve.wait_ge(*aux.taken(("slots",)))
            link(dve.tensor_scalar(cnt[:, 1:2], cnt[:, 0:1], float(P), 1.0, ALU.is_gt, ALU.add))
            dve.tensor_copy(n_pass[:, :], cnt[:, 1:2]).then_inc(passes_ready, 1)
            dve.wait_ge(passes_ready, 1)
            slot_flat = slot_of[:, :, :, :].rearrange("p t s e -> p t (s e)")

            passes = dve.value_load(n_pass[0:1, 0:1], min_val=1, max_val=2)
            with dve.Fori(0, passes) as ps:
                with dve.Fori(0, N_EXP) as e:
                    it = ps * N_EXP + e
                    for t in range(T):
                        at = slot_flat[:, t, bass.ds(it, 1)]
                        dve.tensor_scalar(pick[:, t, :], iota_slot[:, :], at, None, ALU.is_equal)
                    for t in range(T):
                        at = slot_flat[:, t, bass.ds(it, 1)]
                        ins = dve.tensor_scalar(pickg[:, t, :], iota_slot[:, :], at, gated[:, t, bass.ds(e, 1)],
                                                ALU.is_equal, ALU.mult)
                    ins.then_inc(onehot_ready, 1)
                    for j in range(E_GROUPS):
                        i = 2 * j + 1
                        dve.wait_ge(acc_ready, it * len(E_ACC) + (ACC0 + i + 1))
                        dve.wait_ge(*e_taken(ACCR, E_ACC, i - 1, it))
                        if j >= 2:
                            dve.wait_ge(aux_ready, it * len(E_AUX) + (AUX0 + HT0 + j - 2 + 1))
                        dve.tensor_tensor(hidden[:, j % 2, 0:W], silu[:, j % 2, 0:W], acc_bank[(ACC0 + i) % 4][:, :],
                                          ALU.mult).then_inc(acc_taken["dve"], 1)
                    for t in range(T):
                        for h in range(2):
                            i = CB0 + 2 * t + h
                            dve.wait_ge(aux_ready, it * len(E_AUX) + (AUX0 + i + 1))
                            xs = x_sb[:, t, h * W:(h + 1) * W]
                            dve.tensor_tensor(xs, xs, aux_bank[(AUX0 + i) % 4][:, :], ALU.add).then_inc(aux_taken["dve"], 1)

        @block.tensor
        def _(pe):
            def begin(bank_ring, name):
                free = bank_ring.free(name)
                if free is not None:
                    pe.wait_ge(*free)
                return (acc_bank if bank_ring is acc else aux_bank)[bank_ring.bank(name)]

            def used(ins, name):
                assert name not in ends_fill
                return ins.then_inc(unit_used, 1)

            pe.wait_ge(consts_loaded, CONSTS)
            pe.wait_ge(masks_ready, 1)
            b = begin(aux, ("gains",))
            pe.transpose(b[:, 0:NROWS], gain_rows[0:NROWS, :], ident[0:NROWS, 0:NROWS]).then_inc(aux_ready, 1)

            def transposes(kind, l, src):
                for i in range(4):
                    b = begin(aux, (kind, l, i))
                    for c in range(2):
                        for t in range(T):
                            k = 2 * i + c
                            ins = pe.transpose(b[:, (2 * c + t) * P:(2 * c + t + 1) * P], src[:, t, k * P:(k + 1) * P], ident[:, :])
                    ins.then_inc(aux_ready, 1)

            def four(name, blocks):
                b = begin(aux, name)
                for i, src in enumerate(blocks):
                    m = src.shape[1]
                    ins = pe.transpose(b[0:m, i * P:(i + 1) * P], src, ident[:, :])
                ins.then_inc(aux_ready, 1)

            def project(kind, l, g, t, n):
                name = (kind, l, g, t)
                b = begin(acc, name)
                for k in range(KC):
                    if k % 4 == 0:
                        pe.wait_ge(*arrived((kind, l, g, k // 4)))
                    ins = pe.matmul(b[:, 0:n], hT[:, k, t * P:(t + 1) * P], unit((kind, l, g, k // 4))[:, k % 4, :],
                                    start=(k == 0), stop=(k == KC - 1))
                    if t == 1 and k == 3:
                        used(ins, (kind, l, g, 0))
                ins.then_inc(acc_ready, 1)

            for l in range(DEPTH):
                pe.wait_ge(normed, 4 * l + 2)
                transposes("h", l, xn)
                pe.wait_ge(*aux.taken(("h", l, 3)))
                for g, (_, n) in enumerate(ATT_GROUPS):
                    for t in range(T):
                        project("p", l, g, t, n)

                def gate(i):
                    project("g", l, i // 2, i % 2, W)

                gate(0)
                gate(1)
                pe.wait_ge(lowrank_ready, l + 1)
                cq, ckv = proj[:, :, COL["cq"]:COL["ckv"]], proj[:, :, COL["ckv"]:COL["kr"]]
                four(("cq", l), [cq[:, t, c * P:(c + 1) * P] for c in range(2) for t in range(T)])
                four(("ckv", l), [ckv[:, t, :] for t in range(T)])
                pe.wait_ge(roped_a, l + 1)
                four(("ika", l), [ka2[:, t, :] for t in range(T)] + [ik4[:, t, :] for t in range(T)])
                for nm in ("iq", "qa"):
                    four((nm, l), [proj[:, t, COL[nm] + c * P:COL[nm] + (c + 1) * P] for c in range(2) for t in range(T)])
                gate(2)
                pe.wait_ge(mla_loaded, 32 * (l + 1))
                pe.wait_ge(*aux.taken(("ckv", l)))
                for t in range(T):
                    b = begin(aux, ("uq", l, t))
                    for c in range(2):
                        ins = pe.matmul(b[:, 0:384], cqT[:, c, t * P:(t + 1) * P], uq[:, c, :], start=(c == 0), stop=(c == 1))
                    ins.then_inc(aux_ready, 1)
                for t in range(T):
                    b = begin(aux, ("ukv", l, t))
                    pe.matmul(b[:, :], ckvT[:, t * P:(t + 1) * P], ukv[:, :], start=True, stop=True).then_inc(aux_ready, 1)
                pe.wait_ge(*aux.taken(("iq", l)))
                for t in range(T):
                    nk = P * (t + 1)
                    per = W // nk
                    for i in range(2 * (t + 1)):
                        b = begin(aux, ("ix", l, t, i))
                        h0 = i * per
                        pe.matmul(b[:, :].rearrange("p (h k) -> p h k", k=nk), iqT[:, h0 // 4, t * P:(t + 1) * P],
                                  ikz[:, h0 % 4:h0 % 4 + per, 0:nk], start=True, stop=True).then_inc(aux_ready, 1)
                gate(3)
                pe.wait_ge(roped_c, l + 1)
                four(("kc", l), [kc2[:, t, kv, :] for kv in range(C_KV) for t in range(T)])
                for i in range(2):
                    four((f"qc{i}", l), [proj[:, t, COL["qc"] + c * P:COL["qc"] + (c + 1) * P]
                                         for c in (2 * i, 2 * i + 1) for t in range(T)])
                pe.wait_ge(mla_heads_ready, l + 1)
                for i in range(2):
                    four((f"qb{i}", l), [qb[:, t, 96 * h:96 * h + 96] for h in (2 * i, 2 * i + 1) for t in range(T)])
                for i in range(2):
                    four((f"kb{i}", l), [kcat[:, t, h, :] for h in (2 * i, 2 * i + 1) for t in range(T)])
                gate(4)
                gate(5)
                pe.wait_ge(*aux.taken(("kb1", l)))
                for s in range(len(JOBS) + 2):
                    if s < len(JOBS):
                        m, t = JOBS[s]
                        nk = P * (t + 1)
                        per = W // nk
                        for i in range(t + 1):
                            b = begin(aux, ("lg", l, s, i))
                            for j in range(per // 2 if m != "b" else per):
                                if m == "b":
                                    h = i * per + j
                                    ins = pe.matmul(b[:, j * nk:(j + 1) * nk], qbT[0:96, h, t * P:(t + 1) * P],
                                                    kbT[0:96, h, 0:nk], start=True, stop=True)
                                else:
                                    pair = i * per // 2 + j
                                    q, k = (qaT, kaz) if m == "a" else (qcT, kcz[:, int(m[1])])
                                    blk = pair if m == "a" else 2 * int(m[1]) + pair
                                    ins = pe.matmul(b[:, 2 * j * nk:2 * (j + 1) * nk].rearrange("p (h k) -> p h k", k=nk),
                                                    q[:, blk, t * P:(t + 1) * P], k[:, :, 0:nk], start=True, stop=True)
                            ins.then_inc(aux_ready, 1)
                    if s < 6:
                        gate(6 + s)
                    if 1 <= s <= len(JOBS):
                        q, tq = s - 1, JOBS[s - 1][1]
                        pe.wait_ge(probs_ready, len(JOBS) * l + q + 1)
                        for i in range(tq + 1):
                            four(("pt", l, q, i), [logit[:, q % 2, h, i * P:(i + 1) * P] for h in range(4)])
                    if s >= 2:
                        q = s - 2
                        m, t = JOBS[q]
                        pe.wait_ge(*aux.taken(("pt", l, q, t)))
                        b = begin(aux, ("pv", l, q))
                        for h in range(4):
                            for i in range(t + 1):
                                if m == "a":
                                    v = proj[:, i, COL["va"]:COL["va"] + 64]
                                elif m == "b":
                                    v = kvb[:, i, 128 * h + 64:128 * h + 128]
                                else:
                                    v = proj[:, i, COL["vc"] + 64 * int(m[1]):COL["vc"] + 64 * int(m[1]) + 64]
                                ins = pe.matmul(b[:, 64 * h:64 * h + 64], probT[:, q % 2, 4 * i + h, :], v,
                                                start=(i == 0), stop=(i == t))
                        ins.then_inc(aux_ready, 1)
                pe.wait_ge(*aux.taken(("pv", l, len(JOBS) - 1)))
                transposes("yt", l, xn)
                pe.wait_ge(*aux.taken(("yt", l, 3)))
                for m, name, c0, chunks in (("a", "wa", 0, 2), ("b", "wb", 2, 2), ("c", "wc", 4, 4)):
                    for u in range(chunks // 2):
                        pe.wait_ge(*arrived((name, l, u)))
                    for t in range(T):
                        for h in range(2):
                            b = begin(acc, ("m", l, m, t, h))
                            for k in range(chunks):
                                ins = pe.matmul(b[:, :], yT[:, c0 + k, t * P:(t + 1) * P],
                                                unit((name, l, k // 2))[:, k % 2, h * W:(h + 1) * W],
                                                start=(k == 0), stop=(k == chunks - 1))
                                if (t, h) == (1, 1) and k % 2 and k < chunks - 1:
                                    used(ins, (name, l, k // 2))
                            ins.then_inc(acc_ready, 1)
                pe.wait_ge(merged_ready, 2 * (l + 1))
                transposes("mt", l, xn)
                pe.wait_ge(*aux.taken(("mt", l, 3)))
                for t in range(T):
                    for h in range(2):
                        b = begin(acc, ("o", l, t, h))
                        for k in range(KC):
                            if k % 2 == 0:
                                pe.wait_ge(*arrived(("wo", l, k // 2)))
                            ins = pe.matmul(b[:, :], hT[:, k, t * P:(t + 1) * P], unit(("wo", l, k // 2))[:, k % 2, h * W:(h + 1) * W],
                                            start=(k == 0), stop=(k == KC - 1))
                            if (t, h) == (1, 1) and k % 2 and k < KC - 1:
                                used(ins, ("wo", l, k // 2))
                        ins.then_inc(acc_ready, 1)
                pe.wait_ge(normed, 4 * l + 4)
                transposes("f", l, xn)
                pe.wait_ge(*aux.taken(("f", l, 3)))
                if l == 0:
                    def hidden_transposes(j):
                        n = FF_GROUPS[j][1]
                        for t in range(T):
                            pe.wait_ge(hidden_ready, 2 * j + t + 1)
                            four(("ht", j, t), [hidden[:, t, c * P:(c + 1) * P] for c in range(n // P)])

                    for j, (_, n) in enumerate(FF_GROUPS):
                        per = 4 if n > 256 else 8
                        for kind, wn in (("h1", "w1"), ("h3", "w3")):
                            for t in range(T):
                                b = begin(acc, (kind, j, t))
                                for k in range(KC):
                                    if k % per == 0:
                                        pe.wait_ge(*arrived((wn, j, k // per)))
                                    ins = pe.matmul(b[:, 0:n], hT[:, k, t * P:(t + 1) * P], unit((wn, j, k // per))[:, k % per, :],
                                                    start=(k == 0), stop=(k == KC - 1))
                                    if t == 1 and k % per == per - 1 and k < KC - 1:
                                        used(ins, (wn, j, k // per))
                                ins.then_inc(acc_ready, 1)
                            if kind == "h1" and j:
                                hidden_transposes(j - 1)
                    hidden_transposes(len(FF_GROUPS) - 1)
                    pe.wait_ge(*aux.taken(("ht", len(FF_GROUPS) - 1, 1)))
                    banks = [[begin(acc, ("y", t, h)) for h in range(2)] for t in range(T)]
                    for c in range(FF_CHUNKS):
                        if c % 2 == 0:
                            pe.wait_ge(*arrived(("w2", c // 2)))
                        for t in range(T):
                            for h in range(2):
                                ins = pe.matmul(banks[t][h][:, :], ffT[:, c, t * P:(t + 1) * P],
                                                unit(("w2", c // 2))[:, c % 2, h * W:(h + 1) * W],
                                                start=(c == 0), stop=(c == FF_CHUNKS - 1))
                                if c == FF_CHUNKS - 1:
                                    ins.then_inc(acc_ready, 1)
                        if c % 2 and c < FF_CHUNKS - 1:
                            used(ins, ("w2", c // 2))

            for t in range(T):
                b = begin(aux, ("router", t))
                for k in range(KC):
                    ins = pe.matmul(b[:, 0:N_EXP], hT[:, k, t * P:(t + 1) * P], wr[:, k, :], start=(k == 0), stop=(k == KC - 1))
                ins.then_inc(aux_ready, 1)
            pe.wait_ge(routed, 3)
            b = begin(aux, ("slots",))
            pe.matmul(b[:, 0:8], lower[:, :], chosen[:, 0, :], start=True, stop=True)
            pe.matmul(b[:, 8:16], ones[:, :], chosen[:, 0, :], start=True, stop=False)
            pe.matmul(b[:, 8:16], lower[:, :], chosen[:, 1, :], start=False, stop=True)
            pe.matmul(b[:, 16:24], ones[:, :], chosen[:, 0, :], start=True, stop=False)
            pe.matmul(b[:, 16:24], ones[:, :], chosen[:, 1, :], start=False, stop=True).then_inc(aux_ready, 1)
            pe.wait_ge(passes_ready, 1)
            for r in ("act", "dve"):
                pe.wait_ge(acc_taken[r], acc.order.count(r))
                pe.wait_ge(aux_taken[r], aux.order.count(r))

            passes = pe.value_load(n_pass[0:1, 0:1], min_val=1, max_val=2)
            with pe.Fori(0, passes) as ps:
                with pe.Fori(0, N_EXP) as e:
                    it = ps * N_EXP + e

                    def aux_fill(i):
                        pe.wait_ge(*e_free(AUXR, E_AUX, i, it))
                        return aux_bank[(AUX0 + i) % 4]

                    def acc_fill(i):
                        pe.wait_ge(*e_free(ACCR, E_ACC, i, it))
                        return acc_bank[(ACC0 + i) % 4]

                    pe.wait_ge(onehot_ready, it + 1)
                    for i in range(4):
                        b = aux_fill(X0 + i)
                        for c in range(2):
                            k = 2 * i + c
                            for t in range(T):
                                ins = pe.matmul(b[:, c * P:(c + 1) * P], xn[:, t, k * P:(k + 1) * P], pick[:, t, :],
                                                start=(t == 0), stop=(t == T - 1))
                        ins.then_inc(aux_ready, 1)
                    b = aux_fill(PG)
                    for t in range(T):
                        ins = pe.transpose(b[:, t * P:(t + 1) * P], pickg[:, t, :], ident[:, :])
                    ins.then_inc(aux_ready, 1)
                    pe.wait_ge(*e_taken(AUXR, E_AUX, X0 + 3, it))

                    def expert_transposes(j):
                        pe.wait_ge(*e_taken(ACCR, E_ACC, 2 * j + 1, it))
                        b = aux_fill(HT0 + j)
                        for c in range(4):
                            ins = pe.transpose(b[:, c * P:(c + 1) * P], hidden[:, j % 2, c * P:(c + 1) * P], ident[:, :])
                        ins.then_inc(aux_ready, 1)

                    for j in range(E_GROUPS):
                        for side in range(2):
                            b = acc_fill(2 * j + side)
                            for k in range(KC):
                                u = 4 * j + 2 * side + k // 4
                                if k % 4 == 0:
                                    pe.wait_ge(*e_arrived(u, it))
                                ins = pe.matmul(b[:, :], xgT[:, k, :], slot(UNITS0 + u, (4, W))[:, k % 4, :],
                                                start=(k == 0), stop=(k == KC - 1))
                                if k == 3:
                                    ins.then_inc(unit_used, 1)
                            ins.then_inc(acc_ready, 1)
                            if side == 0 and j:
                                expert_transposes(j - 1)
                    expert_transposes(E_GROUPS - 1)
                    pe.wait_ge(*e_taken(AUXR, E_AUX, HT0 + E_GROUPS - 1, it))
                    banks = [acc_fill(2 * E_GROUPS + h) for h in range(2)]
                    for c in range(E_CHUNKS):
                        u = 4 * E_GROUPS + c // 2
                        if c % 2 == 0:
                            pe.wait_ge(*e_arrived(u, it))
                        for h in range(2):
                            ins = pe.matmul(banks[h][:, :], hidT[:, c, :], slot(UNITS0 + u, (2, D_MODEL))[:, c % 2, h * W:(h + 1) * W],
                                            start=(c == 0), stop=(c == E_CHUNKS - 1))
                            if c == E_CHUNKS - 1:
                                ins.then_inc(acc_ready, 1)
                        if c % 2 and c < E_CHUNKS - 1:
                            ins.then_inc(unit_used, 1)
                    pe.wait_ge(*e_taken(ACCR, E_ACC, 2 * E_GROUPS + 1, it))
                    for t in range(T):
                        for h in range(2):
                            b = aux_fill(CB0 + 2 * t + h)
                            pe.matmul(b[:, :], pickT[:, t, :], ysb[:, h * W:(h + 1) * W], start=True, stop=True)\
                              .then_inc(aux_ready, 1)

        @block.sync
        def _(sp):
            n_mla = 0

            def load_mla(l):
                sp.dma_start(uq[:, :, :], w["b_w_uq"][l].rearrange("(c p) n -> p c n", p=P)).then_inc(mla_loaded, 16)
                sp.dma_start(ukv[:, :], w["b_w_ukv"][l]).then_inc(mla_loaded, 16)

            load_mla(0)
            for n, (name, src, shape) in enumerate(units):
                if n >= SLOTS:
                    sp.wait_ge(*released(n - SLOTS))
                if name == ("p", 1, 0, 0):
                    sp.wait_ge(aux_ready, aux.no(("ukv", 0, 1)))
                    load_mla(1)
                sp.dma_start(slot(n, shape), src).then_inc(unit_loaded[n % SLOTS], 16)

            w1, w3 = (w[k][0].rearrange("e (c p) n -> e p c n", p=P) for k in ("moe_w1", "moe_w3"))
            w2 = w["moe_w2"][0].rearrange("e (c p) n -> e p c n", p=P)
            passes_sem = passes_ready

            def expert_unit(u, e, it, wait):
                if wait is not None:
                    sp.wait_ge(*wait)
                if u < 4 * E_GROUPS:
                    j, side, half = u // 4, u // 2 % 2, u % 2
                    src = (w1, w3)[side][bass.ds(e, 1), :, 4 * half:4 * half + 4, j * W:(j + 1) * W]
                    dst = slot(UNITS0 + u, (4, W))
                else:
                    c = 2 * (u - 4 * E_GROUPS)
                    src = w2[bass.ds(e, 1), :, c:c + 2, :]
                    dst = slot(UNITS0 + u, (2, D_MODEL))
                sp.dma_start(dst, src.rearrange("e p c n -> p (e c) n")).then_inc(unit_loaded[(UNITS0 + u) % SLOTS], 16)

            for i in range(SLOTS):
                sp.wait_ge(*released(UNITS0 - SLOTS + i))
            sp.wait_ge(passes_ready, 1)
            passes = sp.value_load(n_pass[0:1, 0:1], min_val=1, max_val=2)
            with sp.Fori(0, passes) as ps:
                with sp.Fori(0, N_EXP) as e:
                    it = ps * N_EXP + e
                    for u in range(E_UNITS):
                        if u >= SLOTS:
                            expert_unit(u, e, it, e_released(u - SLOTS, it))
                        else:
                            s, v = e_released(E_UNITS + u - SLOTS, it)
                            k = len(E_OWN) if s is unit_used else len(E_ACC)
                            expert_unit(u, e, it, (s, v - k))
            n_it = passes * N_EXP
            sp.wait_ge(aux_taken["dve"], n_it * E_AUX.count("dve") + aux.order.count("dve"))
            sp.dma_start(out_view, x_sb[:, :, :]).then_inc(stored, 16)
            sp.wait_ge(stored, 16)


_INS = ['x', 'positions', 'attn_norm_g', 'w_in', 'a_q_norm_g', 'a_k_norm_g', 'b_cq_norm_g', 'b_ckv_norm_g',
        'b_w_uq', 'b_w_ukv', 'b_qn_g', 'b_qr_g', 'b_kn_g', 'b_kr_g', 'c_q_norm_g', 'c_k_norm_g', 'c_sinks',
        'w_a_out', 'w_b_out', 'w_c_out', 'w_o', 'ffn_norm_g', 'ffn_w1', 'ffn_w3', 'ffn_w2',
        'router_w', 'moe_w1', 'moe_w3', 'moe_w2']


def kernel(**inputs):
    import numpy as _np
    import concourse.bacc as _bacc
    from concourse import mybir as _mybir
    from concourse.bass_utils import run_bass_kernel_spmd as _run

    nc = _bacc.Bacc("TRN2", target_bir_lowering=False, num_devices=1)
    arrays, args = {}, {}
    for name in _INS:
        a = _np.ascontiguousarray(inputs[name])
        arrays[f"in_{name}_dram"] = a
        args[name] = nc.dram_tensor(f"in_{name}_dram", a.shape, _mybir.dt.from_np(a.dtype), kind="ExternalInput").ap()
    out = nc.dram_tensor("out_0_dram", inputs["x"].shape, _mybir.dt.from_np(_np.dtype("float32")), kind="ExternalOutput").ap()
    hybrid_layers(nc, args, out)
    r = _run(nc, [arrays], core_ids=[0])
    return r.results[0]["out_0_dram"]
```

```python
from contextlib import ExitStack

import numpy as np

import concourse.bass as bass
from concourse import mybir

F32 = mybir.dt.float32
F32R = mybir.dt.float32r
I32 = mybir.dt.int32
U32 = mybir.dt.uint32
ALU = mybir.AluOpType
ACT = mybir.ActivationFunctionType
AX_X = mybir.AxisListType.X

P = 128
D_MODEL, SEQ, DEPTH = 1024, 256, 2
T = SEQ // P
KC = D_MODEL // P
HEAD, IDX_DIM, IDX_HEADS = 64, 32, 8
TOPK = min(256, SEQ // 4)
A_HEADS, B_HEADS, C_HEADS, C_KV = 4, 4, 8, 2
B_NOPE, B_ROPE, B_V, B_QR, B_KVR = 64, 32, 64, 256, 128
D_FF, N_EXP, E_FF = 2816, 8, 3584
EPS = 1e-6

SIZES = dict(qa=256, ka=64, va=64, iq=256, ik=32, iw=8, cq=256, ckv=128, kr=32, qc=512, kc=128, vc=128)
COL, ATT = {}, 0
for _name, _size in SIZES.items():
    COL[_name] = ATT
    ATT += _size
W = 512
ATT_GROUPS = [(g * W, min(W, ATT - g * W)) for g in range(-(-ATT // W))]
GATE_GROUPS = 3 * D_MODEL // W

MASKED, REMOVED = -1e30, -3e38

UNIT = 2048
RAW, PARTS = 3, 2
E_RAW, E_PARTS = 7, 3
E_GROUPS = E_FF // W
E_CHUNKS = E_FF // P
E_UNITS = 4 * E_GROUPS + E_CHUNKS // 2
FF_GROUPS = [(j * W, min(W, D_FF - j * W)) for j in range(-(-D_FF // W))]
FF_CHUNKS = D_FF // P

MIXERS = ["c0", "c1", "b", "a"]
JOBS = [(m, t) for m in MIXERS for t in range(T)]
Y_COL = dict(a=0, b=256, c0=512, c1=768)
SCALE = dict(a=HEAD ** -0.5, b=(B_NOPE + B_ROPE) ** -0.5, c0=HEAD ** -0.5, c1=HEAD ** -0.5)


class BankRing:

    def __init__(self, taken_by):
        self.taken_by, self.order, self.index, self.highs = taken_by, [], {}, {}

    def add(self, name, reader):
        self.index[name] = len(self.order)
        if reader == "both":
            self.highs[name] = len(self.highs) + 1
            reader = "dve"
        self.order.append(reader)

    def no(self, name):
        return self.index[name] + 1

    def bank(self, name):
        return self.index[name] % 4

    def high(self, name):
        return self.highs[name]

    def count(self, i):
        reader = self.order[i]
        return self.taken_by[reader], self.order[:i + 1].count(reader)

    def taken(self, name):
        return self.count(self.index[name])

    def free(self, name):
        i = self.index[name]
        return self.count(i - 4) if i >= 4 else None


def plan_units(w):
    units = []

    def columns(name, src, c0, n, chunks):
        v = src.rearrange("(c p) n -> p c n", p=P)
        per = UNIT // n if n >= 256 else chunks
        per = min(per, chunks)
        if n > 256:
            per = 4
        for h in range(chunks // per):
            units.append((name + (h,), v[:, h * per:(h + 1) * per, c0:c0 + n], (per, n)))

    def rows(name, src, chunks):
        v = src.rearrange("(c p) n -> p c n", p=P)
        for h in range(chunks // 2):
            units.append((name + (h,), v[:, 2 * h:2 * h + 2, :], (2, D_MODEL)))

    for l in range(DEPTH):
        for g, (c0, n) in enumerate(ATT_GROUPS):
            columns(("p", l, g), w["w_in"][l], c0, n, KC)
        for g in range(GATE_GROUPS):
            columns(("g", l, g), w["w_in"][l], ATT + g * W, W, KC)
        rows(("wa", l), w["w_a_out"][l], 2)
        rows(("wb", l), w["w_b_out"][l], 2)
        rows(("wc", l), w["w_c_out"][l], 4)
        rows(("wo", l), w["w_o"][l], KC)
        if l == 0:
            for j, (c0, n) in enumerate(FF_GROUPS):
                columns(("w1", j), w["ffn_w1"][0], c0, n, KC)
                columns(("w3", j), w["ffn_w3"][0], c0, n, KC)
            rows(("w2",), w["ffn_w2"][0], FF_CHUNKS)
    return units


def hybrid_layers(nc, w, out, stop=None):
    with ExitStack() as ctx:
        def sb(name, shape, dt=F32):
            return ctx.enter_context(nc.sbuf_tensor(name, shape, dt))

        def sem(name):
            return ctx.enter_context(nc.semaphore(name))

        consts_loaded = sem("consts_loaded")
        mla_loaded = sem("mla_loaded")
        raw_loaded = [sem(f"raw_loaded{i}") for i in range(RAW)]
        e_raw_loaded = [sem(f"expert_raw_loaded{i}") for i in range(E_RAW)]
        high_split, e_high_split = sem("high_split_by_pool"), sem("expert_high_split_by_act")
        low_split = dict(pool=sem("low_split_by_pool"), dve=sem("low_split_by_dve"))
        unit_used = sem("unit_used")
        acc_ready, aux_ready = sem("acc_ready"), sem("aux_ready")
        acc_taken = dict(act=sem("acc_taken_by_act"), dve=sem("acc_taken_by_dve"))
        aux_taken = dict(act=sem("aux_taken_by_act"), dve=sem("aux_taken_by_dve"))
        high_taken = sem("high_taken_by_act")
        gates_ready = sem("gates_ready")
        pool_step = sem("pool_step")
        masks_ready = sem("masks_ready")
        dve_step = sem("dve_step")
        angles_ready = sem("angles_ready")
        trig_ready = sem("trig_ready")
        normed = sem("normed")
        lowrank_ready = sem("lowrank_ready")
        roped_a = sem("roped_a")
        roped_c = sem("roped_c")
        mla_heads_ready = sem("mla_heads_ready")
        relu_used = sem("relu_used")
        logits_ready = sem("logits_ready")
        probs_ready = sem("probs_ready")
        merged_ready = sem("merged_ready")
        hidden_ready = sem("hidden_ready")
        routed = sem("routed")
        passes_ready = sem("passes_ready")
        onehot_ready = sem("onehot_ready")
        stored = sem("stored")

        acc_bank = [ctx.enter_context(nc.psum_tensor(f"acc{i}", [P, W], F32)) for i in range(4)]
        aux_bank = [ctx.enter_context(nc.psum_tensor(f"aux{i}", [P, W], F32)) for i in range(4)]

        x_sb = sb("x_sb", [P, T, D_MODEL])
        xn = sb("xn", [P, T, D_MODEL])
        ident = sb("ident", [P, P])
        gainT = sb("gainT", [P, 64])
        lower, ones = sb("lower", [P, P]), sb("ones", [P, P])
        iota8, iota_slot = sb("iota8", [P, 8]), sb("iota_slot", [P, P])
        wr = sb("wr", [P, KC, N_EXP])
        xstat, xrstd = sb("xstat", [P, T]), sb("xrstd", [P, T])
        NST = 18 + 12
        newton = sb("newton", [P, 2, T, NST])

        phases = ExitStack()

        def lay(name, shape, dt=F32):
            return phases.enter_context(nc.sbuf_tensor(name, shape, dt))

        raw = lay("raw", [P, RAW, UNIT])
        part_h, part_l = lay("part_h", [P, PARTS, UNIT], F32R), lay("part_l", [P, PARTS, UNIT], F32R)
        hTh, hTl = lay("hTh", [P, KC, SEQ], F32R), lay("hTl", [P, KC, SEQ], F32R)
        kcz, kaz = lay("kcz", [P, C_KV, 2, SEQ]), lay("kaz", [P, 2, SEQ])
        ikz = lay("ikz", [P, 4, SEQ])
        uq, ukv = lay("uq", [P, 2, 384]), lay("ukv", [P, 512])
        cmask, wmask = lay("cmask", [P, SEQ]), lay("wmask", [P, SEQ])
        GAINS = dict(aq=(0, 64), ak=(64, 64), qn=(128, 64), qr=(192, 32), kn=(224, 64), kr=(288, 32),
                     cq=(320, 64), ck=(384, 64), sink=(448, 8))
        gains = lay("gains", [P, DEPTH, 456])
        cos64, sin64 = lay("cos64", [P, T, 64]), lay("sin64", [P, T, 64])
        cos32, sin32 = lay("cos32", [P, T, 32]), lay("sin32", [P, T, 32])
        invn = lay("invn", [P, NST])

        scratch = ExitStack()

        def mix(name, shape, dt=F32):
            return scratch.enter_context(nc.sbuf_tensor(name, shape, dt))

        proj = mix("proj", [P, T, ATT])
        gates = mix("gates", [P, T, 3 * D_MODEL])
        swing = mix("swing", [P, 1280])
        logit = mix("logit", [P, 2, 4, SEQ])
        probT = mix("probT", [P, 2, 8, P])
        sq = probT[:, :, :, :].rearrange("p a b c -> p (a b c)")
        qcT = mix("qcT", [P, 4, SEQ])
        cqT, iqT = qcT[:, 0:2, :], qcT[:, 2:4, :]
        qaT = mix("qaT", [P, 2, SEQ])
        qbT, kbT = mix("qbT", [P, B_HEADS, SEQ]), mix("kbT", [P, B_HEADS, SEQ])
        ckvT = mix("ckvT", [P, SEQ])
        kc2, ka2, ik4 = mix("kc2", [P, T, C_KV, P]), mix("ka2", [P, T, P]), mix("ik4", [P, T, P])
        qb, kvb = mix("qb", [P, T, 384]), mix("kvb", [P, T, 512])
        kcat = mix("kcat", [P, T, B_HEADS, 96])
        selmask = mix("selmask", [P, T, SEQ])
        ang = mix("ang", [P, 4, T, 32])
        score = ang[:, :, :, :].rearrange("p a t d -> p (a t d)")
        start_of = gates[:, :, :].rearrange("p t n -> p (t n)")
        gain_rows = start_of[0:64, 0:P]
        trig = start_of[:, P:P + 2 * T * 32].rearrange("p (a t d) -> p a t d", a=2, t=T)
        freq, pos_f = start_of[:, 256:288], start_of[:, 288:290]
        pos_i = mix("pos_i", [P, T], I32)
        stat, rstd = mix("stat", [P, T, NST]), mix("rstd", [P, T, NST])
        iws = mix("iws", [P, T, IDX_HEADS])
        top8 = mix("top8", [P, 8])
        nmax, denom = mix("nmax", [P, 2, 4]), mix("denom", [P, 4, 4])
        sinkx, rden = mix("sinkx", [P, 4, 2, 4]), mix("rden", [P, 4, 4])
        scratch.close()

        ffn = ExitStack()
        ffTh = ffn.enter_context(nc.sbuf_tensor("ffTh", [P, FF_CHUNKS, SEQ], F32R))
        ffTl = ffn.enter_context(nc.sbuf_tensor("ffTl", [P, FF_CHUNKS, SEQ], F32R))
        ff_silu = ffn.enter_context(nc.sbuf_tensor("ff_silu", [P, T, W], F32))
        ff_hidden = ffn.enter_context(nc.sbuf_tensor("ff_hidden", [P, T, W], F32))
        ffn.close()
        phases.close()

        e_raw = sb("e_raw", [P, E_RAW, UNIT])
        e_part_h, e_part_l = sb("e_part_h", [P, E_PARTS, UNIT], F32R), sb("e_part_l", [P, E_PARTS, UNIT], F32R)
        h2T = sb("h2T", [P, KC, SEQ])
        rl, rtop, ridx = sb("rl", [P, T, 8]), sb("rtop", [P, T, 8]), sb("ridx", [P, T, 8], U32)
        ridxf = sb("ridxf", [P, T, 8])
        gate2, onehot = sb("gate2", [P, T, 2]), sb("onehot", [P, T, 2, 8])
        chosen, gated = sb("chosen", [P, T, 8]), sb("gated", [P, T, 9])
        slot_flat = sb("slot_flat", [P, T, 2 * N_EXP + 1])
        slot_of = slot_flat[:, :, 0:2 * N_EXP].rearrange("p t (s e) -> p t s e", s=2)
        n_pass = sb("n_pass", [P, 2], I32)
        cnt = sb("cnt", [P, 4])
        pick, pickg, pickT = (sb(n, [P, T, P]) for n in ("pick", "pickg", "pickT"))
        xgTh, xgTl = sb("xgTh", [P, KC, P], F32R), sb("xgTl", [P, KC, P], F32R)
        hidTh, hidTl = sb("hidTh", [P, E_CHUNKS, P], F32R), sb("hidTl", [P, E_CHUNKS, P], F32R)
        silu, hidden = sb("silu", [P, 2, W]), sb("hidden", [P, 2, W])
        ysb = sb("ysb", [P, D_MODEL])

        acc, aux = BankRing(acc_taken), BankRing(aux_taken)
        for l in range(DEPTH):
            for g in range(len(ATT_GROUPS)):
                for t in range(T):
                    acc.add(("p", l, g, t), "act")
            for g in range(GATE_GROUPS):
                for t in range(T):
                    acc.add(("g", l, g, t), "act")
            for m in "abc":
                for t in range(T):
                    for h in range(2):
                        acc.add(("m", l, m, t, h), "dve")
            for t in range(T):
                for h in range(2):
                    acc.add(("o", l, t, h), "dve")
            if l == 0:
                for j in range(len(FF_GROUPS)):
                    for t in range(T):
                        acc.add(("h1", j, t), "act")
                    for t in range(T):
                        acc.add(("h3", j, t), "dve")
                for t in range(T):
                    for h in range(2):
                        acc.add(("y", t, h), "dve")
        aux.add(("gains",), "act")
        for l in range(DEPTH):
            for i in range(4):
                aux.add(("h", l, i), "both")
            for n in ("cq", "ckv", "ika", "iq", "qa"):
                aux.add((n, l), "act")
            for n in ("uq", "ukv"):
                for t in range(T):
                    aux.add((n, l, t), "act")
            for t in range(T):
                for i in range(2 * (t + 1)):
                    aux.add(("ix", l, t, i), "act")
            for n in ("kc", "qc0", "qc1", "qb0", "qb1", "kb0", "kb1"):
                aux.add((n, l), "act")
            for s in range(len(JOBS) + 2):
                if s < len(JOBS):
                    for i in range(JOBS[s][1] + 1):
                        aux.add(("lg", l, s, i), "dve")
                if 1 <= s <= len(JOBS):
                    for i in range(JOBS[s - 1][1] + 1):
                        aux.add(("pt", l, s - 1, i), "act")
                if s >= 2:
                    aux.add(("pv", l, s - 2), "dve")
            for i in range(4):
                aux.add(("yt", l, i), "both")
            for i in range(4):
                aux.add(("mt", l, i), "both")
            for i in range(4):
                aux.add(("f", l, i), "both" if l == 0 else "act")
            if l == 0:
                for j in range(len(FF_GROUPS)):
                    for t in range(T):
                        aux.add(("ht", j, t), "both")
        aux.add(("router", 0), "act")
        aux.add(("router", 1), "act")
        aux.add(("slots",), "dve")
        for i in range(4):
            aux.add(("x", i), "both")
        for h in range(2):
            acc.add(("y0", h), "act")
        ACC0, AUX0 = len(acc.order), len(aux.order)
        E_ACC = ["act", "dve"] * E_GROUPS + ["act", "act"]
        HT = [0, 5] + list(range(7, 7 + E_GROUPS - 2))
        CB, PG = [1, 2, 3, 4], 6
        X0 = 7 + E_GROUPS - 2
        E_AUX = ["act" if i == PG else "dve" for i in range(X0 + 4)]
        HIGH0, E_HIGHS = len(aux.highs), 4 + E_GROUPS
        assert len(E_ACC) % 4 == 0 and len(E_AUX) % 4 == 0

        units = plan_units(w)
        UNITS0 = len(units)
        unit_no = {name: n for n, (name, _, _) in enumerate(units)}
        shape_of = {name: s for name, _, s in units}

        def in_slot(ring, n, shape):
            return ring[:, n, 0:shape[0] * shape[1]].rearrange("p (c n) -> p c n", n=shape[1])

        def parts(name):
            n, shape = unit_no[name], shape_of[name]
            return in_slot(part_h, n % PARTS, shape), in_slot(part_l, n % PARTS, shape)

        def e_parts(u, shape):
            return in_slot(e_part_h, u % E_PARTS, shape), in_slot(e_part_l, u % E_PARTS, shape)

        low_by = ["pool" if name[0] == "g" else "dve" for name, _, _ in units]
        LOW0 = low_by.count("dve")

        def low_done(n):
            return low_split[low_by[n]], low_by[:n + 1].count(low_by[n])

        def arrived(name):
            return low_done(unit_no[name])

        ends_fill = {}
        for l in range(DEPTH):
            for g in range(len(ATT_GROUPS)):
                ends_fill["p", l, g, 1] = ("p", l, g, 1)
            for g in range(GATE_GROUPS):
                ends_fill["g", l, g, 1] = ("g", l, g, 1)
            ends_fill["wa", l, 0] = ("m", l, "a", 1, 1)
            ends_fill["wb", l, 0] = ("m", l, "b", 1, 1)
            ends_fill["wc", l, 1] = ("m", l, "c", 1, 1)
            ends_fill["wo", l, 3] = ("o", l, 1, 1)
        for j, (_, n) in enumerate(FF_GROUPS):
            last = 1 if n > 256 else 0
            ends_fill["w1", j, last] = ("h1", j, 1)
            ends_fill["w3", j, last] = ("h3", j, 1)
        ends_fill["w2", FF_CHUNKS // 2 - 1] = ("y", 1, 1)
        own = [n for n, (name, _, _) in enumerate(units) if name not in ends_fill]
        assert all(name in unit_no for name in ends_fill)
        OWN0 = len(own)

        def released(n):
            name = units[n][0]
            if name in ends_fill:
                return acc_ready, acc.no(ends_fill[name])
            return unit_used, own.index(n) + 1

        E_OWN = [u for u in range(E_UNITS) if not ((u < 4 * E_GROUPS and u % 2) or u == E_UNITS - 1)]

        def e_released(u, it):
            if u in E_OWN:
                return unit_used, it * len(E_OWN) + (OWN0 + E_OWN.index(u) + 1)
            fill = u // 2 + 1 if u < 4 * E_GROUPS else len(E_ACC)
            return acc_ready, it * len(E_ACC) + (ACC0 + fill)

        def e_free_part(u, it):
            if u >= E_PARTS:
                return e_released(u - E_PARTS, it)
            s, v = e_released(E_UNITS + u - E_PARTS, it)
            return s, v - (len(E_OWN) if s is unit_used else len(E_ACC))

        def e_free(ring0, order, i, it):
            base = {r: ring0[1].order.count(r) for r in ("act", "dve")}
            if i >= 4:
                r = order[i - 4]
                return ring0[1].taken_by[r], it * order.count(r) + (base[r] + order[:i - 3].count(r))
            r = order[i - 4]
            return ring0[1].taken_by[r], it * order.count(r) + (base[r] - order[len(order) + i - 3:].count(r))

        def e_taken(ring0, order, i, it):
            r = order[i]
            base = ring0[1].order.count(r)
            return ring0[1].taken_by[r], it * order.count(r) + (base + order[:i + 1].count(r))

        ACCR, AUXR = (ACC0, acc), (AUX0, aux)
        X_AFTER = 4

        def rows_of(name, l, n):
            return w[name][l].rearrange("(c p) -> c p", p=P), n // P
        small = []
        r = 0
        GROW = {}
        for name, n in (("attn_norm_g", D_MODEL), ("ffn_norm_g", D_MODEL), ("b_cq_norm_g", B_QR), ("b_ckv_norm_g", B_KVR)):
            k = DEPTH * n // P
            small.append((gain_rows[r:r + k, :], w[name].rearrange("l (c p) -> (l c) p", p=P)))
            for l in range(DEPTH):
                GROW[name, l] = r + l * n // P
            r += k
        NROWS = r
        for key, name in (("aq", "a_q_norm_g"), ("ak", "a_k_norm_g"), ("qn", "b_qn_g"), ("qr", "b_qr_g"), ("kn", "b_kn_g"),
                          ("kr", "b_kr_g"), ("cq", "c_q_norm_g"), ("ck", "c_k_norm_g"), ("sink", "c_sinks")):
            o, n = GAINS[key]
            small.append((gains[:, :, o:o + n], w[name].partition_broadcast(P)))
        small.append((pos_i[:, :], w["positions"].rearrange("b (t p) -> p (b t)", p=P)))
        small.append((wr[:, :, :], w["router_w"][0].rearrange("(c p) e -> p c e", p=P)))
        x_view = w["x"].rearrange("b (t p) d -> p (b t) d", p=P)
        out_view = out.rearrange("b (t p) d -> p (b t) d", p=P)
        small.append((x_sb[:, :, :], x_view))
        CONSTS = 16 * len(small)

        def gain(key, l, heads):
            o, n = GAINS[key]
            return gains[:, l:l + 1, o:o + n].unsqueeze(1).to_broadcast([P, T, heads, n])

        def heads_of(buf, c0, heads, d):
            return buf[:, :, c0:c0 + heads * d].rearrange("p t (h d) -> p t h d", d=d)

        block = ctx.enter_context(nc.Block())

        @block.scalar
        def _(act):
            for dst, src in small:
                act.dma_start(dst, src, allow_slow_non_contiguous=(dst.dtype == I32)).then_inc(consts_loaded, 16)

            def take_aux(name, dst, src=None, func=ACT.Copy, **kw):
                act.wait_ge(aux_ready, aux.no(name))
                b = aux_bank[aux.bank(name)]
                return act.activation(dst, b[:, :] if src is None else src(b), func, **kw).then_inc(aux_taken["act"], 1)

            take_aux(("gains",), gainT[:, 0:NROWS], lambda b: b[:, 0:NROWS])
            act.wait_ge(angles_ready, 1)
            act.activation(trig[:, :, :, :], ang[:, 2:4, :, :], ACT.Sin).then_inc(trig_ready, 1)

            def take_high(name, cols):
                act.wait_ge(aux_ready, aux.no(name))
                b = aux_bank[aux.bank(name)]
                n = cols.shape[1] * cols.shape[2]
                act.activation(cols, b[:, 0:n].rearrange("p (c n) -> p c n", n=cols.shape[2]), ACT.Copy)\
                   .then_inc(high_taken, 1)

            def take_transposed(kind, l, row, dst):
                for i in range(4):
                    act.wait_ge(aux_ready, aux.no((kind, l, i)))
                    b = aux_bank[aux.bank((kind, l, i))]
                    for c in range(2):
                        ins = act.activation(dst[:, 2 * i + c, :], b[:, c * SEQ:(c + 1) * SEQ], ACT.Copy,
                                             scale=gainT[:, row + 2 * i + c:row + 2 * i + c + 1])
                    ins.then_inc(high_taken if (kind, l, i) in aux.highs else aux_taken["act"], 1)

            for l in range(DEPTH):
                act.wait_ge(*aux.taken(("gains",)))
                take_transposed("h", l, GROW["attn_norm_g", l], hTh)
                for g, (c0, n) in enumerate(ATT_GROUPS):
                    for t in range(T):
                        act.wait_ge(acc_ready, acc.no(("p", l, g, t)))
                        act.activation(proj[:, t, c0:c0 + n], acc_bank[acc.bank(("p", l, g, t))][:, 0:n], ACT.Copy)\
                           .then_inc(acc_taken["act"], 1)

                def take_gates(g, func):
                    for t in range(T):
                        act.wait_ge(acc_ready, acc.no(("g", l, g, t)))
                        act.activation(gates[:, t, g * W:(g + 1) * W], acc_bank[acc.bank(("g", l, g, t))][:, :],
                                       func).then_inc(acc_taken["act"], 1)

                take_gates(0, ACT.Sigmoid)
                act.wait_ge(aux_ready, aux.no(("cq", l)))
                b, r = aux_bank[aux.bank(("cq", l))], GROW["b_cq_norm_g", l]
                for c in range(2):
                    ins = act.activation(cqT[:, c, :], b[:, c * SEQ:(c + 1) * SEQ], ACT.Copy, scale=gainT[:, r + c:r + c + 1])
                ins.then_inc(aux_taken["act"], 1)
                r = GROW["b_ckv_norm_g", l]
                take_aux(("ckv", l), ckvT[:, :], lambda b: b[:, 0:SEQ], scale=gainT[:, r:r + 1])
                act.wait_ge(aux_ready, aux.no(("ika", l)))
                b = aux_bank[aux.bank(("ika", l))]
                for v in range(2):
                    act.activation(kaz[64 * v:64 * v + 64, v, :], b[64 * v:64 * v + 64, 0:SEQ], ACT.Copy)
                for v in range(4):
                    ins = act.activation(ikz[32 * v:32 * v + 32, v, :], b[32 * v:32 * v + 32, SEQ:2 * SEQ], ACT.Copy)
                ins.then_inc(aux_taken["act"], 1)
                take_aux(("iq", l), iqT[:, :, :].rearrange("p a b -> p (a b)"))
                take_aux(("qa", l), qaT[:, :, :].rearrange("p a b -> p (a b)"))
                for t in range(T):
                    take_aux(("uq", l, t), qb[:, t, :], lambda b: b[:, 0:384])
                for t in range(T):
                    take_aux(("ukv", l, t), kvb[:, t, :])
                n = 0
                act.wait_ge(roped_c, l + 1)
                for t in range(T):
                    for i in range(2 * (t + 1)):
                        k = 6 * l + n
                        if n >= 2:
                            act.wait_ge(relu_used, k - 1)
                        act.wait_ge(aux_ready, aux.no(("ix", l, t, i)))
                        act.activation(swing[:, (n % 2) * W:(n % 2 + 1) * W], aux_bank[aux.bank(("ix", l, t, i))][:, :],
                                       ACT.Relu).then_inc(aux_taken["act"], 1)
                        n += 1
                take_gates(1, ACT.Sigmoid)
                act.wait_ge(aux_ready, aux.no(("kc", l)))
                b = aux_bank[aux.bank(("kc", l))]
                for kv in range(C_KV):
                    for v in range(2):
                        ins = act.activation(kcz[64 * v:64 * v + 64, kv, v, :],
                                             b[64 * v:64 * v + 64, kv * SEQ:(kv + 1) * SEQ], ACT.Copy)
                ins.then_inc(aux_taken["act"], 1)
                for i in range(2):
                    take_aux((f"qc{i}", l), qcT[:, 2 * i:2 * i + 2, :].rearrange("p a b -> p (a b)"))
                for nm, dst in (("qb", qbT), ("kb", kbT)):
                    for i in range(2):
                        take_aux((f"{nm}{i}", l), dst[0:96, 2 * i:2 * i + 2, :].rearrange("p a b -> p (a b)"),
                                 lambda b: b[0:96, :])
                take_gates(2, ACT.Sigmoid)
                for s in range(len(JOBS) + 2):
                    if s < len(JOBS):
                        m, t = JOBS[s]
                        nk, job = P * (t + 1), len(JOBS) * l + s
                        act.wait_ge(logits_ready, job + 1)
                        if m[0] == "c":
                            act.activation(sinkx[:, s % 4, 1, :], sinkx[:, s % 4, 0, :], ACT.Exp)
                        for h in range(4):
                            row = logit[:, s % 2, h, 0:nk]
                            ins = act.activation(row, row, ACT.Exp, bias=nmax[:, s % 2, h:h + 1],
                                                 accum_out=denom[:, s % 4, h:h + 1])
                        ins.then_inc(probs_ready, 1)
                    if s in (1, 3, 5):
                        take_gates(3 + s // 2, ACT.Copy)
                    if 1 <= s <= len(JOBS):
                        q, tq = s - 1, JOBS[s - 1][1]
                        if q >= 2:
                            act.wait_ge(aux_ready, aux.no(("pv", l, q - 2)))
                        for i in range(tq + 1):
                            take_aux(("pt", l, q, i), probT[:, q % 2, 4 * i:4 * i + 4, :].rearrange("p a b -> p (a b)"))
                for i in range(4):
                    if i == 0:
                        act.wait_ge(acc_ready, acc.no(("g", l, GATE_GROUPS - 1, T - 1)))
                    take_high(("yt", l, i), hTh[:, 2 * i:2 * i + 2, :])
                late = gates[:, :, 3 * W:]
                act.wait_ge(*acc.taken(("g", l, GATE_GROUPS - 1, T - 1)))
                act.activation(late, late, ACT.Sigmoid).then_inc(gates_ready, 1)
                act.wait_ge(acc_ready, acc.no(("m", l, "c", 1, 1)))
                for i in range(4):
                    take_high(("mt", l, i), hTh[:, 2 * i:2 * i + 2, :])
                act.wait_ge(acc_ready, acc.no(("o", l, 1, 1)))
                take_transposed("f", l, GROW["ffn_norm_g", l], hTh if l == 0 else h2T)
                if l == 0:
                    def take_hidden(j):
                        n = FF_GROUPS[j][1]
                        for t in range(T):
                            take_high(("ht", j, t), ffTh[:, 4 * j:4 * j + n // P, t * P:(t + 1) * P])

                    for j, (_, n) in enumerate(FF_GROUPS):
                        for t in range(T):
                            act.wait_ge(acc_ready, acc.no(("h1", j, t)))
                            if j:
                                act.wait_ge(*acc.taken(("h3", j - 1, t)))
                            act.activation(ff_silu[:, t, 0:n], acc_bank[acc.bank(("h1", j, t))][:, 0:n], ACT.Silu)\
                               .then_inc(acc_taken["act"], 1)
                        if j:
                            take_hidden(j - 1)
                    take_hidden(len(FF_GROUPS) - 1)

            for t in range(T):
                take_aux(("router", t), rl[:, t, :], lambda b: b[:, 0:N_EXP])
            act.wait_ge(routed, 1)
            act.activation(gate2[:, :, 1:2], gate2[:, :, 0:1], ACT.Exp).then_inc(routed, 1)

            def take_gathered(i, ready):
                row = GROW["ffn_norm_g", 1]
                act.wait_ge(aux_ready, ready)
                for c in range(2):
                    k = 2 * i + c
                    ins = act.activation(xgTh[:, k, :], aux_bank[(AUX0 + i) % 4][:, c * P:(c + 1) * P], ACT.Copy,
                                         scale=gainT[:, row + k:row + k + 1])
                ins.then_inc(high_taken, 1)

            def take_result(it):
                for h in range(2):
                    act.wait_ge(acc_ready, it * len(E_ACC) + (ACC0 - 1 + h))
                    act.activation(ysb[:, h * W:(h + 1) * W], acc_bank[(ACC0 - 2 + h) % 4][:, :], ACT.Copy)\
                       .then_inc(acc_taken["act"], 1)

            for i in range(4):
                take_gathered(i, aux.no(("x", i)))
            act.wait_ge(passes_ready, 1)
            passes = act.value_load(n_pass[0:1, 0:1], min_val=1, max_val=2)
            with act.Fori(0, passes) as ps:
                with act.Fori(0, N_EXP) as e:
                    it = ps * N_EXP + e

                    def split_high(u):
                        act.wait_ge(e_raw_loaded[u % E_RAW], it * (16 * (E_UNITS // E_RAW)) + 16 * (u // E_RAW + 1))
                        act.wait_ge(*e_free_part(u, it))
                        act.activation(e_part_h[:, u % E_PARTS, :], e_raw[:, u % E_RAW, :], ACT.Copy).then_inc(e_high_split, 1)

                    def take_expert_hidden(j):
                        act.wait_ge(aux_ready, it * len(E_AUX) + (AUX0 + HT[j] + 1))
                        act.activation(hidTh[:, 4 * j:4 * j + 4, :].rearrange("p a b -> p (a b)"),
                                       aux_bank[(AUX0 + HT[j]) % 4][:, :], ACT.Copy).then_inc(high_taken, 1)

                    for u in range(3):
                        split_high(u)
                    for j in range(E_GROUPS):
                        split_high(4 * j + 3)
                        if j == 0:
                            take_result(it)
                        act.wait_ge(acc_ready, it * len(E_ACC) + (ACC0 + 2 * j + 1))
                        if j >= 2:
                            act.wait_ge(*e_taken(ACCR, E_ACC, 2 * j - 3, it))
                        act.activation(silu[:, j % 2, 0:W], acc_bank[(ACC0 + 2 * j) % 4][:, :], ACT.Silu)\
                           .then_inc(acc_taken["act"], 1)
                        split_high(4 * j + 4)
                        if j:
                            take_expert_hidden(j - 1)
                        if j == 2:
                            act.wait_ge(aux_ready, it * len(E_AUX) + (AUX0 + PG + 1))
                            act.activation(pickT[:, :, :].rearrange("p a b -> p (a b)"),
                                           aux_bank[(AUX0 + PG) % 4][:, 0:T * P], ACT.Copy).then_inc(aux_taken["act"], 1)
                        split_high(4 * j + 5)
                        split_high(4 * j + 6)
                    for u in range(4 * E_GROUPS + 3, E_UNITS):
                        split_high(u)
                        if u == 4 * E_GROUPS + 4:
                            take_expert_hidden(E_GROUPS - 1)
                        if u == 4 * E_GROUPS + X_AFTER + 2:
                            for i in range(4):
                                take_gathered(i, it * len(E_AUX) + (AUX0 + X0 + i + 1))
            take_result(passes * N_EXP)

        @block.gpsimd
        def _(pool):
            steps = [0]

            def link(ins):
                steps[0] += 1
                ins.then_inc(pool_step, 1)
                pool.wait_ge(pool_step, steps[0])

            inv_freq = np.float32(10000.0) ** (-np.arange(32, dtype=np.float32) / np.float32(32))
            for i in range(32):
                pool.memset(freq[:, i:i + 1], float(inv_freq[i]))
            for c0, c1, n in ((0, 5, 64), (5, 6, B_QR), (6, 7, B_KVR), (7, 8, B_ROPE), (8, 18, 64),
                              (18, 22, 64), (22, 26, 32), (26, 30, 64)):
                pool.memset(invn[:, c0:c1], 1.0 / n)
            for z in (kcz[:, :, :, :], kaz[:, :, :], ikz[:, :, :], cmask[:, :], wmask[:, :], ident[:, :]):
                pool.memset(z, 0.0)
            pool.memset(ones[:, :], 1.0)
            link(pool.memset(lower[:, :], 1.0))
            pool.affine_select(out=ident[:, :], in_=ident[:, :], compare_op=ALU.not_equal, fill=1.0, base=0,
                               pattern=[[-1, P]], channel_multiplier=1)
            pool.affine_select(out=cmask[:, P:], in_=cmask[:, P:], compare_op=ALU.is_ge, fill=MASKED, base=0,
                               pattern=[[-1, P]], channel_multiplier=1)
            pool.affine_select(out=wmask[:, P:], in_=wmask[:, P:], compare_op=ALU.is_ge, fill=MASKED, base=0,
                               pattern=[[-1, P]], channel_multiplier=1)
            pool.affine_select(out=wmask[:, 0:P], in_=wmask[:, 0:P], compare_op=ALU.is_gt, fill=MASKED, base=0,
                               pattern=[[1, P]], channel_multiplier=-1)
            pool.affine_select(out=lower[:, :], in_=lower[:, :], compare_op=ALU.is_gt, fill=0.0, base=0,
                               pattern=[[1, P]], channel_multiplier=-1)
            pool.iota(iota8[:, :], pattern=[[1, N_EXP]], base=0, channel_multiplier=0, allow_small_or_imprecise_dtypes=True)
            pool.iota(iota_slot[:, :], pattern=[[1, P]], base=0, channel_multiplier=0,
                      allow_small_or_imprecise_dtypes=True).then_inc(masks_ready, 1)
            for n, (name, _, shape) in enumerate(units):
                k = shape[0] * shape[1]
                pool.wait_ge(raw_loaded[n % RAW], 16 * (n // RAW + 1))
                if n >= PARTS:
                    pool.wait_ge(*released(n - PARTS))
                pool.tensor_scalar(part_h[:, n % PARTS, 0:k], raw[:, n % RAW, 0:k], 1.0, 1.0, ALU.mult, ALU.mult)\
                    .then_inc(high_split, 1)
                if low_by[n] == "pool":
                    pool.wait_ge(high_split, n + 1)
                    pool.tensor_tensor(part_l[:, n % PARTS, 0:k], raw[:, n % RAW, 0:k],
                                       part_h[:, n % PARTS, 0:k].bitcast(F32), ALU.subtract).then_inc(low_split["pool"], 1)

        @block.vector
        def _(dve):
            steps, splits = [0], [0]

            def link(ins):
                steps[0] += 1
                ins.then_inc(dve_step, 1)
                dve.wait_ge(dve_step, steps[0])

            def root(y, v, tmp):
                link(dve.tensor_scalar(tmp.bitcast(I32), v.bitcast(I32), 1, None, ALU.logical_shift_right))
                link(dve.tensor_scalar(y.bitcast(I32), tmp.bitcast(I32), -1.0, float(0x5f3759df), ALU.mult, ALU.add))
                for _ in range(3):
                    link(dve.tensor_tensor(tmp, y, y, ALU.mult))
                    link(dve.scalar_tensor_tensor(out=tmp, in0=tmp, scalar=-0.5, in1=v, op0=ALU.mult, op1=ALU.mult))
                    link(dve.scalar_tensor_tensor(out=y, in0=tmp, scalar=1.5, in1=y, op0=ALU.add, op1=ALU.mult))

            own_units = [n for n in range(UNITS0) if low_by[n] == "dve"]

            def split_low(count):
                for n in own_units[splits[0]:splits[0] + count]:
                    k = units[n][2][0] * units[n][2][1]
                    dve.wait_ge(high_split, n + 1)
                    dve.tensor_tensor(part_l[:, n % PARTS, 0:k], raw[:, n % RAW, 0:k],
                                      part_h[:, n % PARTS, 0:k].bitcast(F32), ALU.subtract).then_inc(low_split["dve"], 1)
                splits[0] += count

            def name_of_next():
                return units[own_units[splits[0]]][0]

            def take_low(name, dst, high, rows=None):
                dve.wait_ge(high_taken, aux.high(name))
                b = aux_bank[aux.bank(name)]
                n = dst.shape[2]
                if rows is None:
                    dve.tensor_tensor(dst, b[:, 0:dst.shape[1] * n].rearrange("p (c n) -> p c n", n=n), high.bitcast(F32),
                                      ALU.subtract).then_inc(aux_taken["dve"], 1)
                    return
                for c in range(2):
                    ins = dve.scalar_tensor_tensor(out=dst[:, c, :], in0=b[:, c * n:(c + 1) * n], scalar=rows[:, c:c + 1],
                                                   in1=high[:, c, :].bitcast(F32), op0=ALU.mult, op1=ALU.subtract)
                ins.then_inc(aux_taken["dve"], 1)

            def take_low_four(kind, l, row=None):
                for i in range(4):
                    rows = None if row is None else gainT[:, row + 2 * i:row + 2 * i + 2]
                    take_low((kind, l, i), hTl[:, 2 * i:2 * i + 2, :], hTh[:, 2 * i:2 * i + 2, :], rows)

            dve.wait_ge(consts_loaded, CONSTS)
            dve.wait_ge(masks_ready, 1)
            TWO_PI, MAGIC = 2.0 * np.pi, 1.5 * 2.0 ** 23
            C1 = 6.28125
            C2 = float(np.round((TWO_PI - C1) * 2 ** 19) / 2 ** 19)
            C3 = float(TWO_PI - C1 - C2)
            link(dve.tensor_copy(pos_f[:, :], pos_i[:, :]))
            link(dve.tensor_tensor(ang[:, 0, :, :], freq[:, :].unsqueeze(1).to_broadcast([P, T, 32]),
                                   pos_f[:, :].unsqueeze(2).to_broadcast([P, T, 32]), ALU.mult))
            for row, turn, shift in ((2, 0.0, 0.0), (3, 0.25, np.pi / 2)):
                r = ang[:, row, :, :]
                k = ang[:, 1, :, :]
                link(dve.tensor_scalar(k, ang[:, 0, :, :], float(1.0 / TWO_PI), turn, ALU.mult, ALU.add))
                link(dve.tensor_scalar(k, k, MAGIC, None, ALU.add))
                link(dve.tensor_scalar(k, k, -MAGIC, None, ALU.add))
                link(dve.scalar_tensor_tensor(out=r, in0=k, scalar=-C1, in1=ang[:, 0, :, :], op0=ALU.mult, op1=ALU.add))
                link(dve.scalar_tensor_tensor(out=r, in0=k, scalar=-C2, in1=r, op0=ALU.mult, op1=ALU.add))
                link(dve.scalar_tensor_tensor(out=r, in0=k, scalar=-C3, in1=r, op0=ALU.mult, op1=ALU.add))
                link(dve.tensor_scalar(r, r, float(shift), 3.1415925, ALU.add, ALU.min))
                ins = dve.tensor_scalar(r, r, -3.1415925, None, ALU.max)
                if row == 2:
                    link(ins)
            ins.then_inc(angles_ready, 1)
            dve.wait_ge(trig_ready, 1)
            sin, cos = trig[:, 0, :, :], trig[:, 1, :, :]
            for h in range(2):
                dve.tensor_copy(cos64[:, :, 32 * h:32 * h + 32], cos)
                dve.tensor_copy(cos32[:, :, 16 * h:16 * h + 16], cos[:, :, 0:32:2])
                dve.tensor_scalar(sin64[:, :, 32 * h:32 * h + 32], sin, 2.0 * h - 1.0, None, ALU.mult)
                ins = dve.tensor_scalar(sin32[:, :, 16 * h:16 * h + 16], sin[:, :, 0:32:2], 2.0 * h - 1.0, None, ALU.mult)
            link(ins)

            def norm_x():
                for t in range(T):
                    ins = dve.scalar_tensor_tensor(out=swing[:, 0:D_MODEL], in0=x_sb[:, t, :], scalar=1.0, in1=x_sb[:, t, :],
                                                   op0=ALU.mult, op1=ALU.mult, accum_out=xstat[:, t:t + 1])
                    link(ins)
                link(dve.tensor_scalar(xstat[:, :], xstat[:, :], 1.0 / D_MODEL, EPS, ALU.mult, ALU.add))
                root(xrstd[:, :], xstat[:, :], newton[:, 0, :, 0])
                for t in range(T):
                    dve.tensor_scalar(xn[:, t, :], x_sb[:, t, :], xrstd[:, t:t + 1], None, ALU.mult).then_inc(normed, 1)

            def mean_square(dst, view, width):
                link(dve.tensor_reduce(dst, view, AX_X, ALU.add))

            def finish_means(c0, c1):
                link(dve.tensor_tensor(stat[:, :, c0:c1], stat[:, :, c0:c1],
                                       invn[:, c0:c1].unsqueeze(1).to_broadcast([P, T, c1 - c0]), ALU.mult))
                link(dve.tensor_scalar(stat[:, :, c0:c1], stat[:, :, c0:c1], EPS, None, ALU.add))
                root(rstd[:, :, c0:c1], stat[:, :, c0:c1], newton[:, 0, :, c0:c1])

            def scale_heads(v, c0, heads, d):
                r = rstd[:, :, c0:c0 + heads].unsqueeze(3).to_broadcast([P, T, heads, d])
                link(dve.tensor_tensor(v, v, r, ALU.mult))

            def rotate(v, heads, d, dsts):
                half = d // 2
                cs, sn = (cos64, sin64) if d == 64 else (cos32, sin32)
                tmp = swing[:, 0:T * heads * d].rearrange("p (t h d) -> p t h d", t=T, d=d)

                def over(a):
                    return a.unsqueeze(2).to_broadcast([P, T, heads, a.shape[-1]])
                dve.tensor_tensor(tmp[:, :, :, 0:half], v[:, :, :, half:], over(sn[:, :, 0:half]), ALU.mult)
                link(dve.tensor_tensor(tmp[:, :, :, half:], v[:, :, :, 0:half], over(sn[:, :, half:]), ALU.mult))
                link(dve.tensor_tensor(v, v, over(cs[:, :, :]), ALU.mult))
                for dst in dsts:
                    ins = dve.tensor_tensor(dst, v, tmp, ALU.add)
                return ins

            def squares(c0, n, off):
                v = sq[:, off:off + T * n].rearrange("p (t n) -> p t n", t=T)
                link(dve.tensor_tensor(v, proj[:, :, c0:c0 + n], proj[:, :, c0:c0 + n], ALU.mult))
                return v

            def add_to_x(l_fill, t, h):
                b = acc_bank[acc.bank(l_fill)]
                dve.wait_ge(acc_ready, acc.no(l_fill))
                xs = x_sb[:, t, h * W:(h + 1) * W]
                dve.tensor_tensor(xs, xs, b[:, :], ALU.add).then_inc(acc_taken["dve"], 1)

            for l in range(DEPTH):
                if l:
                    dve.wait_ge(*acc.taken(("y", 1, 1)))
                norm_x()
                if l == 0:
                    split_low(1)
                dve.wait_ge(*aux.taken(("gains",)))
                take_low_four("h", l, GROW["attn_norm_g", l])
                split_low(2 * len(ATT_GROUPS) - 1)
                dve.wait_ge(*acc.taken(("p", l, len(ATT_GROUPS) - 1, 1)))
                v = squares(COL["cq"], 416, 0)
                mean_square(stat[:, :, 5:6], v[:, :, 0:256].unsqueeze(2), 256)
                mean_square(stat[:, :, 6:7], v[:, :, 256:384].unsqueeze(2), 128)
                mean_square(stat[:, :, 7:8], v[:, :, 384:416].unsqueeze(2), 32)
                v = squares(0, 320, 900)
                mean_square(stat[:, :, 0:5], v.rearrange("p t (h d) -> p t h d", d=64), 64)
                finish_means(0, 8)
                scale_heads(heads_of(proj, COL["cq"], 1, 256), 5, 1, 256)
                dve.tensor_tensor(heads_of(proj, COL["ckv"], 1, 128), heads_of(proj, COL["ckv"], 1, 128),
                                  rstd[:, :, 6:7].unsqueeze(3).to_broadcast([P, T, 1, 128]), ALU.mult).then_inc(lowrank_ready, 1)
                link(rotate(heads_of(proj, COL["iq"], 8, 32), 8, 32, [heads_of(proj, COL["iq"], 8, 32)]))
                link(rotate(heads_of(proj, COL["ik"], 1, 32), 1, 32,
                            [ik4[:, :, 32 * v:32 * v + 32].unsqueeze(2) for v in range(4)]))
                qa, ka = heads_of(proj, COL["qa"], 4, 64), heads_of(proj, COL["ka"], 1, 64)
                scale_heads(heads_of(proj, 0, 5, 64), 0, 5, 64)
                dve.tensor_tensor(qa, qa, gain("aq", l, 4), ALU.mult)
                link(dve.tensor_tensor(ka, ka, gain("ak", l, 1), ALU.mult))
                link(rotate(qa, 4, 64, [qa]))
                link(dve.tensor_scalar(iws[:, :, :], proj[:, :, COL["iw"]:COL["iw"] + 8],
                                       float(IDX_HEADS ** -0.5 * IDX_DIM ** -0.5), None, ALU.mult))
                rotate(ka, 1, 64, [ka2[:, :, 64 * v:64 * v + 64].unsqueeze(2) for v in range(2)]).then_inc(roped_a, 1)
                dve.wait_ge(roped_a, l + 1)
                kr = heads_of(proj, COL["kr"], 1, 32)
                scale_heads(kr, 7, 1, 32)
                link(dve.tensor_tensor(kr, kr, gain("kr", l, 1), ALU.mult))
                link(rotate(kr, 1, 32, [kcat[:, :, h:h + 1, 64:96] for h in range(B_HEADS)]))
                v = squares(COL["qc"], 640, 0)
                mean_square(stat[:, :, 8:18], v.rearrange("p t (h d) -> p t h d", d=64), 64)
                finish_means(8, 18)
                qc, kc = heads_of(proj, COL["qc"], 8, 64), heads_of(proj, COL["kc"], 2, 64)
                scale_heads(heads_of(proj, COL["qc"], 10, 64), 8, 10, 64)
                dve.tensor_tensor(qc, qc, gain("cq", l, 8), ALU.mult)
                link(dve.tensor_tensor(kc, kc, gain("ck", l, 2), ALU.mult))
                link(rotate(qc, 8, 64, [qc]))
                rotate(kc, 2, 64, [kc2[:, :, :, 64 * v:64 * v + 64] for v in range(2)]).then_inc(roped_c, 1)

                dve.wait_ge(*aux.taken(("ukv", l, 1)))
                v = sq[:, 0:T * 384].rearrange("p (t h d) -> p t h d", t=T, d=96)
                qbh = qb[:, :, :].rearrange("p t (h d) -> p t h d", d=96)
                kvh = kvb[:, :, :].rearrange("p t (h d) -> p t h d", d=128)
                vk = sq[:, 1024:1024 + T * 256].rearrange("p (t h d) -> p t h d", t=T, d=64)
                dve.tensor_tensor(v, qbh, qbh, ALU.mult)
                link(dve.tensor_tensor(vk, kvh[:, :, :, 0:64], kvh[:, :, :, 0:64], ALU.mult))
                mean_square(stat[:, :, 18:22], v[:, :, :, 0:64], 64)
                mean_square(stat[:, :, 22:26], v[:, :, :, 64:96], 32)
                mean_square(stat[:, :, 26:30], vk, 64)
                finish_means(18, 30)
                scale_heads(qbh[:, :, :, 0:64], 18, 4, 64)
                scale_heads(qbh[:, :, :, 64:96], 22, 4, 32)
                scale_heads(kvh[:, :, :, 0:64], 26, 4, 64)
                dve.tensor_tensor(qbh[:, :, :, 0:64], qbh[:, :, :, 0:64], gain("qn", l, 4), ALU.mult)
                link(dve.tensor_tensor(qbh[:, :, :, 64:96], qbh[:, :, :, 64:96], gain("qr", l, 4), ALU.mult))
                tmp = sq[:, 0:T * 128].rearrange("p (t h d) -> p t h d", t=T, d=32)
                qr = qbh[:, :, :, 64:96]

                def over(a):
                    return a.unsqueeze(2).to_broadcast([P, T, 4, a.shape[-1]])
                dve.tensor_tensor(tmp[:, :, :, 0:16], qr[:, :, :, 16:32], over(sin32[:, :, 0:16]), ALU.mult)
                link(dve.tensor_tensor(tmp[:, :, :, 16:32], qr[:, :, :, 0:16], over(sin32[:, :, 16:32]), ALU.mult))
                link(dve.tensor_tensor(qr, qr, over(cos32[:, :, :]), ALU.mult))
                dve.tensor_tensor(qr, qr, tmp, ALU.add)
                dve.tensor_tensor(kcat[:, :, :, 0:64], kvh[:, :, :, 0:64], gain("kn", l, 4), ALU.mult)\
                   .then_inc(mla_heads_ready, 1)

                n = 0
                for t in range(T):
                    nk = P * (t + 1)
                    per = W // nk
                    for i in range(2 * (t + 1)):
                        dve.wait_ge(*aux.taken(("ix", l, t, i)))
                        for j in range(per):
                            h = i * per + j
                            rel = swing[:, (n % 2) * W + j * nk:(n % 2) * W + (j + 1) * nk]
                            wgt = iws[:, t, h:h + 1]
                            if h == 0:
                                ins = dve.tensor_scalar(score[:, 0:nk], rel, wgt, None, ALU.mult)
                            else:
                                ins = dve.scalar_tensor_tensor(out=score[:, 0:nk], in0=rel, scalar=wgt, in1=score[:, 0:nk],
                                                               op0=ALU.mult, op1=ALU.add)
                            if j < per - 1:
                                link(ins)
                        n += 1
                        ins.then_inc(relu_used, 1)
                        dve.wait_ge(relu_used, 6 * l + n)
                    bias = cmask[:, SEQ - nk:]
                    link(dve.tensor_tensor(score[:, 0:nk], score[:, 0:nk], bias, ALU.add))
                    for r in range(TOPK // 8):
                        link(dve.max(top8[:, :], score[:, 0:nk]))
                        link(dve.match_replace(score[:, 0:nk], top8[:, :], score[:, 0:nk], REMOVED))
                    link(dve.tensor_scalar(selmask[:, t, 0:nk], score[:, 0:nk], REMOVED * 0.5, MASKED, ALU.is_gt, ALU.mult))
                    link(dve.tensor_tensor(selmask[:, t, 0:nk], selmask[:, t, 0:nk], bias, ALU.add))

                for s in range(len(JOBS) + 2):
                    if s < len(JOBS):
                        m, t = JOBS[s]
                        nk = P * (t + 1)
                        per = W // nk
                        mask = dict(a=selmask[:, t, 0:nk], b=cmask[:, SEQ - nk:]).get(m, wmask[:, SEQ - nk:])
                        if s >= 2:
                            dve.wait_ge(aux_ready, aux.no(("pt", l, s - 2, JOBS[s - 2][1])))
                        for i in range(t + 1):
                            dve.wait_ge(aux_ready, aux.no(("lg", l, s, i)))
                            b = aux_bank[aux.bank(("lg", l, s, i))]
                            dve.scalar_tensor_tensor(out=logit[:, s % 2, i * per:(i + 1) * per, 0:nk],
                                                     in0=b[:, :].rearrange("p (h k) -> p h k", k=nk), scalar=SCALE[m],
                                                     in1=mask.unsqueeze(1).to_broadcast([P, per, nk]),
                                                     op0=ALU.mult, op1=ALU.add).then_inc(aux_taken["dve"], 1)
                        dve.wait_ge(*aux.taken(("lg", l, s, t)))
                        red = dve.tensor_reduce(nmax[:, s % 2, :], logit[:, s % 2, :, 0:nk], AX_X, ALU.max, negate=True)
                        if m[0] == "c":
                            link(red)
                            o = GAINS["sink"][0] + 4 * int(m[1])
                            sink = gains[:, l, o:o + 4]
                            link(dve.scalar_tensor_tensor(out=nmax[:, s % 2, :], in0=sink, scalar=-1.0, in1=nmax[:, s % 2, :],
                                                          op0=ALU.mult, op1=ALU.min))
                            red = dve.tensor_tensor(sinkx[:, s % 4, 0, :], sink, nmax[:, s % 2, :], ALU.add)
                        red.then_inc(logits_ready, 1)
                    if s >= 2:
                        q = s - 2
                        m, t = JOBS[q]
                        dve.wait_ge(probs_ready, len(JOBS) * l + q + 1)
                        if m[0] == "c":
                            link(dve.tensor_tensor(denom[:, q % 4, :], denom[:, q % 4, :], sinkx[:, q % 4, 1, :], ALU.add))
                        link(dve.reciprocal(rden[:, q % 4, :], denom[:, q % 4, :]))
                        dve.wait_ge(aux_ready, aux.no(("pv", l, q)))
                        b = aux_bank[aux.bank(("pv", l, q))]
                        c0 = Y_COL[m]
                        dve.tensor_tensor(xn[:, t, c0:c0 + 256].rearrange("p (h d) -> p h d", d=64),
                                          b[:, 0:256].rearrange("p (h d) -> p h d", d=64),
                                          rden[:, q % 4, :].unsqueeze(2).to_broadcast([P, 4, 64]), ALU.mult)\
                           .then_inc(aux_taken["dve"], 1)

                split_low(2)
                take_low_four("yt", l)
                dve.wait_ge(*acc.taken(("g", l, 2, 1)))
                for gi, m in enumerate("abc"):
                    if m != "a":
                        split_low(1)
                    for t in range(T):
                        for h in range(2):
                            name = ("m", l, m, t, h)
                            dve.wait_ge(acc_ready, acc.no(name))
                            b = acc_bank[acc.bank(name)]
                            if m == "b" and (t, h) == (0, 0):
                                dve.wait_ge(gates_ready, l + 1)
                            e = gates[:, t, gi * D_MODEL + h * W:gi * D_MODEL + (h + 1) * W]
                            dst = xn[:, t, h * W:(h + 1) * W]
                            o = dst if m == "a" else swing[:, 0:W]
                            dve.tensor_tensor(o, b[:, :], e, ALU.mult).then_inc(acc_taken["dve"], 1)
                            if name[2:] == ("a", 1, 1):
                                split_low(1)
                            if m != "a":
                                dve.wait_ge(*acc.taken(name))
                                ins = dve.tensor_tensor(dst, dst, swing[:, 0:W], ALU.add)
                                if m == "c" and h == 1:
                                    ins.then_inc(merged_ready, 1)
                                    dve.wait_ge(merged_ready, 2 * l + t + 1)
                                else:
                                    link(ins)
                take_low_four("mt", l)
                split_low(3)
                if l == 0:
                    split_low(1)
                for t in range(T):
                    for h in range(2):
                        add_to_x(("o", l, t, h), t, h)
                dve.wait_ge(*acc.taken(("o", l, 1, 1)))
                norm_x()
                if l == 0:
                    take_low_four("f", l, GROW["ffn_norm_g", l])
                    split_low(1)

                    def take_hidden_low(j):
                        c0, n = 4 * j, FF_GROUPS[j][1] // P
                        for t in range(T):
                            at = (slice(None), slice(c0, c0 + n), slice(t * P, (t + 1) * P))
                            take_low(("ht", j, t), ffTl[at], ffTh[at])

                    for j, (_, n) in enumerate(FF_GROUPS):
                        wide = n > 256
                        split_low(1)
                        if j:
                            take_hidden_low(j - 1)
                        if wide:
                            split_low(2)
                        for t in range(T):
                            dve.wait_ge(acc_ready, acc.no(("h3", j, t)))
                            dve.wait_ge(*acc.taken(("h1", j, t)))
                            dve.tensor_tensor(ff_hidden[:, t, 0:n], ff_silu[:, t, 0:n],
                                              acc_bank[acc.bank(("h3", j, t))][:, 0:n], ALU.mult).then_inc(acc_taken["dve"], 1)
                        split_low(1)
                    split_low(1)
                    take_hidden_low(len(FF_GROUPS) - 1)
                    while name_of_next()[0] == "w2":
                        split_low(1)
                    split_low(1)
                    for t in range(T):
                        for h in range(2):
                            add_to_x(("y", t, h), t, h)

            for t in range(T):
                dve.wait_ge(*aux.taken(("router", t)))
                link(dve.max(rtop[:, t, :], rl[:, t, :]))
                link(dve.max_index(ridx[:, t, :], rtop[:, t, :], rl[:, t, :]))
            link(dve.tensor_copy(ridxf[:, :, :], ridx[:, :, :]))
            dve.tensor_tensor(gate2[:, :, 0:1], rtop[:, :, 1:2], rtop[:, :, 0:1], ALU.subtract).then_inc(routed, 1)
            for k in range(2):
                dve.tensor_tensor(onehot[:, :, k, :], iota8[:, :].unsqueeze(1).to_broadcast([P, T, 8]),
                                  ridxf[:, :, k:k + 1].to_broadcast([P, T, 8]), ALU.is_equal)
            dve.wait_ge(routed, 2)
            link(dve.tensor_scalar(gate2[:, :, 0:1], gate2[:, :, 1:2], 1.0, None, ALU.add))
            link(dve.reciprocal(gate2[:, :, 0:1], gate2[:, :, 0:1]))
            link(dve.tensor_tensor(gate2[:, :, 1:2], gate2[:, :, 1:2], gate2[:, :, 0:1], ALU.mult))
            link(dve.tensor_tensor(gated[:, :, 0:8], onehot[:, :, 0, :], gate2[:, :, 0:1].to_broadcast([P, T, 8]), ALU.mult))
            link(dve.tensor_tensor(chosen[:, :, :], onehot[:, :, 1, :], gate2[:, :, 1:2].to_broadcast([P, T, 8]), ALU.mult))
            link(dve.tensor_tensor(gated[:, :, 0:8], gated[:, :, 0:8], chosen[:, :, :], ALU.add))
            dve.tensor_tensor(chosen[:, :, :], onehot[:, :, 0, :], onehot[:, :, 1, :], ALU.add).then_inc(routed, 1)
            link(dve.tensor_copy(gated[:, :, 8:9], gated[:, :, 0:1]))
            dve.memset(pickT[:, :, :], 0.0)
            link(dve.memset(slot_flat[:, :, 2 * N_EXP:], -1.0))
            dve.wait_ge(routed, 3)
            dve.wait_ge(aux_ready, aux.no(("slots",)))
            b = aux_bank[aux.bank(("slots",))]
            link(dve.scalar_tensor_tensor(out=slot_of[:, :, 0, :], in0=b[:, 0:16].rearrange("p (t e) -> p t e", t=T),
                                          scalar=1.0, in1=chosen[:, :, :], op0=ALU.add, op1=ALU.mult))
            link(dve.tensor_scalar(slot_of[:, :, 0, :], slot_of[:, :, 0, :], -1.0, None, ALU.add))
            link(dve.tensor_scalar(slot_of[:, :, 1, :], slot_of[:, :, 0, :], float(-P), None, ALU.add))

            def make_picks(slot, expert):
                for t in range(T):
                    dve.tensor_scalar(pick[:, t, :], iota_slot[:, :], slot_flat[:, t, slot], None, ALU.is_equal)
                for t in range(T):
                    ins = dve.tensor_scalar(pickg[:, t, :], iota_slot[:, :], slot_flat[:, t, slot], gated[:, t, expert],
                                            ALU.is_equal, ALU.mult)
                ins.then_inc(onehot_ready, 1)

            def take_gathered_low(i, high):
                row = GROW["ffn_norm_g", 1]
                dve.wait_ge(high_taken, high)
                for c in range(2):
                    k = 2 * i + c
                    ins = dve.scalar_tensor_tensor(
                        out=xgTl[:, k, :], in0=aux_bank[(AUX0 + i) % 4][:, c * P:(c + 1) * P],
                        scalar=gainT[:, row + k:row + k + 1], in1=xgTh[:, k, :].bitcast(F32),
                        op0=ALU.mult, op1=ALU.subtract)
                ins.then_inc(aux_taken["dve"], 1)

            def add_result(t, h, fill, ready):
                dve.wait_ge(aux_ready, ready)
                xs = x_sb[:, t, h * W:(h + 1) * W]
                dve.tensor_tensor(xs, xs, aux_bank[(AUX0 + fill) % 4][:, :], ALU.add).then_inc(aux_taken["dve"], 1)

            make_picks(slice(0, 1), slice(0, 1))
            dve.tensor_reduce(cnt[:, 0:1], b[:, 16:24], AX_X, ALU.max).then_inc(aux_taken["dve"], 1)
            dve.wait_ge(*aux.taken(("slots",)))
            link(dve.tensor_scalar(cnt[:, 1:2], cnt[:, 0:1], float(P), 1.0, ALU.is_gt, ALU.add))
            link(dve.tensor_scalar(cnt[:, 2:3], cnt[:, 1:2], float(N_EXP), -1.0, ALU.mult, ALU.add))
            dve.tensor_copy(n_pass[:, :], cnt[:, 1:3]).then_inc(passes_ready, 1)
            for i in range(4):
                take_gathered_low(i, aux.high(("x", i)))
            dve.wait_ge(passes_ready, 1)

            passes = dve.value_load(n_pass[0:1, 0:1], min_val=1, max_val=2)
            with dve.Fori(0, passes) as ps:
                with dve.Fori(0, N_EXP) as e:
                    it = ps * N_EXP + e

                    def split_expert_low(u):
                        dve.wait_ge(e_high_split, it * E_UNITS + (u + 1))
                        dve.tensor_tensor(e_part_l[:, u % E_PARTS, :], e_raw[:, u % E_RAW, :],
                                          e_part_h[:, u % E_PARTS, :].bitcast(F32), ALU.subtract).then_inc(low_split["dve"], 1)

                    def take_expert_low(j):
                        dve.wait_ge(high_taken, it * E_HIGHS + (HIGH0 + j + 1))
                        at = lambda b: b[:, 4 * j:4 * j + 4, :].rearrange("p a b -> p (a b)")
                        dve.tensor_tensor(at(hidTl), aux_bank[(AUX0 + HT[j]) % 4][:, :], at(hidTh).bitcast(F32),
                                          ALU.subtract).then_inc(aux_taken["dve"], 1)

                    def add_tile(t):
                        for h in range(2):
                            fill = CB[2 * t + h]
                            add_result(t, h, fill, it * len(E_AUX) + (AUX0 + fill + 1))

                    for u in range(3):
                        split_expert_low(u)
                    for j in range(E_GROUPS):
                        i = 2 * j + 1
                        split_expert_low(4 * j + 3)
                        if j:
                            take_expert_low(j - 1)
                        if j == 1:
                            add_tile(0)
                        split_expert_low(4 * j + 4)
                        split_expert_low(4 * j + 5)
                        dve.wait_ge(acc_ready, it * len(E_ACC) + (ACC0 + i + 1))
                        dve.wait_ge(*e_taken(ACCR, E_ACC, i - 1, it))
                        dve.tensor_tensor(hidden[:, j % 2, 0:W], silu[:, j % 2, 0:W], acc_bank[(ACC0 + i) % 4][:, :],
                                          ALU.mult).then_inc(acc_taken["dve"], 1)
                        if j == 1:
                            add_tile(1)
                        split_expert_low(4 * j + 6)
                        if j == 3:
                            dve.wait_ge(aux_ready, it * len(E_AUX) + (AUX0 + PG + 1))
                            make_picks(bass.ds(it + 1, 1), bass.ds(e + 1, 1))
                    for u in range(4 * E_GROUPS + 3, E_UNITS):
                        split_expert_low(u)
                        if u == 4 * E_GROUPS + 4:
                            take_expert_low(E_GROUPS - 1)
                        if u == 4 * E_GROUPS + X_AFTER + 2:
                            for i in range(4):
                                take_gathered_low(i, it * E_HIGHS + (HIGH0 + E_GROUPS + i + 1))
            for t in range(T):
                for h in range(2):
                    add_result(t, h, 2 * t + h, passes * (N_EXP * len(E_AUX)) + (AUX0 + 2 * t + h + 1))

        @block.tensor
        def _(pe):
            def begin(bank_ring, name):
                free = bank_ring.free(name)
                if free is not None:
                    pe.wait_ge(*free)
                return (acc_bank if bank_ring is acc else aux_bank)[bank_ring.bank(name)]

            def used(ins, name):
                assert name not in ends_fill
                return ins.then_inc(unit_used, 1)

            pe.wait_ge(consts_loaded, CONSTS)
            pe.wait_ge(masks_ready, 1)
            b = begin(aux, ("gains",))
            pe.transpose(b[:, 0:NROWS], gain_rows[0:NROWS, :], ident[0:NROWS, 0:NROWS]).then_inc(aux_ready, 1)

            def transposes(kind, l, src):
                for i in range(4):
                    b = begin(aux, (kind, l, i))
                    for c in range(2):
                        for t in range(T):
                            k = 2 * i + c
                            ins = pe.transpose(b[:, (2 * c + t) * P:(2 * c + t + 1) * P], src[:, t, k * P:(k + 1) * P], ident[:, :])
                    ins.then_inc(aux_ready, 1)

            def four(name, blocks):
                b = begin(aux, name)
                for i, src in enumerate(blocks):
                    m = src.shape[1]
                    ins = pe.transpose(b[0:m, i * P:(i + 1) * P], src, ident[:, :])
                ins.then_inc(aux_ready, 1)

            def three(out, xh, xl, wh, wl, first, last):
                pe.matmul(out, xh, wh, start=first, stop=False)
                pe.matmul(out, xh, wl, start=False, stop=False)
                return pe.matmul(out, xl, wh, start=False, stop=last)

            def stream(fills, names, xh, xl, chunks, cols, taken={}, between=None):
                banks = {}
                k0 = 0
                for u, name in enumerate(names):
                    if between is not None:
                        between(u)
                    wh, wl = parts(name)
                    pe.wait_ge(*arrived(name))
                    for (t, h), fill in fills.items():
                        if u == 0:
                            banks[t, h] = begin(acc, fill)
                        for c in range(shape_of[name][0]):
                            k, m, b = k0 + c, cols(h), banks[t, h]
                            if k in taken and (t, h) == (0, 0):
                                pe.wait_ge(*aux.taken(taken[k]))
                            n = wh[:, c, m].shape[1]
                            ins = three(b[:, 0:n], xh[:, k, t * P:(t + 1) * P], xl[:, k, t * P:(t + 1) * P],
                                        wh[:, c, m], wl[:, c, m], k == 0, k == chunks - 1)
                            if k == chunks - 1:
                                ins.then_inc(acc_ready, 1)
                    k0 += shape_of[name][0]
                    if name not in ends_fill:
                        used(ins, name)

            def pairs(kind, l, first=0, last=KC):
                return {k - first: (kind, l, k // 2) for k in range(first, last, 2)}

            def project(kind, l, g, half, banks={}):
                name = (kind, l, g, half)
                wh, wl = parts(name)
                n = shape_of[name][1]
                pe.wait_ge(*arrived(name))
                for t in range(T):
                    if half == 0:
                        banks[t] = begin(acc, (kind, l, g, t))
                    for c in range(4):
                        k = 4 * half + c
                        if (kind, g, t) == ("p", 0, 0) and k % 2 == 0:
                            pe.wait_ge(*aux.taken(("h", l, k // 2)))
                        ins = three(banks[t][:, 0:n], hTh[:, k, t * P:(t + 1) * P], hTl[:, k, t * P:(t + 1) * P],
                                    wh[:, c, :], wl[:, c, :], k == 0, k == KC - 1)
                    if half == 1:
                        ins.then_inc(acc_ready, 1)
                if half == 0:
                    used(ins, name)

            for l in range(DEPTH):
                pe.wait_ge(normed, 4 * l + 2)
                transposes("h", l, xn)
                for g in range(len(ATT_GROUPS)):
                    for half in range(2):
                        project("p", l, g, half)

                def gate(i):
                    project("g", l, i // 2, i % 2)

                gate(0)
                gate(1)
                pe.wait_ge(lowrank_ready, l + 1)
                cq, ckv = proj[:, :, COL["cq"]:COL["ckv"]], proj[:, :, COL["ckv"]:COL["kr"]]
                four(("cq", l), [cq[:, t, c * P:(c + 1) * P] for c in range(2) for t in range(T)])
                four(("ckv", l), [ckv[:, t, :] for t in range(T)])
                pe.wait_ge(roped_a, l + 1)
                four(("ika", l), [ka2[:, t, :] for t in range(T)] + [ik4[:, t, :] for t in range(T)])
                for nm in ("iq", "qa"):
                    four((nm, l), [proj[:, t, COL[nm] + c * P:COL[nm] + (c + 1) * P] for c in range(2) for t in range(T)])
                gate(2)
                pe.wait_ge(mla_loaded, 32 * (l + 1))
                pe.wait_ge(*aux.taken(("ckv", l)))
                for t in range(T):
                    b = begin(aux, ("uq", l, t))
                    for c in range(2):
                        ins = pe.matmul(b[:, 0:384], cqT[:, c, t * P:(t + 1) * P], uq[:, c, :], start=(c == 0), stop=(c == 1))
                    ins.then_inc(aux_ready, 1)
                for t in range(T):
                    b = begin(aux, ("ukv", l, t))
                    pe.matmul(b[:, :], ckvT[:, t * P:(t + 1) * P], ukv[:, :], start=True, stop=True).then_inc(aux_ready, 1)
                pe.wait_ge(*aux.taken(("iq", l)))
                for t in range(T):
                    nk = P * (t + 1)
                    per = W // nk
                    for i in range(2 * (t + 1)):
                        b = begin(aux, ("ix", l, t, i))
                        h0 = i * per
                        pe.matmul(b[:, :].rearrange("p (h k) -> p h k", k=nk), iqT[:, h0 // 4, t * P:(t + 1) * P],
                                  ikz[:, h0 % 4:h0 % 4 + per, 0:nk], start=True, stop=True).then_inc(aux_ready, 1)
                gate(3)
                pe.wait_ge(roped_c, l + 1)
                four(("kc", l), [kc2[:, t, kv, :] for kv in range(C_KV) for t in range(T)])
                for i in range(2):
                    four((f"qc{i}", l), [proj[:, t, COL["qc"] + c * P:COL["qc"] + (c + 1) * P]
                                         for c in (2 * i, 2 * i + 1) for t in range(T)])
                pe.wait_ge(mla_heads_ready, l + 1)
                for i in range(2):
                    four((f"qb{i}", l), [qb[:, t, 96 * h:96 * h + 96] for h in (2 * i, 2 * i + 1) for t in range(T)])
                for i in range(2):
                    four((f"kb{i}", l), [kcat[:, t, h, :] for h in (2 * i, 2 * i + 1) for t in range(T)])
                gate(4)
                gate(5)
                pe.wait_ge(*aux.taken(("kb1", l)))
                for s in range(len(JOBS) + 2):
                    if s < len(JOBS):
                        m, t = JOBS[s]
                        nk = P * (t + 1)
                        per = W // nk
                        for i in range(t + 1):
                            b = begin(aux, ("lg", l, s, i))
                            for j in range(per // 2 if m != "b" else per):
                                if m == "b":
                                    h = i * per + j
                                    ins = pe.matmul(b[:, j * nk:(j + 1) * nk], qbT[0:96, h, t * P:(t + 1) * P],
                                                    kbT[0:96, h, 0:nk], start=True, stop=True)
                                else:
                                    pair = i * per // 2 + j
                                    q, k = (qaT, kaz) if m == "a" else (qcT, kcz[:, int(m[1])])
                                    blk = pair if m == "a" else 2 * int(m[1]) + pair
                                    ins = pe.matmul(b[:, 2 * j * nk:2 * (j + 1) * nk].rearrange("p (h k) -> p h k", k=nk),
                                                    q[:, blk, t * P:(t + 1) * P], k[:, :, 0:nk], start=True, stop=True)
                            ins.then_inc(aux_ready, 1)
                    if s < 6:
                        gate(6 + s)
                    if 1 <= s <= len(JOBS):
                        q, tq = s - 1, JOBS[s - 1][1]
                        pe.wait_ge(probs_ready, len(JOBS) * l + q + 1)
                        for i in range(tq + 1):
                            four(("pt", l, q, i), [logit[:, q % 2, h, i * P:(i + 1) * P] for h in range(4)])
                    if s >= 2:
                        q = s - 2
                        m, t = JOBS[q]
                        pe.wait_ge(*aux.taken(("pt", l, q, t)))
                        b = begin(aux, ("pv", l, q))
                        for h in range(4):
                            for i in range(t + 1):
                                if m == "a":
                                    v = proj[:, i, COL["va"]:COL["va"] + 64]
                                elif m == "b":
                                    v = kvb[:, i, 128 * h + 64:128 * h + 128]
                                else:
                                    v = proj[:, i, COL["vc"] + 64 * int(m[1]):COL["vc"] + 64 * int(m[1]) + 64]
                                ins = pe.matmul(b[:, 64 * h:64 * h + 64], probT[:, q % 2, 4 * i + h, :], v,
                                                start=(i == 0), stop=(i == t))
                        ins.then_inc(aux_ready, 1)
                pe.wait_ge(*aux.taken(("pv", l, len(JOBS) - 1)))
                transposes("yt", l, xn)
                side = lambda h: slice(h * W, (h + 1) * W)
                for m, name, c0, chunks in (("a", "wa", 0, 2), ("b", "wb", 2, 2), ("c", "wc", 4, 4)):
                    stream({(t, h): ("m", l, m, t, h) for t in range(T) for h in range(2)},
                           [(name, l, u) for u in range(chunks // 2)], hTh[:, c0:c0 + chunks, :], hTl[:, c0:c0 + chunks, :],
                           chunks, side, pairs("yt", l, c0, c0 + chunks))
                pe.wait_ge(merged_ready, 2 * (l + 1))
                transposes("mt", l, xn)
                stream({(t, h): ("o", l, t, h) for t in range(T) for h in range(2)},
                       [("wo", l, u) for u in range(KC // 2)], hTh, hTl, KC, side, pairs("mt", l))
                pe.wait_ge(normed, 4 * l + 4)
                transposes("f", l, xn)
                if l == 0:
                    def hidden_transposes(j):
                        n = FF_GROUPS[j][1]
                        for t in range(T):
                            pe.wait_ge(*acc.taken(("h3", j, t)))
                            four(("ht", j, t), [ff_hidden[:, t, c * P:(c + 1) * P] for c in range(n // P)])

                    for j, (_, n) in enumerate(FF_GROUPS):
                        for kind, wn in (("h1", "w1"), ("h3", "w3")):
                            stream({(t, 0): (kind, j, t) for t in range(T)},
                                   [(wn, j, u) for u in range(2 if n > 256 else 1)], hTh, hTl, KC, lambda h, n=n: slice(0, n),
                                   pairs("f", 0) if (kind, j) == ("h1", 0) else {})
                            if kind == "h1" and j:
                                hidden_transposes(j - 1)

                    def last_hidden(u):
                        if u == 2:
                            hidden_transposes(len(FF_GROUPS) - 1)

                    stream({(t, h): ("y", t, h) for t in range(T) for h in range(2)},
                           [("w2", u) for u in range(FF_CHUNKS // 2)], ffTh, ffTl, FF_CHUNKS, side,
                           {4 * j: ("ht", j, 1) for j in range(len(FF_GROUPS))}, last_hidden)

            for t in range(T):
                b = begin(aux, ("router", t))
                for k in range(KC):
                    if t == 0 and k % 2 == 0:
                        pe.wait_ge(*aux.taken(("f", DEPTH - 1, k // 2)))
                    ins = pe.matmul(b[:, 0:N_EXP], h2T[:, k, t * P:(t + 1) * P], wr[:, k, :], start=(k == 0), stop=(k == KC - 1))
                ins.then_inc(aux_ready, 1)
            pe.wait_ge(routed, 3)
            b = begin(aux, ("slots",))
            pe.matmul(b[:, 0:8], lower[:, :], chosen[:, 0, :], start=True, stop=True)
            pe.matmul(b[:, 8:16], ones[:, :], chosen[:, 0, :], start=True, stop=False)
            pe.matmul(b[:, 8:16], lower[:, :], chosen[:, 1, :], start=False, stop=True)
            pe.matmul(b[:, 16:24], ones[:, :], chosen[:, 0, :], start=True, stop=False)
            pe.matmul(b[:, 16:24], ones[:, :], chosen[:, 1, :], start=False, stop=True).then_inc(aux_ready, 1)
            def gather(i, b):
                for c in range(2):
                    k = 2 * i + c
                    for t in range(T):
                        ins = pe.matmul(b[:, c * P:(c + 1) * P], xn[:, t, k * P:(k + 1) * P], pick[:, t, :],
                                        start=(t == 0), stop=(t == T - 1))
                ins.then_inc(aux_ready, 1)

            pe.wait_ge(onehot_ready, 1)
            for i in range(4):
                gather(i, begin(aux, ("x", i)))
            for h in range(2):
                b = begin(acc, ("y0", h))
                pe.matmul(b[:, :], pickT[:, 0, :], xn[:, 0, h * W:(h + 1) * W], start=True, stop=True).then_inc(acc_ready, 1)
            pe.wait_ge(passes_ready, 1)
            pe.wait_ge(acc_taken["act"], acc.order.count("act") - 2)
            pe.wait_ge(acc_taken["dve"], acc.order.count("dve"))

            def combine(t, h, b):
                pe.matmul(b[:, :], pickT[:, t, :], ysb[:, h * W:(h + 1) * W], start=True, stop=True).then_inc(aux_ready, 1)

            passes = pe.value_load(n_pass[0:1, 0:1], min_val=1, max_val=2)
            with pe.Fori(0, passes) as ps:
                with pe.Fori(0, N_EXP) as e:
                    it = ps * N_EXP + e

                    def aux_fill(i):
                        pe.wait_ge(*e_free(AUXR, E_AUX, i, it))
                        return aux_bank[(AUX0 + i) % 4]

                    def acc_fill(i):
                        pe.wait_ge(*e_free(ACCR, E_ACC, i, it))
                        return acc_bank[(ACC0 + i) % 4]

                    pe.wait_ge(aux_taken["dve"], it * E_AUX.count("dve") + aux.order.count("dve"))

                    def expert_transposes(j):
                        pe.wait_ge(*e_taken(ACCR, E_ACC, 2 * j + 1, it))
                        b = aux_fill(HT[j])
                        for c in range(4):
                            ins = pe.transpose(b[:, c * P:(c + 1) * P], hidden[:, j % 2, c * P:(c + 1) * P], ident[:, :])
                        ins.then_inc(aux_ready, 1)

                    for j in range(E_GROUPS):
                        for side in range(2):
                            b = acc_fill(2 * j + side)
                            for k in range(KC):
                                u = 4 * j + 2 * side + k // 4
                                if k % 4 == 0:
                                    pe.wait_ge(low_split["dve"], it * E_UNITS + (LOW0 + u + 1))
                                wh, wl = e_parts(u, (4, W))
                                ins = three(b[:, :], xgTh[:, k, :], xgTl[:, k, :], wh[:, k % 4, :], wl[:, k % 4, :],
                                            k == 0, k == KC - 1)
                                if k == 3:
                                    ins.then_inc(unit_used, 1)
                            ins.then_inc(acc_ready, 1)
                            if side == 0 and j:
                                expert_transposes(j - 1)
                            if j == 1:
                                if side == 0:
                                    pe.wait_ge(acc_taken["act"], it * E_ACC.count("act") + acc.order.count("act"))
                                for h in range(2):
                                    combine(side, h, aux_fill(CB[2 * side + h]))
                            if j == 2 and side == 0:
                                b = aux_fill(PG)
                                for t in range(T):
                                    ins = pe.transpose(b[:, t * P:(t + 1) * P], pickg[:, t, :], ident[:, :])
                                ins.then_inc(aux_ready, 1)
                    pe.wait_ge(*e_taken(AUXR, E_AUX, HT[-2], it))
                    banks = [acc_fill(2 * E_GROUPS + h) for h in range(2)]
                    for c in range(E_CHUNKS):
                        u = 4 * E_GROUPS + c // 2
                        if c % 2 == 0:
                            pe.wait_ge(low_split["dve"], it * E_UNITS + (LOW0 + u + 1))
                        if c == 4 * (E_GROUPS - 1):
                            pe.wait_ge(*e_taken(AUXR, E_AUX, HT[-1], it))
                        wh, wl = e_parts(u, (2, D_MODEL))
                        for h in range(2):
                            m = slice(h * W, (h + 1) * W)
                            ins = three(banks[h][:, :], hidTh[:, c, :], hidTl[:, c, :], wh[:, c % 2, m], wl[:, c % 2, m],
                                        c == 0, c == E_CHUNKS - 1)
                            if c == E_CHUNKS - 1:
                                ins.then_inc(acc_ready, 1)
                        if c % 2 and c < E_CHUNKS - 1:
                            ins.then_inc(unit_used, 1)
                        if c == 3:
                            expert_transposes(E_GROUPS - 1)
                        if c == 2 * X_AFTER + 1:
                            pe.wait_ge(onehot_ready, it + 2)
                            for i in range(4):
                                gather(i, aux_fill(X0 + i))
            n_it = passes * N_EXP
            pe.wait_ge(acc_taken["act"], n_it * E_ACC.count("act") + acc.order.count("act"))
            for t in range(T):
                for h in range(2):
                    pe.wait_ge(*e_free(AUXR, E_AUX, 2 * t + h, n_it))
                    combine(t, h, aux_bank[(AUX0 + 2 * t + h) % 4])

        @block.sync
        def _(sp):
            n_mla = 0

            def load_mla(l):
                sp.dma_start(uq[:, :, :], w["b_w_uq"][l].rearrange("(c p) n -> p c n", p=P)).then_inc(mla_loaded, 16)
                sp.dma_start(ukv[:, :], w["b_w_ukv"][l]).then_inc(mla_loaded, 16)

            load_mla(0)
            for n, (name, src, shape) in enumerate(units):
                if n >= RAW:
                    sp.wait_ge(*low_done(n - RAW))
                if name == ("p", 1, 0, 0):
                    sp.wait_ge(aux_ready, aux.no(("ukv", 0, 1)))
                    load_mla(1)
                sp.dma_start(in_slot(raw, n % RAW, shape), src).then_inc(raw_loaded[n % RAW], 16)

            w1, w3 = (w[k][0].rearrange("e (c p) n -> e p c n", p=P) for k in ("moe_w1", "moe_w3"))
            w2 = w["moe_w2"][0].rearrange("e (c p) n -> e p c n", p=P)

            def expert_unit(u, e, it):
                sp.wait_ge(low_split["dve"], it * E_UNITS + (LOW0 + u + 1 - E_RAW))
                if u < 4 * E_GROUPS:
                    j, side, half = u // 4, u // 2 % 2, u % 2
                    src = (w1, w3)[side][bass.ds(e, 1), :, 4 * half:4 * half + 4, j * W:(j + 1) * W]
                    dst = in_slot(e_raw, u % E_RAW, (4, W))
                else:
                    c = 2 * (u - 4 * E_GROUPS)
                    src = w2[bass.ds(e, 1), :, c:c + 2, :]
                    dst = in_slot(e_raw, u % E_RAW, (2, D_MODEL))
                sp.dma_start(dst, src.rearrange("e p c n -> p (e c) n")).then_inc(e_raw_loaded[u % E_RAW], 16)

            sp.wait_ge(acc_ready, acc.no(("o", DEPTH - 1, 1, 1)))
            for u in range(E_RAW):
                expert_unit(u, 0, 0)
            sp.wait_ge(passes_ready, 1)
            more = sp.value_load(n_pass[0:1, 1:2], min_val=N_EXP - 1, max_val=2 * N_EXP - 1)
            with sp.Fori(0, more) as it:
                this, following = it & (N_EXP - 1), (it + 1) & (N_EXP - 1)
                for expert in (this, following):
                    sp.compute_val(expert * (D_MODEL * E_FF))
                    sp.compute_val(expert * (D_MODEL * E_FF) * 4)
                for u in range(E_RAW, E_UNITS):
                    expert_unit(u, this, it)
                for u in range(E_RAW):
                    expert_unit(u, following, it + 1)
            for u in range(E_RAW, E_UNITS):
                expert_unit(u, N_EXP - 1, more)
            n_it = more + 1
            done = len([r for r in E_AUX if r == "dve"])
            for t in range(T):
                sp.wait_ge(aux_taken["dve"], n_it * done + (aux.order.count("dve") + 2 * (t + 1)))
                sp.dma_start(out_view[:, t, :], x_sb[:, t, :]).then_inc(stored, 16)
            sp.wait_ge(stored, 16 * T)


_INS = ['x', 'positions', 'attn_norm_g', 'w_in', 'a_q_norm_g', 'a_k_norm_g', 'b_cq_norm_g', 'b_ckv_norm_g',
        'b_w_uq', 'b_w_ukv', 'b_qn_g', 'b_qr_g', 'b_kn_g', 'b_kr_g', 'c_q_norm_g', 'c_k_norm_g', 'c_sinks',
        'w_a_out', 'w_b_out', 'w_c_out', 'w_o', 'ffn_norm_g', 'ffn_w1', 'ffn_w3', 'ffn_w2',
        'router_w', 'moe_w1', 'moe_w3', 'moe_w2']


def kernel(**inputs):
    import numpy as _np
    import concourse.bacc as _bacc
    from concourse import mybir as _mybir
    from concourse.bass_utils import run_bass_kernel_spmd as _run

    nc = _bacc.Bacc("TRN2", target_bir_lowering=False, num_devices=1)
    arrays, args = {}, {}
    for name in _INS:
        a = _np.ascontiguousarray(inputs[name])
        arrays[f"in_{name}_dram"] = a
        args[name] = nc.dram_tensor(f"in_{name}_dram", a.shape, _mybir.dt.from_np(a.dtype), kind="ExternalInput").ap()
    out = nc.dram_tensor("out_0_dram", inputs["x"].shape, _mybir.dt.from_np(_np.dtype("float32")), kind="ExternalOutput").ap()
    hybrid_layers(nc, args, out)
    r = _run(nc, [arrays], core_ids=[0])
    return r.results[0]["out_0_dram"]
```

```python
from contextlib import ExitStack

import numpy as np

import concourse.bass as bass
from concourse import mybir

F32 = mybir.dt.float32
F32R = mybir.dt.float32r
I32 = mybir.dt.int32
U32 = mybir.dt.uint32
ALU = mybir.AluOpType
ACT = mybir.ActivationFunctionType
AX_X = mybir.AxisListType.X

P = 128
D_MODEL, SEQ, DEPTH = 1024, 256, 2
T = SEQ // P
KC = D_MODEL // P
HEAD, IDX_DIM, IDX_HEADS = 64, 32, 8
TOPK = min(256, SEQ // 4)
B_HEADS, C_KV = 4, 2
B_NOPE, B_ROPE, B_QR, B_KVR = 64, 32, 256, 128
D_FF, N_EXP, E_FF = 2816, 8, 3584
EPS = 1e-6

SIZES = dict(qa=256, ka=64, va=64, iq=256, ik=32, iw=8, cq=256, ckv=128, kr=32, qc=512, kc=128, vc=128)
COL, ATT = {}, 0
for _name, _size in SIZES.items():
    COL[_name] = ATT
    ATT += _size
W = 512
ATT_GROUPS = [(g * W, min(W, ATT - g * W)) for g in range(-(-ATT // W))]
GATE_GROUPS = 3 * D_MODEL // W
GATE_ORDER = [4, 5, 2, 3, 0, 1]
LAST_GATE = GATE_ORDER[-1]

MASKED, REMOVED = -1e30, -3e38

UNIT = 2048
RAW, PARTS = 3, 2
E_RAW, E_PARTS = 7, 3
E_GROUPS = E_FF // W
E_CHUNKS = E_FF // P
E_UNITS = 4 * E_GROUPS + E_CHUNKS // 2
FF_GROUPS = [(j * W, min(W, D_FF - j * W)) for j in range(-(-D_FF // W))]
FF_CHUNKS = D_FF // P

MIXERS = ["c0", "c1", "b", "a"]
JOBS = [(m, t) for m in MIXERS for t in range(T)]
Y_COL = dict(a=0, b=256, c0=512, c1=768)
SCALE = dict(a=HEAD ** -0.5, b=(B_NOPE + B_ROPE) ** -0.5, c0=HEAD ** -0.5, c1=HEAD ** -0.5)


class BankRing:

    def __init__(self, taken_by):
        self.taken_by, self.order, self.index, self.highs = taken_by, [], {}, {}

    def add(self, name, reader):
        self.index[name] = len(self.order)
        if reader == "both":
            self.highs[name] = len(self.highs) + 1
            reader = "dve"
        self.order.append(reader)

    def no(self, name):
        return self.index[name] + 1

    def bank(self, name):
        return self.index[name] % 4

    def high(self, name):
        return self.highs[name]

    def count(self, i):
        reader = self.order[i]
        return self.taken_by[reader], self.order[:i + 1].count(reader)

    def taken(self, name):
        return self.count(self.index[name])

    def free(self, name):
        i = self.index[name]
        return self.count(i - 4) if i >= 4 else None


def plan_units(w):
    units = []

    def columns(name, src, c0, n, chunks):
        v = src.rearrange("(c p) n -> p c n", p=P)
        per = UNIT // n if n >= 256 else chunks
        per = min(per, chunks)
        if n > 256:
            per = 4
        for h in range(chunks // per):
            units.append((name + (h,), v[:, h * per:(h + 1) * per, c0:c0 + n], (per, n)))

    def rows(name, src, chunks):
        v = src.rearrange("(c p) n -> p c n", p=P)
        for h in range(chunks // 2):
            units.append((name + (h,), v[:, 2 * h:2 * h + 2, :], (2, D_MODEL)))

    for l in range(DEPTH):
        for g, (c0, n) in enumerate(ATT_GROUPS):
            columns(("p", l, g), w["w_in"][l], c0, n, KC)
        for g in GATE_ORDER:
            columns(("g", l, g), w["w_in"][l], ATT + g * W, W, KC)
        rows(("wc", l), w["w_c_out"][l], 4)
        rows(("wb", l), w["w_b_out"][l], 2)
        rows(("wa", l), w["w_a_out"][l], 2)
        rows(("wo", l), w["w_o"][l], KC)
        if l == 0:
            for j, (c0, n) in enumerate(FF_GROUPS):
                columns(("w1", j), w["ffn_w1"][0], c0, n, KC)
                columns(("w3", j), w["ffn_w3"][0], c0, n, KC)
            rows(("w2",), w["ffn_w2"][0], FF_CHUNKS)
    return units


def hybrid_layers(nc, w, out):
    with ExitStack() as ctx:
        def sb(name, shape, dt=F32):
            return ctx.enter_context(nc.sbuf_tensor(name, shape, dt))

        def sem(name):
            return ctx.enter_context(nc.semaphore(name))

        x_loaded = [sem(f"x_loaded{t}") for t in range(T)]
        rows_loaded = sem("gain_rows_loaded")
        consts_loaded = sem("consts_loaded")
        ident_ready = sem("ident_ready")
        tables_ready = sem("tables_ready")
        mla_loaded = sem("mla_loaded")
        raw_loaded = [sem(f"raw_loaded{i}") for i in range(RAW)]
        e_raw_loaded = [sem(f"expert_raw_loaded{i}") for i in range(E_RAW)]
        high_split, e_high_split = sem("high_split_by_pool"), sem("expert_high_split_by_act")
        low_split = dict(pool=sem("low_split_by_pool"), dve=sem("low_split_by_dve"))
        unit_used = sem("unit_used")
        acc_ready, aux_ready = sem("acc_ready"), sem("aux_ready")
        acc_taken = dict(act=sem("acc_taken_by_act"), dve=sem("acc_taken_by_dve"))
        aux_taken = dict(act=sem("aux_taken_by_act"), dve=sem("aux_taken_by_dve"))
        high_taken = sem("high_taken_by_act")
        gates_ready = sem("gates_ready")
        pool_step = sem("pool_step")
        masks_ready = sem("masks_ready")
        dve_step = sem("dve_step")
        angles_ready = sem("angles_ready")
        trig_ready = sem("trig_ready")
        normed = sem("normed")
        lowrank_ready = sem("lowrank_ready")
        roped_a = sem("roped_a")
        roped_c = sem("roped_c")
        mla_heads_ready = sem("mla_heads_ready")
        relu_used = sem("relu_used")
        logits_ready = sem("logits_ready")
        probs_ready = sem("probs_ready")
        merged_ready = sem("merged_ready")
        hidden_ready = sem("hidden_ready")
        routed = sem("routed")
        chosen_ready = sem("chosen_ready")
        passes_ready = sem("passes_ready")
        onehot_ready = sem("onehot_ready")
        stored = sem("stored")

        acc_bank = [ctx.enter_context(nc.psum_tensor(f"acc{i}", [P, W], F32)) for i in range(4)]
        aux_bank = [ctx.enter_context(nc.psum_tensor(f"aux{i}", [P, W], F32)) for i in range(4)]

        x_sb = sb("x_sb", [P, T, D_MODEL])
        xn = sb("xn", [P, T, D_MODEL])
        ident = sb("ident", [P, P])
        gainT = sb("gainT", [P, 64])
        lower, ones = sb("lower", [P, P]), sb("ones", [P, P])
        iota8, iota_slot = sb("iota8", [P, 8]), sb("iota_slot", [P, P])
        wr = sb("wr", [P, KC, N_EXP])
        xstat, xrstd = sb("xstat", [P, T]), sb("xrstd", [P, T])
        NST = 18 + 12
        newton = sb("newton", [P, 2, T, NST])

        phases = ExitStack()

        def lay(name, shape, dt=F32):
            return phases.enter_context(nc.sbuf_tensor(name, shape, dt))

        raw = lay("raw", [P, RAW, UNIT])
        part_h, part_l = lay("part_h", [P, PARTS, UNIT], F32R), lay("part_l", [P, PARTS, UNIT], F32R)
        hTh, hTl = lay("hTh", [P, KC, SEQ], F32R), lay("hTl", [P, KC, SEQ], F32R)
        kcz, kaz = lay("kcz", [P, C_KV, 2, SEQ]), lay("kaz", [P, 2, SEQ])
        ikz = lay("ikz", [P, 4, SEQ])
        uq, ukv = lay("uq", [P, 2, 384]), lay("ukv", [P, 512])
        cmask, wmask = lay("cmask", [P, SEQ]), lay("wmask", [P, SEQ])
        GAINS = dict(aq=(0, 64), ak=(64, 64), qn=(128, 64), qr=(192, 32), kn=(224, 64), kr=(288, 32),
                     cq=(320, 64), ck=(384, 64), sink=(448, 8))
        gains = lay("gains", [P, DEPTH, 456])
        cos64, sin64 = lay("cos64", [P, T, 64]), lay("sin64", [P, T, 64])
        cos32, sin32 = lay("cos32", [P, T, 32]), lay("sin32", [P, T, 32])
        invn = lay("invn", [P, NST])

        scratch = ExitStack()

        def mix(name, shape, dt=F32):
            return scratch.enter_context(nc.sbuf_tensor(name, shape, dt))

        proj = mix("proj", [P, T, ATT])
        gates = mix("gates", [P, T, 3 * D_MODEL])
        swing = mix("swing", [P, 1280])
        logit = mix("logit", [P, 2, 4, SEQ])
        probT = mix("probT", [P, 2, 8, P])
        sq = probT[:, :, :, :].rearrange("p a b c -> p (a b c)")
        qcT = mix("qcT", [P, 4, SEQ])
        cqT = qcT[:, 0:2, :]
        iqT = proj[:, :, COL["iq"]:COL["iq"] + SEQ]
        qaT = mix("qaT", [P, 2, SEQ])
        qbT, kbT = mix("qbT", [P, B_HEADS, SEQ]), mix("kbT", [P, B_HEADS, SEQ])
        ckvT = mix("ckvT", [P, SEQ])
        kc2, ka2, ik4 = mix("kc2", [P, T, C_KV, P]), mix("ka2", [P, T, P]), mix("ik4", [P, T, P])
        qb, kvb = mix("qb", [P, T, 384]), mix("kvb", [P, T, 512])
        kcat = mix("kcat", [P, T, B_HEADS, 96])
        selmask = mix("selmask", [P, T, SEQ])
        ang = mix("ang", [P, 4, T, 32])
        merged = proj[:, :, COL["iq"]:COL["iq"] + D_MODEL]
        score = proj[:, :, COL["cq"]:COL["cq"] + SEQ]
        start_of = gates[:, :, :].rearrange("p t n -> p (t n)")
        gain_rows = start_of[0:64, 0:P]
        trig = start_of[:, P:P + 2 * T * 32].rearrange("p (a t d) -> p a t d", a=2, t=T)
        freq, pos_f = start_of[:, 256:288], start_of[:, 288:290]
        pos_i = mix("pos_i", [P, T], I32)
        stat, rstd = mix("stat", [P, T, NST]), mix("rstd", [P, T, NST])
        iws = mix("iws", [P, T, IDX_HEADS])
        top8 = mix("top8", [P, 8])
        nmax, denom = mix("nmax", [P, 2, 4]), mix("denom", [P, 4, 4])
        sinkx, rden = mix("sinkx", [P, 4, 2, 4]), mix("rden", [P, 4, 4])
        scratch.close()

        ffn = ExitStack()
        ffTh = ffn.enter_context(nc.sbuf_tensor("ffTh", [P, FF_CHUNKS, SEQ], F32R))
        ffTl = ffn.enter_context(nc.sbuf_tensor("ffTl", [P, FF_CHUNKS, SEQ], F32R))
        ff_silu = ffn.enter_context(nc.sbuf_tensor("ff_silu", [P, T, W], F32))
        ff_hidden = ffn.enter_context(nc.sbuf_tensor("ff_hidden", [P, T, W], F32))
        ffn.close()
        phases.close()

        e_raw = sb("e_raw", [P, E_RAW, UNIT])
        e_part_h, e_part_l = sb("e_part_h", [P, E_PARTS, UNIT], F32R), sb("e_part_l", [P, E_PARTS, UNIT], F32R)
        h2T = sb("h2T", [P, KC, SEQ])
        rl, rtop, ridx = sb("rl", [P, T, 8]), sb("rtop", [P, T, 8]), sb("ridx", [P, T, 8], U32)
        ridxf = sb("ridxf", [P, T, 8])
        gate2, onehot = sb("gate2", [P, T, 2]), sb("onehot", [P, T, 2, 8])
        chosen, gated = sb("chosen", [P, T, 8]), sb("gated", [P, T, 9])
        slot_flat = sb("slot_flat", [P, T, 2 * N_EXP + 1])
        slot_of = slot_flat[:, :, 0:2 * N_EXP].rearrange("p t (s e) -> p t s e", s=2)
        n_pass = sb("n_pass", [P, 2], I32)
        cnt = sb("cnt", [P, 4])
        pick, pickg, pickT = (sb(n, [P, T, P]) for n in ("pick", "pickg", "pickT"))
        xgTh, xgTl = sb("xgTh", [P, KC, P], F32R), sb("xgTl", [P, KC, P], F32R)
        hidTh, hidTl = sb("hidTh", [P, E_CHUNKS, P], F32R), sb("hidTl", [P, E_CHUNKS, P], F32R)
        silu, hidden = sb("silu", [P, 2, W]), sb("hidden", [P, 2, W])
        ysb = sb("ysb", [P, D_MODEL])

        acc, aux = BankRing(acc_taken), BankRing(aux_taken)
        for l in range(DEPTH):
            for g in range(len(ATT_GROUPS)):
                for t in range(T):
                    acc.add(("p", l, g, t), "act")
            for g in GATE_ORDER:
                for t in range(T):
                    acc.add(("g", l, g, t), "act")
            for m in "cba":
                for t in range(T):
                    for h in range(2):
                        acc.add(("m", l, m, t, h), "dve")
            for t in range(T):
                for h in range(2):
                    acc.add(("o", l, t, h), "dve")
            if l == 0:
                for j in range(len(FF_GROUPS)):
                    for t in range(T):
                        acc.add(("h1", j, t), "act")
                    for t in range(T):
                        acc.add(("h3", j, t), "dve")
                for t in range(T):
                    for h in range(2):
                        acc.add(("y", t, h), "dve")
        aux.add(("gains",), "act")
        for l in range(DEPTH):
            for i in range(4):
                aux.add(("h", l, i), "both")
            for n in ("cq", "ckv", "ika", "iq", "qa"):
                aux.add((n, l), "act")
            for n in ("uq", "ukv"):
                for t in range(T):
                    aux.add((n, l, t), "act")
            for n in ("kc", "qc0", "qc1", "qb0", "qb1", "kb0", "kb1"):
                aux.add((n, l), "act")
            for t in range(T):
                for i in range(2 * (t + 1)):
                    aux.add(("ix", l, t, i), "act")
            for s in range(len(JOBS) + 2):
                if s < len(JOBS):
                    for i in range(JOBS[s][1] + 1):
                        aux.add(("lg", l, s, i), "dve")
                if s == 6:
                    aux.add(("yt", l, 2), "both")
                    aux.add(("yt", l, 3), "both")
                if s == 9:
                    aux.add(("yt", l, 1), "both")
                if 1 <= s <= len(JOBS):
                    for i in range(JOBS[s - 1][1] + 1):
                        aux.add(("pt", l, s - 1, i), "act")
                if s >= 2:
                    aux.add(("pv", l, s - 2), "dve")
            aux.add(("yt", l, 0), "both")
            for i in range(4):
                aux.add(("mt", l, i), "both")
            for i in range(4):
                aux.add(("f", l, i), "both" if l == 0 else ("act", "dve")[i % 2])
            if l == 0:
                for j in range(len(FF_GROUPS)):
                    for t in range(T):
                        aux.add(("ht", j, t), "both")
        aux.add(("router", 0), "act")
        aux.add(("router", 1), "act")
        aux.add(("slots",), "dve")
        for i in range(4):
            aux.add(("x", i), "dve")
        for h in range(2):
            acc.add(("y0", h), "act")
        ACC0, AUX0 = len(acc.order), len(aux.order)
        E_ACC = ["act", "dve"] * E_GROUPS + ["act", "act"]
        HT = [0, 5] + list(range(7, 7 + E_GROUPS - 2))
        CB, PG = [1, 2, 3, 4], 6
        X0 = 7 + E_GROUPS - 2
        E_AUX = ["act" if i == PG else "dve" for i in range(X0 + 4)]
        HIGH0, E_HIGHS = len(aux.highs), 4 + E_GROUPS
        assert len(E_ACC) % 4 == 0 and len(E_AUX) % 4 == 0

        units = plan_units(w)
        UNITS0 = len(units)
        unit_no = {name: n for n, (name, _, _) in enumerate(units)}
        shape_of = {name: s for name, _, s in units}

        def in_slot(ring, n, shape):
            return ring[:, n, 0:shape[0] * shape[1]].rearrange("p (c n) -> p c n", n=shape[1])

        def parts(name):
            n, shape = unit_no[name], shape_of[name]
            return in_slot(part_h, n % PARTS, shape), in_slot(part_l, n % PARTS, shape)

        def e_parts(u, shape):
            return in_slot(e_part_h, u % E_PARTS, shape), in_slot(e_part_l, u % E_PARTS, shape)

        by_pool = lambda name: name[0] == "wo" and name[2] == 0 or name[0] == "g" and name[2:] != (GATE_ORDER[0], 0)
        low_by = ["pool" if by_pool(name) else "dve" for name, _, _ in units]
        LOW0 = low_by.count("dve")

        def low_done(n):
            return low_split[low_by[n]], low_by[:n + 1].count(low_by[n])

        def arrived(name):
            return low_done(unit_no[name])

        ends_fill = {}
        for l in range(DEPTH):
            for g in range(len(ATT_GROUPS)):
                ends_fill["p", l, g, 1] = ("p", l, g, 1)
            for g in range(GATE_GROUPS):
                ends_fill["g", l, g, 1] = ("g", l, g, 1)
            ends_fill["wa", l, 0] = ("m", l, "a", 1, 1)
            ends_fill["wb", l, 0] = ("m", l, "b", 1, 1)
            ends_fill["wc", l, 1] = ("m", l, "c", 1, 1)
            ends_fill["wo", l, 3] = ("o", l, 1, 1)
        for j, (_, n) in enumerate(FF_GROUPS):
            last = 1 if n > 256 else 0
            ends_fill["w1", j, last] = ("h1", j, 1)
            ends_fill["w3", j, last] = ("h3", j, 1)
        ends_fill["w2", FF_CHUNKS // 2 - 1] = ("y", 1, 1)
        own = [n for n, (name, _, _) in enumerate(units) if name not in ends_fill]
        assert all(name in unit_no for name in ends_fill)
        OWN0 = len(own)

        def released(n):
            name = units[n][0]
            if name in ends_fill:
                return acc_ready, acc.no(ends_fill[name])
            return unit_used, own.index(n) + 1

        E_OWN = [u for u in range(E_UNITS) if not ((u < 4 * E_GROUPS and u % 2) or u == E_UNITS - 1)]

        def e_released(u, it):
            if u in E_OWN:
                return unit_used, it * len(E_OWN) + (OWN0 + E_OWN.index(u) + 1)
            fill = u // 2 + 1 if u < 4 * E_GROUPS else len(E_ACC)
            return acc_ready, it * len(E_ACC) + (ACC0 + fill)

        def e_free_part(u, it):
            if u >= E_PARTS:
                return e_released(u - E_PARTS, it)
            s, v = e_released(E_UNITS + u - E_PARTS, it)
            return s, v - (len(E_OWN) if s is unit_used else len(E_ACC))

        def e_free(ring0, order, i, it):
            base = {r: ring0[1].order.count(r) for r in ("act", "dve")}
            if i >= 4:
                r = order[i - 4]
                return ring0[1].taken_by[r], it * order.count(r) + (base[r] + order[:i - 3].count(r))
            r = order[i - 4]
            return ring0[1].taken_by[r], it * order.count(r) + (base[r] - order[len(order) + i - 3:].count(r))

        def e_taken(ring0, order, i, it):
            r = order[i]
            base = ring0[1].order.count(r)
            return ring0[1].taken_by[r], it * order.count(r) + (base + order[:i + 1].count(r))

        ACCR, AUXR = (ACC0, acc), (AUX0, aux)
        X_AFTER = 4

        small, rows_in = [], []
        r = 0
        GROW = {}
        for name, n in (("attn_norm_g", D_MODEL), ("ffn_norm_g", D_MODEL), ("b_cq_norm_g", B_QR), ("b_ckv_norm_g", B_KVR)):
            k = DEPTH * n // P
            rows_in.append((gain_rows[r:r + k, :], w[name].rearrange("l (c p) -> (l c) p", p=P)))
            for l in range(DEPTH):
                GROW[name, l] = r + l * n // P
            r += k
        NROWS = r
        for key, name in (("aq", "a_q_norm_g"), ("ak", "a_k_norm_g"), ("qn", "b_qn_g"), ("qr", "b_qr_g"), ("kn", "b_kn_g"),
                          ("kr", "b_kr_g"), ("cq", "c_q_norm_g"), ("ck", "c_k_norm_g"), ("sink", "c_sinks")):
            o, n = GAINS[key]
            small.append((gains[:, :, o:o + n], w[name].partition_broadcast(P)))
        small.append((pos_i[:, :], w["positions"].rearrange("b (t p) -> p (b t)", p=P)))
        small.append((wr[:, :, :], w["router_w"][0].rearrange("(c p) e -> p c e", p=P)))
        x_view = w["x"].rearrange("b (t p) d -> p (b t) d", p=P)
        out_view = out.rearrange("b (t p) d -> p (b t) d", p=P)
        ROWS, CONSTS = 16 * len(rows_in), 16 * len(small)

        def gain(key, l, heads):
            o, n = GAINS[key]
            return gains[:, l:l + 1, o:o + n].unsqueeze(1).to_broadcast([P, T, heads, n])

        def heads_of(buf, c0, heads, d):
            return buf[:, :, c0:c0 + heads * d].rearrange("p t (h d) -> p t h d", d=d)

        block = ctx.enter_context(nc.Block())

        @block.scalar
        def _(act):
            for dst, src in small:
                act.dma_start(dst, src, allow_slow_non_contiguous=(dst.dtype == I32)).then_inc(consts_loaded, 16)

            def take_aux(name, dst, src=None, func=ACT.Copy, **kw):
                act.wait_ge(aux_ready, aux.no(name))
                b = aux_bank[aux.bank(name)]
                return act.activation(dst, b[:, :] if src is None else src(b), func, **kw).then_inc(aux_taken["act"], 1)

            take_aux(("gains",), gainT[:, 0:NROWS], lambda b: b[:, 0:NROWS])
            def take_high(name, cols):
                act.wait_ge(aux_ready, aux.no(name))
                b = aux_bank[aux.bank(name)]
                n = cols.shape[1] * cols.shape[2]
                act.activation(cols, b[:, 0:n].rearrange("p (c n) -> p c n", n=cols.shape[2]), ACT.Copy)\
                   .then_inc(high_taken, 1)

            def take_transposed(kind, l, row, dst):
                for i in range(4):
                    if (kind, l) == ("f", DEPTH - 1) and i % 2:
                        continue
                    act.wait_ge(aux_ready, aux.no((kind, l, i)))
                    b = aux_bank[aux.bank((kind, l, i))]
                    for c in range(2):
                        ins = act.activation(dst[:, 2 * i + c, :], b[:, c * SEQ:(c + 1) * SEQ], ACT.Copy,
                                             scale=gainT[:, row + 2 * i + c:row + 2 * i + c + 1])
                    ins.then_inc(high_taken if (kind, l, i) in aux.highs else aux_taken["act"], 1)

            for l in range(DEPTH):
                act.wait_ge(*aux.taken(("gains",)))
                take_transposed("h", l, GROW["attn_norm_g", l], hTh)
                for g, (c0, n) in enumerate(ATT_GROUPS):
                    for t in range(T):
                        act.wait_ge(acc_ready, acc.no(("p", l, g, t)))
                        act.activation(proj[:, t, c0:c0 + n], acc_bank[acc.bank(("p", l, g, t))][:, 0:n], ACT.Copy)\
                           .then_inc(acc_taken["act"], 1)
                    if (l, g) == (0, 0):
                        act.wait_ge(angles_ready, 2)
                        act.activation(trig[:, :, :, :], ang[:, 2:4, :, :], ACT.Sin).then_inc(trig_ready, 1)

                def take_gates(g, func):
                    for t in range(T):
                        act.wait_ge(acc_ready, acc.no(("g", l, g, t)))
                        act.activation(gates[:, t, g * W:(g + 1) * W], acc_bank[acc.bank(("g", l, g, t))][:, :],
                                       func).then_inc(acc_taken["act"], 1)

                if l == 0:
                    act.wait_ge(tables_ready, 1)
                take_gates(GATE_ORDER[0], ACT.Sigmoid)
                act.wait_ge(aux_ready, aux.no(("cq", l)))
                b, r = aux_bank[aux.bank(("cq", l))], GROW["b_cq_norm_g", l]
                for c in range(2):
                    ins = act.activation(cqT[:, c, :], b[:, c * SEQ:(c + 1) * SEQ], ACT.Copy, scale=gainT[:, r + c:r + c + 1])
                ins.then_inc(aux_taken["act"], 1)
                r = GROW["b_ckv_norm_g", l]
                take_aux(("ckv", l), ckvT[:, :], lambda b: b[:, 0:SEQ], scale=gainT[:, r:r + 1])
                act.wait_ge(aux_ready, aux.no(("ika", l)))
                b = aux_bank[aux.bank(("ika", l))]
                for v in range(2):
                    act.activation(kaz[64 * v:64 * v + 64, v, :], b[64 * v:64 * v + 64, 0:SEQ], ACT.Copy)
                for v in range(4):
                    ins = act.activation(ikz[32 * v:32 * v + 32, v, :], b[32 * v:32 * v + 32, SEQ:2 * SEQ], ACT.Copy)
                ins.then_inc(aux_taken["act"], 1)
                take_aux(("iq", l), iqT, lambda b: b[:, :].rearrange("p (a b) -> p a b", a=2))
                take_aux(("qa", l), qaT[:, :, :].rearrange("p a b -> p (a b)"))
                for t in range(T):
                    take_aux(("uq", l, t), qb[:, t, :], lambda b: b[:, 0:384])
                for t in range(T):
                    take_aux(("ukv", l, t), kvb[:, t, :])
                take_gates(GATE_ORDER[1], ACT.Sigmoid)
                act.wait_ge(aux_ready, aux.no(("kc", l)))
                b = aux_bank[aux.bank(("kc", l))]
                for kv in range(C_KV):
                    for v in range(2):
                        ins = act.activation(kcz[64 * v:64 * v + 64, kv, v, :],
                                             b[64 * v:64 * v + 64, kv * SEQ:(kv + 1) * SEQ], ACT.Copy)
                ins.then_inc(aux_taken["act"], 1)
                for i in range(2):
                    take_aux((f"qc{i}", l), qcT[:, 2 * i:2 * i + 2, :].rearrange("p a b -> p (a b)"))
                for nm, dst in (("qb", qbT), ("kb", kbT)):
                    for i in range(2):
                        take_aux((f"{nm}{i}", l), dst[0:96, 2 * i:2 * i + 2, :].rearrange("p a b -> p (a b)"),
                                 lambda b: b[0:96, :])
                n = 0
                act.wait_ge(roped_c, l + 1)
                for t in range(T):
                    for i in range(2 * (t + 1)):
                        k = 6 * l + n
                        if n >= 2:
                            act.wait_ge(relu_used, k - 1)
                        act.wait_ge(aux_ready, aux.no(("ix", l, t, i)))
                        act.activation(swing[:, (n % 2) * W:(n % 2 + 1) * W], aux_bank[aux.bank(("ix", l, t, i))][:, :],
                                       ACT.Relu).then_inc(aux_taken["act"], 1)
                        n += 1
                take_gates(GATE_ORDER[2], ACT.Sigmoid)

                def take_head_outputs(i):
                    take_high(("yt", l, i), hTh[:, 2 * i:2 * i + 2, :])

                for s in range(len(JOBS) + 2):
                    if s == 6:
                        act.wait_ge(acc_ready, acc.no(("g", l, LAST_GATE, T - 1)))
                        take_head_outputs(2)
                        take_head_outputs(3)
                    if s < len(JOBS):
                        m, t = JOBS[s]
                        nk, job = P * (t + 1), len(JOBS) * l + s
                        act.wait_ge(logits_ready, job + 1)
                        if m[0] == "c":
                            act.activation(sinkx[:, s % 4, 1, :], sinkx[:, s % 4, 0, :], ACT.Exp)
                        for h in range(4):
                            row = logit[:, s % 2, h, 0:nk]
                            ins = act.activation(row, row, ACT.Exp, bias=nmax[:, s % 2, h:h + 1],
                                                 accum_out=denom[:, s % 4, h:h + 1])
                        ins.then_inc(probs_ready, 1)
                    if s in (1, 3, 5):
                        take_gates(GATE_ORDER[3 + s // 2], ACT.Copy)
                    if s == len(JOBS) - 1:
                        act.wait_ge(*acc.taken(("g", l, LAST_GATE, T - 1)))
                        for c0, n in ((0, 2 * W), (3 * W, W)):
                            late = gates[:, :, c0:c0 + n]
                            ins = act.activation(late, late, ACT.Sigmoid)
                        ins.then_inc(gates_ready, 1)
                    if 1 <= s <= len(JOBS):
                        q, tq = s - 1, JOBS[s - 1][1]
                        if q >= 2:
                            act.wait_ge(aux_ready, aux.no(("pv", l, q - 2)))
                        for i in range(tq + 1):
                            take_aux(("pt", l, q, i), probT[:, q % 2, 4 * i:4 * i + 4, :].rearrange("p a b -> p (a b)"))
                    if s == 9:
                        take_head_outputs(1)
                take_head_outputs(0)
                act.wait_ge(acc_ready, acc.no(("m", l, "a", 1, 1)))
                for i in range(4):
                    take_high(("mt", l, i), hTh[:, 2 * i:2 * i + 2, :])
                act.wait_ge(acc_ready, acc.no(("o", l, 1, 1)))
                take_transposed("f", l, GROW["ffn_norm_g", l], hTh if l == 0 else h2T)
                if l == 0:
                    def take_hidden(j):
                        n = FF_GROUPS[j][1]
                        for t in range(T):
                            take_high(("ht", j, t), ffTh[:, 4 * j:4 * j + n // P, t * P:(t + 1) * P])

                    for j, (_, n) in enumerate(FF_GROUPS):
                        for t in range(T):
                            act.wait_ge(acc_ready, acc.no(("h1", j, t)))
                            if j:
                                act.wait_ge(*acc.taken(("h3", j - 1, t)))
                            act.activation(ff_silu[:, t, 0:n], acc_bank[acc.bank(("h1", j, t))][:, 0:n], ACT.Silu)\
                               .then_inc(acc_taken["act"], 1)
                        if j:
                            take_hidden(j - 1)
                    take_hidden(len(FF_GROUPS) - 1)

            for t in range(T):
                take_aux(("router", t), rl[:, t, :], lambda b: b[:, 0:N_EXP])
            act.wait_ge(routed, 1)
            act.activation(gate2[:, :, 1:2], gate2[:, :, 0:1], ACT.Exp).then_inc(routed, 1)

            def take_gathered(i, ready):
                row = GROW["ffn_norm_g", 1]
                act.wait_ge(aux_ready, ready)
                for c in range(2):
                    k = 2 * i + c
                    ins = act.activation(xgTh[:, k, :], aux_bank[(AUX0 + i) % 4][:, c * P:(c + 1) * P], ACT.Copy,
                                         scale=gainT[:, row + k:row + k + 1])
                ins.then_inc(high_taken, 1)

            def take_result(it):
                for h in range(2):
                    act.wait_ge(acc_ready, it * len(E_ACC) + (ACC0 - 1 + h))
                    act.activation(ysb[:, h * W:(h + 1) * W], acc_bank[(ACC0 - 2 + h) % 4][:, :], ACT.Copy)\
                       .then_inc(acc_taken["act"], 1)

            act.wait_ge(passes_ready, 1)
            passes = act.value_load(n_pass[0:1, 0:1], min_val=1, max_val=2)
            with act.Fori(0, passes) as ps:
                with act.Fori(0, N_EXP) as e:
                    it = ps * N_EXP + e

                    def split_high(u):
                        act.wait_ge(e_raw_loaded[u % E_RAW], it * (16 * (E_UNITS // E_RAW)) + 16 * (u // E_RAW + 1))
                        act.wait_ge(*e_free_part(u, it))
                        act.activation(e_part_h[:, u % E_PARTS, :], e_raw[:, u % E_RAW, :], ACT.Copy).then_inc(e_high_split, 1)

                    def take_expert_hidden(j):
                        act.wait_ge(aux_ready, it * len(E_AUX) + (AUX0 + HT[j] + 1))
                        act.activation(hidTh[:, 4 * j:4 * j + 4, :].rearrange("p a b -> p (a b)"),
                                       aux_bank[(AUX0 + HT[j]) % 4][:, :], ACT.Copy).then_inc(high_taken, 1)

                    for u in range(3):
                        split_high(u)
                    for j in range(E_GROUPS):
                        split_high(4 * j + 3)
                        if j == 0:
                            take_result(it)
                        act.wait_ge(acc_ready, it * len(E_ACC) + (ACC0 + 2 * j + 1))
                        if j >= 2:
                            act.wait_ge(*e_taken(ACCR, E_ACC, 2 * j - 3, it))
                        act.activation(silu[:, j % 2, 0:W], acc_bank[(ACC0 + 2 * j) % 4][:, :], ACT.Silu)\
                           .then_inc(acc_taken["act"], 1)
                        split_high(4 * j + 4)
                        if j:
                            take_expert_hidden(j - 1)
                        if j == 2:
                            act.wait_ge(aux_ready, it * len(E_AUX) + (AUX0 + PG + 1))
                            act.activation(pickT[:, :, :].rearrange("p a b -> p (a b)"),
                                           aux_bank[(AUX0 + PG) % 4][:, 0:T * P], ACT.Copy).then_inc(aux_taken["act"], 1)
                        split_high(4 * j + 5)
                        split_high(4 * j + 6)
                    for u in range(4 * E_GROUPS + 3, E_UNITS):
                        split_high(u)
                        if u == 4 * E_GROUPS + 4:
                            take_expert_hidden(E_GROUPS - 1)
                        if u == 4 * E_GROUPS + X_AFTER + 2:
                            for i in range(4):
                                take_gathered(i, it * len(E_AUX) + (AUX0 + X0 + i + 1))
            take_result(passes * N_EXP)

        @block.gpsimd
        def _(pool):
            steps = [0]

            def link(ins):
                steps[0] += 1
                ins.then_inc(pool_step, 1)
                pool.wait_ge(pool_step, steps[0])

            link(pool.memset(ident[:, :], 0.0))
            pool.affine_select(out=ident[:, :], in_=ident[:, :], compare_op=ALU.not_equal, fill=1.0, base=0,
                               pattern=[[-1, P]], channel_multiplier=1).then_inc(ident_ready, 1)
            inv_freq = np.float32(10000.0) ** (-np.arange(32, dtype=np.float32) / np.float32(32))
            for i in range(32):
                pool.memset(freq[:, i:i + 1], float(inv_freq[i]))
            for c0, c1, n in ((0, 5, 64), (5, 6, B_QR), (6, 7, B_KVR), (7, 8, B_ROPE), (8, 18, 64),
                              (18, 22, 64), (22, 26, 32), (26, 30, 64)):
                pool.memset(invn[:, c0:c1], 1.0 / n)
            for z in (kcz[:, :, :, :], kaz[:, :, :], ikz[:, :, :], cmask[:, :], wmask[:, :]):
                pool.memset(z, 0.0)
            pool.memset(ones[:, :], 1.0)
            link(pool.memset(lower[:, :], 1.0))
            pool.affine_select(out=cmask[:, P:], in_=cmask[:, P:], compare_op=ALU.is_ge, fill=MASKED, base=0,
                               pattern=[[-1, P]], channel_multiplier=1)
            pool.affine_select(out=wmask[:, P:], in_=wmask[:, P:], compare_op=ALU.is_ge, fill=MASKED, base=0,
                               pattern=[[-1, P]], channel_multiplier=1)
            pool.affine_select(out=wmask[:, 0:P], in_=wmask[:, 0:P], compare_op=ALU.is_gt, fill=MASKED, base=0,
                               pattern=[[1, P]], channel_multiplier=-1)
            pool.affine_select(out=lower[:, :], in_=lower[:, :], compare_op=ALU.is_gt, fill=0.0, base=0,
                               pattern=[[1, P]], channel_multiplier=-1)
            pool.iota(iota8[:, :], pattern=[[1, N_EXP]], base=0, channel_multiplier=0, allow_small_or_imprecise_dtypes=True)
            pool.iota(iota_slot[:, :], pattern=[[1, P]], base=0, channel_multiplier=0,
                      allow_small_or_imprecise_dtypes=True).then_inc(masks_ready, 1)
            for n, (name, _, shape) in enumerate(units):
                k = shape[0] * shape[1]
                pool.wait_ge(raw_loaded[n % RAW], 16 * (n // RAW + 1))
                if n >= PARTS:
                    pool.wait_ge(*released(n - PARTS))
                pool.tensor_scalar(part_h[:, n % PARTS, 0:k], raw[:, n % RAW, 0:k], 1.0, 1.0, ALU.mult, ALU.mult)\
                    .then_inc(high_split, 1)
                if low_by[n] == "pool":
                    pool.wait_ge(high_split, n + 1)
                    pool.tensor_tensor(part_l[:, n % PARTS, 0:k], raw[:, n % RAW, 0:k],
                                       part_h[:, n % PARTS, 0:k].bitcast(F32), ALU.subtract).then_inc(low_split["pool"], 1)

        @block.vector
        def _(dve):
            steps, splits = [0], [0]

            def link(ins):
                steps[0] += 1
                ins.then_inc(dve_step, 1)
                dve.wait_ge(dve_step, steps[0])

            def root(y, v, tmp):
                link(dve.tensor_scalar(tmp.bitcast(I32), v.bitcast(I32), 1, None, ALU.logical_shift_right))
                link(dve.tensor_scalar(y.bitcast(I32), tmp.bitcast(I32), -1.0, float(0x5f3759df), ALU.mult, ALU.add))
                for _ in range(3):
                    link(dve.tensor_tensor(tmp, y, y, ALU.mult))
                    link(dve.scalar_tensor_tensor(out=tmp, in0=tmp, scalar=-0.5, in1=v, op0=ALU.mult, op1=ALU.mult))
                    link(dve.scalar_tensor_tensor(out=y, in0=tmp, scalar=1.5, in1=y, op0=ALU.add, op1=ALU.mult))

            own_units = [n for n in range(UNITS0) if low_by[n] == "dve"]

            def split_low(count):
                for n in own_units[splits[0]:splits[0] + count]:
                    k = units[n][2][0] * units[n][2][1]
                    dve.wait_ge(high_split, n + 1)
                    dve.tensor_tensor(part_l[:, n % PARTS, 0:k], raw[:, n % RAW, 0:k],
                                      part_h[:, n % PARTS, 0:k].bitcast(F32), ALU.subtract).then_inc(low_split["dve"], 1)
                splits[0] += count

            def name_of_next():
                return units[own_units[splits[0]]][0]

            def take_low(name, dst, high, rows=None):
                dve.wait_ge(high_taken, aux.high(name))
                b = aux_bank[aux.bank(name)]
                n = dst.shape[2]
                if rows is None:
                    dve.tensor_tensor(dst, b[:, 0:dst.shape[1] * n].rearrange("p (c n) -> p c n", n=n), high.bitcast(F32),
                                      ALU.subtract).then_inc(aux_taken["dve"], 1)
                    return
                for c in range(2):
                    ins = dve.scalar_tensor_tensor(out=dst[:, c, :], in0=b[:, c * n:(c + 1) * n], scalar=rows[:, c:c + 1],
                                                   in1=high[:, c, :].bitcast(F32), op0=ALU.mult, op1=ALU.subtract)
                ins.then_inc(aux_taken["dve"], 1)

            def take_low_four(kind, l, row=None):
                for i in range(4):
                    rows = None if row is None else gainT[:, row + 2 * i:row + 2 * i + 2]
                    take_low((kind, l, i), hTl[:, 2 * i:2 * i + 2, :], hTh[:, 2 * i:2 * i + 2, :], rows)

            def find_angles(row, turn, shift):
                if row == 2:
                    dve.wait_ge(consts_loaded, CONSTS)
                    dve.wait_ge(masks_ready, 1)
                TWO_PI, MAGIC = 2.0 * np.pi, 1.5 * 2.0 ** 23
                C1 = 6.28125
                C2 = float(np.round((TWO_PI - C1) * 2 ** 19) / 2 ** 19)
                C3 = float(TWO_PI - C1 - C2)
                if row == 2:
                    link(dve.tensor_copy(pos_f[:, :], pos_i[:, :]))
                    link(dve.tensor_tensor(ang[:, 0, :, :], freq[:, :].unsqueeze(1).to_broadcast([P, T, 32]),
                                           pos_f[:, :].unsqueeze(2).to_broadcast([P, T, 32]), ALU.mult))
                r, k = ang[:, row, :, :], ang[:, 1, :, :]
                link(dve.tensor_scalar(k, ang[:, 0, :, :], float(1.0 / TWO_PI), turn, ALU.mult, ALU.add))
                link(dve.tensor_scalar(k, k, MAGIC, None, ALU.add))
                link(dve.tensor_scalar(k, k, -MAGIC, None, ALU.add))
                link(dve.scalar_tensor_tensor(out=r, in0=k, scalar=-C1, in1=ang[:, 0, :, :], op0=ALU.mult, op1=ALU.add))
                link(dve.scalar_tensor_tensor(out=r, in0=k, scalar=-C2, in1=r, op0=ALU.mult, op1=ALU.add))
                link(dve.scalar_tensor_tensor(out=r, in0=k, scalar=-C3, in1=r, op0=ALU.mult, op1=ALU.add))
                link(dve.tensor_scalar(r, r, float(shift), 3.1415925, ALU.add, ALU.min))
                dve.tensor_scalar(r, r, -3.1415925, None, ALU.max).then_inc(angles_ready, 1)
                dve.wait_ge(angles_ready, row - 1)

            def spread_tables():
                dve.wait_ge(trig_ready, 1)
                sin, cos = trig[:, 0, :, :], trig[:, 1, :, :]
                for h in range(2):
                    dve.tensor_copy(cos64[:, :, 32 * h:32 * h + 32], cos)
                    dve.tensor_copy(cos32[:, :, 16 * h:16 * h + 16], cos[:, :, 0:32:2])
                    dve.tensor_scalar(sin64[:, :, 32 * h:32 * h + 32], sin, 2.0 * h - 1.0, None, ALU.mult)
                    ins = dve.tensor_scalar(sin32[:, :, 16 * h:16 * h + 16], sin[:, :, 0:32:2], 2.0 * h - 1.0, None, ALU.mult)
                link(ins)
                dve.memset(top8[:, :], 0.0).then_inc(tables_ready, 1)

            def norm_x(fill=None):
                for t in range(T):
                    if fill is None:
                        dve.wait_ge(x_loaded[t], 16)
                    else:
                        for h in range(2):
                            add_to_x(fill(t, h), t, h)
                        dve.wait_ge(*acc.taken(fill(t, 1)))
                    ins = dve.scalar_tensor_tensor(out=xn[:, t, :], in0=x_sb[:, t, :], scalar=1.0, in1=x_sb[:, t, :],
                                                   op0=ALU.mult, op1=ALU.mult, accum_out=xstat[:, t:t + 1])
                    link(ins)
                link(dve.tensor_scalar(xstat[:, :], xstat[:, :], 1.0 / D_MODEL, EPS, ALU.mult, ALU.add))
                root(xrstd[:, :], xstat[:, :], newton[:, 0, :, 0])
                for t in range(T):
                    dve.tensor_scalar(xn[:, t, :], x_sb[:, t, :], xrstd[:, t:t + 1], None, ALU.mult).then_inc(normed, 1)

            def sum_squares(dst, view):
                link(dve.tensor_reduce(dst, view, AX_X, ALU.add))

            def finish_means(c0, c1):
                link(dve.tensor_tensor(stat[:, :, c0:c1], stat[:, :, c0:c1],
                                       invn[:, c0:c1].unsqueeze(1).to_broadcast([P, T, c1 - c0]), ALU.mult))
                link(dve.tensor_scalar(stat[:, :, c0:c1], stat[:, :, c0:c1], EPS, None, ALU.add))
                root(rstd[:, :, c0:c1], stat[:, :, c0:c1], newton[:, 0, :, c0:c1])

            def scale_heads(v, c0, heads, d):
                r = rstd[:, :, c0:c0 + heads].unsqueeze(3).to_broadcast([P, T, heads, d])
                link(dve.tensor_tensor(v, v, r, ALU.mult))

            def rotate(v, heads, d, dsts):
                half = d // 2
                cs, sn = (cos64, sin64) if d == 64 else (cos32, sin32)
                tmp = swing[:, 0:T * heads * d].rearrange("p (t h d) -> p t h d", t=T, d=d)

                def over(a):
                    return a.unsqueeze(2).to_broadcast([P, T, heads, a.shape[-1]])
                dve.tensor_tensor(tmp[:, :, :, 0:half], v[:, :, :, half:], over(sn[:, :, 0:half]), ALU.mult)
                link(dve.tensor_tensor(tmp[:, :, :, half:], v[:, :, :, 0:half], over(sn[:, :, half:]), ALU.mult))
                link(dve.tensor_tensor(v, v, over(cs[:, :, :]), ALU.mult))
                for dst in dsts:
                    ins = dve.tensor_tensor(dst, v, tmp, ALU.add)
                return ins

            def squares(c0, n, off):
                v = sq[:, off:off + T * n].rearrange("p (t n) -> p t n", t=T)
                link(dve.tensor_tensor(v, proj[:, :, c0:c0 + n], proj[:, :, c0:c0 + n], ALU.mult))
                return v

            def add_to_x(l_fill, t, h):
                b = acc_bank[acc.bank(l_fill)]
                dve.wait_ge(acc_ready, acc.no(l_fill))
                xs = x_sb[:, t, h * W:(h + 1) * W]
                dve.tensor_tensor(xs, xs, b[:, :], ALU.add).then_inc(acc_taken["dve"], 1)

            for l in range(DEPTH):
                norm_x((lambda t, h: ("y", t, h)) if l else None)
                split_low(1)
                dve.wait_ge(*aux.taken(("gains",)))
                take_low_four("h", l, GROW["attn_norm_g", l])
                split_low(2)
                if l == 0:
                    find_angles(2, 0.0, 0.0)
                split_low(1)
                if l == 0:
                    find_angles(3, 0.25, np.pi / 2)
                qa, ka = heads_of(proj, COL["qa"], 4, 64), heads_of(proj, COL["ka"], 1, 64)
                dve.wait_ge(*acc.taken(("p", l, 0, 1)))
                v = squares(0, 320, 900)
                sum_squares(stat[:, :, 0:5], v.rearrange("p t (h d) -> p t h d", d=64))
                split_low(1)
                finish_means(0, 5)
                split_low(1)
                scale_heads(heads_of(proj, 0, 5, 64), 0, 5, 64)
                dve.tensor_tensor(qa, qa, gain("aq", l, 4), ALU.mult)
                link(dve.tensor_tensor(ka, ka, gain("ak", l, 1), ALU.mult))
                split_low(1)
                if l == 0:
                    spread_tables()
                link(rotate(qa, 4, 64, [qa]))
                split_low(1)
                link(rotate(ka, 1, 64, [ka2[:, :, 64 * v:64 * v + 64].unsqueeze(2) for v in range(2)]))
                dve.wait_ge(*acc.taken(("p", l, 1, 1)))
                link(dve.tensor_scalar(iws[:, :, :], proj[:, :, COL["iw"]:COL["iw"] + 8],
                                       float(IDX_HEADS ** -0.5 * IDX_DIM ** -0.5), None, ALU.mult))
                link(rotate(heads_of(proj, COL["ik"], 1, 32), 1, 32,
                            [ik4[:, :, 32 * v:32 * v + 32].unsqueeze(2) for v in range(4)]))
                split_low(1)
                rotate(heads_of(proj, COL["iq"], 8, 32), 8, 32, [heads_of(proj, COL["iq"], 8, 32)]).then_inc(roped_a, 1)
                dve.wait_ge(roped_a, l + 1)
                dve.wait_ge(*acc.taken(("p", l, 2, 1)))
                v = squares(COL["cq"], 416, 0)
                sum_squares(stat[:, :, 5:6], v[:, :, 0:256].unsqueeze(2))
                sum_squares(stat[:, :, 6:7], v[:, :, 256:384].unsqueeze(2))
                sum_squares(stat[:, :, 7:8], v[:, :, 384:416].unsqueeze(2))
                finish_means(5, 8)
                scale_heads(heads_of(proj, COL["cq"], 1, 256), 5, 1, 256)
                dve.tensor_tensor(heads_of(proj, COL["ckv"], 1, 128), heads_of(proj, COL["ckv"], 1, 128),
                                  rstd[:, :, 6:7].unsqueeze(3).to_broadcast([P, T, 1, 128]), ALU.mult).then_inc(lowrank_ready, 1)
                kr = heads_of(proj, COL["kr"], 1, 32)
                scale_heads(kr, 7, 1, 32)
                link(dve.tensor_tensor(kr, kr, gain("kr", l, 1), ALU.mult))
                link(rotate(kr, 1, 32, [kcat[:, :, h:h + 1, 64:96] for h in range(B_HEADS)]))
                dve.wait_ge(*acc.taken(("p", l, len(ATT_GROUPS) - 1, 1)))
                v = squares(COL["qc"], 640, 0)
                sum_squares(stat[:, :, 8:18], v.rearrange("p t (h d) -> p t h d", d=64))
                finish_means(8, 18)
                qc, kc = heads_of(proj, COL["qc"], 8, 64), heads_of(proj, COL["kc"], 2, 64)
                scale_heads(heads_of(proj, COL["qc"], 10, 64), 8, 10, 64)
                dve.tensor_tensor(qc, qc, gain("cq", l, 8), ALU.mult)
                link(dve.tensor_tensor(kc, kc, gain("ck", l, 2), ALU.mult))
                link(rotate(qc, 8, 64, [qc]))
                rotate(kc, 2, 64, [kc2[:, :, :, 64 * v:64 * v + 64] for v in range(2)]).then_inc(roped_c, 1)

                dve.wait_ge(*aux.taken(("ukv", l, 1)))
                v = sq[:, 0:T * 384].rearrange("p (t h d) -> p t h d", t=T, d=96)
                qbh = qb[:, :, :].rearrange("p t (h d) -> p t h d", d=96)
                kvh = kvb[:, :, :].rearrange("p t (h d) -> p t h d", d=128)
                vk = sq[:, 1024:1024 + T * 256].rearrange("p (t h d) -> p t h d", t=T, d=64)
                dve.tensor_tensor(v, qbh, qbh, ALU.mult)
                link(dve.tensor_tensor(vk, kvh[:, :, :, 0:64], kvh[:, :, :, 0:64], ALU.mult))
                sum_squares(stat[:, :, 18:22], v[:, :, :, 0:64])
                sum_squares(stat[:, :, 22:26], v[:, :, :, 64:96])
                sum_squares(stat[:, :, 26:30], vk)
                finish_means(18, 30)
                scale_heads(qbh[:, :, :, 0:64], 18, 4, 64)
                scale_heads(qbh[:, :, :, 64:96], 22, 4, 32)
                scale_heads(kvh[:, :, :, 0:64], 26, 4, 64)
                dve.tensor_tensor(qbh[:, :, :, 0:64], qbh[:, :, :, 0:64], gain("qn", l, 4), ALU.mult)
                link(dve.tensor_tensor(qbh[:, :, :, 64:96], qbh[:, :, :, 64:96], gain("qr", l, 4), ALU.mult))
                tmp = sq[:, 0:T * 128].rearrange("p (t h d) -> p t h d", t=T, d=32)
                qr = qbh[:, :, :, 64:96]

                def over(a):
                    return a.unsqueeze(2).to_broadcast([P, T, 4, a.shape[-1]])
                dve.tensor_tensor(tmp[:, :, :, 0:16], qr[:, :, :, 16:32], over(sin32[:, :, 0:16]), ALU.mult)
                link(dve.tensor_tensor(tmp[:, :, :, 16:32], qr[:, :, :, 0:16], over(sin32[:, :, 16:32]), ALU.mult))
                link(dve.tensor_tensor(qr, qr, over(cos32[:, :, :]), ALU.mult))
                dve.tensor_tensor(qr, qr, tmp, ALU.add)
                dve.tensor_tensor(kcat[:, :, :, 0:64], kvh[:, :, :, 0:64], gain("kn", l, 4), ALU.mult)\
                   .then_inc(mla_heads_ready, 1)

                n = 0
                for t in range(T):
                    nk = P * (t + 1)
                    per = W // nk
                    for i in range(2 * (t + 1)):
                        dve.wait_ge(*aux.taken(("ix", l, t, i)))
                        for j in range(per):
                            h = i * per + j
                            rel = swing[:, (n % 2) * W + j * nk:(n % 2) * W + (j + 1) * nk]
                            wgt = iws[:, t, h:h + 1]
                            if h == 0:
                                ins = dve.tensor_scalar(score[:, t, 0:nk], rel, wgt, None, ALU.mult)
                            else:
                                ins = dve.scalar_tensor_tensor(out=score[:, t, 0:nk], in0=rel, scalar=wgt, in1=score[:, t, 0:nk],
                                                               op0=ALU.mult, op1=ALU.add)
                            if j < per - 1:
                                link(ins)
                        n += 1
                        ins.then_inc(relu_used, 1)
                        dve.wait_ge(relu_used, 6 * l + n)
                    link(dve.tensor_tensor(score[:, t, 0:nk], score[:, t, 0:nk], cmask[:, SEQ - nk:], ALU.add))

                def take_output(i):
                    take_low(("yt", l, i), hTl[:, 2 * i:2 * i + 2, :], hTh[:, 2 * i:2 * i + 2, :])

                def merge(m):
                    gi = "abc".index(m)
                    for t in range(T):
                        for h in range(2):
                            name = ("m", l, m, t, h)
                            dve.wait_ge(acc_ready, acc.no(name))
                            b = acc_bank[acc.bank(name)]
                            e = gates[:, t, gi * D_MODEL + h * W:gi * D_MODEL + (h + 1) * W]
                            to = merged[:, t, :] if m == "c" else swing[:, 0:D_MODEL]
                            dve.tensor_tensor(to[:, h * W:(h + 1) * W], b[:, :], e, ALU.mult).then_inc(acc_taken["dve"], 1)
                        dve.wait_ge(*acc.taken(name))
                        if m != "c":
                            ins = dve.tensor_tensor(merged[:, t, :], merged[:, t, :], swing[:, 0:D_MODEL], ALU.add)
                            if m == "a":
                                ins.then_inc(merged_ready, 1)
                                dve.wait_ge(merged_ready, 2 * l + t + 1)
                            else:
                                link(ins)

                def best_of(t, rounds):
                    nk = P * (t + 1)
                    for r in rounds:
                        link(dve.max(top8[:, :], score[:, t, 0:nk]))
                        link(dve.match_replace(score[:, t, 0:nk], top8[:, :], score[:, t, 0:nk], REMOVED))
                    if rounds[-1] == TOPK // 8 - 1:
                        link(dve.tensor_scalar(selmask[:, t, 0:nk], score[:, t, 0:nk], REMOVED * 0.5, MASKED, ALU.is_gt, ALU.mult))
                        link(dve.tensor_tensor(selmask[:, t, 0:nk], selmask[:, t, 0:nk], cmask[:, SEQ - nk:], ALU.add))

                half = TOPK // 16
                rounds = (range(0, half), range(half, TOPK // 8))

                for s in range(len(JOBS) + 2):
                    if s < len(JOBS):
                        m, t = JOBS[s]
                        nk = P * (t + 1)
                        per = W // nk
                        mask = dict(a=selmask[:, t, 0:nk], b=cmask[:, SEQ - nk:]).get(m, wmask[:, SEQ - nk:])
                        if s >= 2:
                            dve.wait_ge(aux_ready, aux.no(("pt", l, s - 2, JOBS[s - 2][1])))
                        for i in range(t + 1):
                            dve.wait_ge(aux_ready, aux.no(("lg", l, s, i)))
                            b = aux_bank[aux.bank(("lg", l, s, i))]
                            dve.scalar_tensor_tensor(out=logit[:, s % 2, i * per:(i + 1) * per, 0:nk],
                                                     in0=b[:, :].rearrange("p (h k) -> p h k", k=nk), scalar=SCALE[m],
                                                     in1=mask.unsqueeze(1).to_broadcast([P, per, nk]),
                                                     op0=ALU.mult, op1=ALU.add).then_inc(aux_taken["dve"], 1)
                        dve.wait_ge(*aux.taken(("lg", l, s, t)))
                        red = dve.tensor_reduce(nmax[:, s % 2, :], logit[:, s % 2, :, 0:nk], AX_X, ALU.max, negate=True)
                        if m[0] == "c":
                            link(red)
                            o = GAINS["sink"][0] + 4 * int(m[1])
                            sink = gains[:, l, o:o + 4]
                            link(dve.scalar_tensor_tensor(out=nmax[:, s % 2, :], in0=sink, scalar=-1.0, in1=nmax[:, s % 2, :],
                                                          op0=ALU.mult, op1=ALU.min))
                            red = dve.tensor_tensor(sinkx[:, s % 4, 0, :], sink, nmax[:, s % 2, :], ALU.add)
                        red.then_inc(logits_ready, 1)
                        if s < 4:
                            best_of(s // 2, rounds[s % 2])
                        if s == 6:
                            take_output(2)
                            take_output(3)
                        if s == 7:
                            split_low(1)
                            dve.wait_ge(*acc.taken(("g", l, 5, 1)))
                            merge("c")
                    if s == 9:
                        take_output(1)
                    if s >= 2:
                        q = s - 2
                        m, t = JOBS[q]
                        dve.wait_ge(probs_ready, len(JOBS) * l + q + 1)
                        if m[0] == "c":
                            link(dve.tensor_tensor(denom[:, q % 4, :], denom[:, q % 4, :], sinkx[:, q % 4, 1, :], ALU.add))
                        link(dve.reciprocal(rden[:, q % 4, :], denom[:, q % 4, :]))
                        dve.wait_ge(aux_ready, aux.no(("pv", l, q)))
                        b = aux_bank[aux.bank(("pv", l, q))]
                        c0 = Y_COL[m]
                        dve.tensor_tensor(xn[:, t, c0:c0 + 256].rearrange("p (h d) -> p h d", d=64),
                                          b[:, 0:256].rearrange("p (h d) -> p h d", d=64),
                                          rden[:, q % 4, :].unsqueeze(2).to_broadcast([P, 4, 64]), ALU.mult)\
                           .then_inc(aux_taken["dve"], 1)
                    if s == 6:
                        split_low(2)
                    if s == 8:
                        split_low(1)

                take_output(0)
                dve.wait_ge(*acc.taken(("g", l, 2, 1)))
                dve.wait_ge(gates_ready, l + 1)
                merge("b")
                merge("a")
                take_low_four("mt", l)
                split_low(3)
                norm_x(lambda t, h, l=l: ("o", l, t, h))
                if l == 0:
                    split_low(1)
                    take_low_four("f", l, GROW["ffn_norm_g", l])
                    split_low(1)

                    def take_hidden_low(j):
                        c0, n = 4 * j, FF_GROUPS[j][1] // P
                        for t in range(T):
                            at = (slice(None), slice(c0, c0 + n), slice(t * P, (t + 1) * P))
                            take_low(("ht", j, t), ffTl[at], ffTh[at])

                    for j, (_, n) in enumerate(FF_GROUPS):
                        wide = n > 256
                        split_low(1)
                        if j:
                            take_hidden_low(j - 1)
                        if wide:
                            split_low(2)
                        for t in range(T):
                            dve.wait_ge(acc_ready, acc.no(("h3", j, t)))
                            dve.wait_ge(*acc.taken(("h1", j, t)))
                            dve.tensor_tensor(ff_hidden[:, t, 0:n], ff_silu[:, t, 0:n],
                                              acc_bank[acc.bank(("h3", j, t))][:, 0:n], ALU.mult).then_inc(acc_taken["dve"], 1)
                        split_low(1)
                    split_low(1)
                    take_hidden_low(len(FF_GROUPS) - 1)
                    while name_of_next()[0] == "w2":
                        split_low(1)

            row = GROW["ffn_norm_g", DEPTH - 1]
            for i in (1, 3):
                dve.wait_ge(aux_ready, aux.no(("f", DEPTH - 1, i)))
                b = aux_bank[aux.bank(("f", DEPTH - 1, i))]
                for c in range(2):
                    k = 2 * i + c
                    ins = dve.tensor_scalar(h2T[:, k, :], b[:, c * SEQ:(c + 1) * SEQ], gainT[:, row + k:row + k + 1], None,
                                            ALU.mult)
                ins.then_inc(aux_taken["dve"], 1)
            for t in range(T):
                dve.wait_ge(*aux.taken(("router", t)))
                link(dve.max(rtop[:, t, :], rl[:, t, :]))
                link(dve.max_index(ridx[:, t, :], rtop[:, t, :], rl[:, t, :]))
            link(dve.tensor_copy(ridxf[:, :, :], ridx[:, :, :]))
            dve.tensor_tensor(gate2[:, :, 0:1], rtop[:, :, 1:2], rtop[:, :, 0:1], ALU.subtract).then_inc(routed, 1)
            for k in range(2):
                ins = dve.tensor_tensor(onehot[:, :, k, :], iota8[:, :].unsqueeze(1).to_broadcast([P, T, 8]),
                                        ridxf[:, :, k:k + 1].to_broadcast([P, T, 8]), ALU.is_equal)
            link(ins)
            dve.tensor_tensor(chosen[:, :, :], onehot[:, :, 0, :], onehot[:, :, 1, :], ALU.add).then_inc(chosen_ready, 1)
            dve.wait_ge(routed, 2)
            link(dve.tensor_scalar(gate2[:, :, 0:1], gate2[:, :, 1:2], 1.0, None, ALU.add))
            link(dve.reciprocal(gate2[:, :, 0:1], gate2[:, :, 0:1]))
            link(dve.tensor_tensor(gate2[:, :, 1:2], gate2[:, :, 1:2], gate2[:, :, 0:1], ALU.mult))
            link(dve.tensor_tensor(gated[:, :, 0:8], onehot[:, :, 0, :], gate2[:, :, 0:1].to_broadcast([P, T, 8]), ALU.mult))
            link(dve.tensor_tensor(onehot[:, :, 1, :], onehot[:, :, 1, :], gate2[:, :, 1:2].to_broadcast([P, T, 8]), ALU.mult))
            link(dve.tensor_tensor(gated[:, :, 0:8], gated[:, :, 0:8], onehot[:, :, 1, :], ALU.add))
            link(dve.tensor_copy(gated[:, :, 8:9], gated[:, :, 0:1]))
            dve.memset(pickT[:, :, :], 0.0)
            link(dve.memset(slot_flat[:, :, 2 * N_EXP:], -1.0))
            dve.wait_ge(chosen_ready, 1)
            dve.wait_ge(aux_ready, aux.no(("slots",)))
            b = aux_bank[aux.bank(("slots",))]
            link(dve.scalar_tensor_tensor(out=slot_of[:, :, 0, :], in0=b[:, 0:16].rearrange("p (t e) -> p t e", t=T),
                                          scalar=1.0, in1=chosen[:, :, :], op0=ALU.add, op1=ALU.mult))
            link(dve.tensor_scalar(slot_of[:, :, 0, :], slot_of[:, :, 0, :], -1.0, None, ALU.add))
            link(dve.tensor_scalar(slot_of[:, :, 1, :], slot_of[:, :, 0, :], float(-P), None, ALU.add))

            def make_picks(slot, expert):
                for t in range(T):
                    dve.tensor_scalar(pick[:, t, :], iota_slot[:, :], slot_flat[:, t, slot], None, ALU.is_equal)
                for t in range(T):
                    ins = dve.tensor_scalar(pickg[:, t, :], iota_slot[:, :], slot_flat[:, t, slot], gated[:, t, expert],
                                            ALU.is_equal, ALU.mult)
                ins.then_inc(onehot_ready, 1)

            def take_gathered_low(i, high=None):
                if high is not None:
                    dve.wait_ge(high_taken, high)
                for c in range(2):
                    k = 2 * i + c
                    ins = dve.scalar_tensor_tensor(
                        out=xgTl[:, k, :], in0=aux_bank[(AUX0 + i) % 4][:, c * P:(c + 1) * P],
                        scalar=gainT[:, row + k:row + k + 1], in1=xgTh[:, k, :].bitcast(F32),
                        op0=ALU.mult, op1=ALU.subtract)
                ins.then_inc(aux_taken["dve"], 1)

            def add_result(t, h, fill, ready):
                dve.wait_ge(aux_ready, ready)
                xs = x_sb[:, t, h * W:(h + 1) * W]
                dve.tensor_tensor(xs, xs, aux_bank[(AUX0 + fill) % 4][:, :], ALU.add).then_inc(aux_taken["dve"], 1)

            make_picks(slice(0, 1), slice(0, 1))
            dve.tensor_reduce(cnt[:, 0:1], b[:, 16:24], AX_X, ALU.max).then_inc(aux_taken["dve"], 1)
            dve.wait_ge(*aux.taken(("slots",)))
            link(dve.tensor_scalar(cnt[:, 1:2], cnt[:, 0:1], float(P), 1.0, ALU.is_gt, ALU.add))
            link(dve.tensor_scalar(cnt[:, 2:3], cnt[:, 1:2], float(N_EXP), -1.0, ALU.mult, ALU.add))
            dve.tensor_copy(n_pass[:, :], cnt[:, 1:3]).then_inc(passes_ready, 1)
            for i in range(4):
                dve.wait_ge(aux_ready, aux.no(("x", i)))
                for c in range(2):
                    k = 2 * i + c
                    ins = dve.tensor_scalar(xgTh[:, k, :], aux_bank[(AUX0 + i) % 4][:, c * P:(c + 1) * P],
                                            gainT[:, row + k:row + k + 1], None, ALU.mult)
                link(ins)
                take_gathered_low(i)
            dve.wait_ge(passes_ready, 1)

            passes = dve.value_load(n_pass[0:1, 0:1], min_val=1, max_val=2)
            with dve.Fori(0, passes) as ps:
                with dve.Fori(0, N_EXP) as e:
                    it = ps * N_EXP + e

                    def split_expert_low(u):
                        dve.wait_ge(e_high_split, it * E_UNITS + (u + 1))
                        dve.tensor_tensor(e_part_l[:, u % E_PARTS, :], e_raw[:, u % E_RAW, :],
                                          e_part_h[:, u % E_PARTS, :].bitcast(F32), ALU.subtract).then_inc(low_split["dve"], 1)

                    def take_expert_low(j):
                        dve.wait_ge(high_taken, it * E_HIGHS + (HIGH0 + j + 1))
                        at = lambda b: b[:, 4 * j:4 * j + 4, :].rearrange("p a b -> p (a b)")
                        dve.tensor_tensor(at(hidTl), aux_bank[(AUX0 + HT[j]) % 4][:, :], at(hidTh).bitcast(F32),
                                          ALU.subtract).then_inc(aux_taken["dve"], 1)

                    def add_tile(t):
                        for h in range(2):
                            fill = CB[2 * t + h]
                            add_result(t, h, fill, it * len(E_AUX) + (AUX0 + fill + 1))

                    for u in range(3):
                        split_expert_low(u)
                    for j in range(E_GROUPS):
                        i = 2 * j + 1
                        split_expert_low(4 * j + 3)
                        if j:
                            take_expert_low(j - 1)
                        if j == 1:
                            add_tile(0)
                        split_expert_low(4 * j + 4)
                        split_expert_low(4 * j + 5)
                        dve.wait_ge(acc_ready, it * len(E_ACC) + (ACC0 + i + 1))
                        dve.wait_ge(*e_taken(ACCR, E_ACC, i - 1, it))
                        dve.tensor_tensor(hidden[:, j % 2, 0:W], silu[:, j % 2, 0:W], acc_bank[(ACC0 + i) % 4][:, :],
                                          ALU.mult).then_inc(acc_taken["dve"], 1)
                        if j == 1:
                            add_tile(1)
                        split_expert_low(4 * j + 6)
                        if j == 3:
                            dve.wait_ge(aux_ready, it * len(E_AUX) + (AUX0 + PG + 1))
                            make_picks(bass.ds(it + 1, 1), bass.ds(e + 1, 1))
                    for u in range(4 * E_GROUPS + 3, E_UNITS):
                        split_expert_low(u)
                        if u == 4 * E_GROUPS + 4:
                            take_expert_low(E_GROUPS - 1)
                        if u == 4 * E_GROUPS + X_AFTER + 2:
                            for i in range(4):
                                take_gathered_low(i, it * E_HIGHS + (HIGH0 + E_GROUPS + i + 1))
            for t in range(T):
                for h in range(2):
                    add_result(t, h, 2 * t + h, passes * (N_EXP * len(E_AUX)) + (AUX0 + 2 * t + h + 1))

        @block.tensor
        def _(pe):
            def begin(bank_ring, name):
                free = bank_ring.free(name)
                if free is not None:
                    pe.wait_ge(*free)
                return (acc_bank if bank_ring is acc else aux_bank)[bank_ring.bank(name)]

            def used(ins, name):
                assert name not in ends_fill
                return ins.then_inc(unit_used, 1)

            def keep_warm(bank_ring, name, count):
                b = begin(bank_ring, name)
                for _ in range(count):
                    pe.matmul(b[:, :].rearrange("p (a b) -> p a b", a=4), ident[:, :],
                              ident[:, :].unsqueeze(1).to_broadcast([P, 4, P]), start=True, stop=True)

            pe.wait_ge(rows_loaded, ROWS)
            pe.wait_ge(ident_ready, 1)
            b = begin(aux, ("gains",))
            pe.transpose(b[:, 0:NROWS], gain_rows[0:NROWS, :], ident[0:NROWS, 0:NROWS]).then_inc(aux_ready, 1)

            def transposes(kind, l, src, fills=range(4)):
                for i in fills:
                    b = begin(aux, (kind, l, i))
                    for c in range(2):
                        for t in range(T):
                            k = 2 * i + c
                            ins = pe.transpose(b[:, (2 * c + t) * P:(2 * c + t + 1) * P], src[:, t, k * P:(k + 1) * P], ident[:, :])
                    ins.then_inc(aux_ready, 1)

            def four(name, blocks):
                b = begin(aux, name)
                for i, src in enumerate(blocks):
                    m = src.shape[1]
                    ins = pe.transpose(b[0:m, i * P:(i + 1) * P], src, ident[:, :])
                ins.then_inc(aux_ready, 1)

            def three(out, xh, xl, wh, wl, first, last):
                pe.matmul(out, xh, wh, start=first, stop=False)
                pe.matmul(out, xh, wl, start=False, stop=False)
                return pe.matmul(out, xl, wh, start=False, stop=last)

            def stream(fills, names, xh, xl, chunks, cols, taken={}, between=None):
                banks = {}
                k0 = 0
                for u, name in enumerate(names):
                    if between is not None:
                        between(u)
                    wh, wl = parts(name)
                    pe.wait_ge(*arrived(name))
                    for (t, h), fill in fills.items():
                        if u == 0:
                            banks[t, h] = begin(acc, fill)
                        for c in range(shape_of[name][0]):
                            k, m, b = k0 + c, cols(h), banks[t, h]
                            if k in taken and (t, h) == (0, 0):
                                pe.wait_ge(*aux.taken(taken[k]))
                            n = wh[:, c, m].shape[1]
                            ins = three(b[:, 0:n], xh[:, k, t * P:(t + 1) * P], xl[:, k, t * P:(t + 1) * P],
                                        wh[:, c, m], wl[:, c, m], k == 0, k == chunks - 1)
                            if k == chunks - 1:
                                ins.then_inc(acc_ready, 1)
                    k0 += shape_of[name][0]
                    if name not in ends_fill:
                        used(ins, name)

            def pairs(kind, l, first=0, last=KC):
                return {k - first: (kind, l, k // 2) for k in range(first, last, 2)}

            def project(kind, l, g, half, banks={}):
                name = (kind, l, g, half)
                wh, wl = parts(name)
                n = shape_of[name][1]
                pe.wait_ge(*arrived(name))
                for t in range(T):
                    if half == 0:
                        banks[t] = begin(acc, (kind, l, g, t))
                    for c in range(4):
                        k = 4 * half + c
                        if (kind, g, t) == ("p", 0, 0) and k % 2 == 0:
                            pe.wait_ge(*aux.taken(("h", l, k // 2)))
                        ins = three(banks[t][:, 0:n], hTh[:, k, t * P:(t + 1) * P], hTl[:, k, t * P:(t + 1) * P],
                                    wh[:, c, :], wl[:, c, :], k == 0, k == KC - 1)
                    if half == 1:
                        ins.then_inc(acc_ready, 1)
                if half == 0:
                    used(ins, name)

            for l in range(DEPTH):
                keep_warm(aux, ("h", l, 0), 6)
                pe.wait_ge(normed, 4 * l + 2)
                transposes("h", l, xn)
                for g in range(len(ATT_GROUPS)):
                    for half in range(2):
                        project("p", l, g, half)

                def gate(i):
                    project("g", l, GATE_ORDER[i // 2], i % 2)

                gate(0)
                gate(1)
                pe.wait_ge(lowrank_ready, l + 1)
                cq, ckv = proj[:, :, COL["cq"]:COL["ckv"]], proj[:, :, COL["ckv"]:COL["kr"]]
                four(("cq", l), [cq[:, t, c * P:(c + 1) * P] for c in range(2) for t in range(T)])
                four(("ckv", l), [ckv[:, t, :] for t in range(T)])
                pe.wait_ge(roped_a, l + 1)
                four(("ika", l), [ka2[:, t, :] for t in range(T)] + [ik4[:, t, :] for t in range(T)])
                for nm in ("iq", "qa"):
                    four((nm, l), [proj[:, t, COL[nm] + c * P:COL[nm] + (c + 1) * P] for c in range(2) for t in range(T)])
                pe.wait_ge(mla_loaded, 32 * (l + 1))
                pe.wait_ge(*aux.taken(("ckv", l)))
                for t in range(T):
                    b = begin(aux, ("uq", l, t))
                    for c in range(2):
                        ins = pe.matmul(b[:, 0:384], cqT[:, c, t * P:(t + 1) * P], uq[:, c, :], start=(c == 0), stop=(c == 1))
                    ins.then_inc(aux_ready, 1)
                for t in range(T):
                    b = begin(aux, ("ukv", l, t))
                    pe.matmul(b[:, :], ckvT[:, t * P:(t + 1) * P], ukv[:, :], start=True, stop=True).then_inc(aux_ready, 1)
                gate(2)
                gate(3)
                pe.wait_ge(roped_c, l + 1)
                four(("kc", l), [kc2[:, t, kv, :] for kv in range(C_KV) for t in range(T)])
                for i in range(2):
                    four((f"qc{i}", l), [proj[:, t, COL["qc"] + c * P:COL["qc"] + (c + 1) * P]
                                         for c in (2 * i, 2 * i + 1) for t in range(T)])
                gate(4)
                pe.wait_ge(mla_heads_ready, l + 1)
                for i in range(2):
                    four((f"qb{i}", l), [qb[:, t, 96 * h:96 * h + 96] for h in (2 * i, 2 * i + 1) for t in range(T)])
                for i in range(2):
                    four((f"kb{i}", l), [kcat[:, t, h, :] for h in (2 * i, 2 * i + 1) for t in range(T)])
                pe.wait_ge(*aux.taken(("iq", l)))
                for t in range(T):
                    nk = P * (t + 1)
                    per = W // nk
                    for i in range(2 * (t + 1)):
                        b = begin(aux, ("ix", l, t, i))
                        h0 = i * per
                        pe.matmul(b[:, :].rearrange("p (h k) -> p h k", k=nk), iqT[:, h0 // 4, t * P:(t + 1) * P],
                                  ikz[:, h0 % 4:h0 % 4 + per, 0:nk], start=True, stop=True).then_inc(aux_ready, 1)
                gate(5)
                side = lambda h: slice(h * W, (h + 1) * W)

                def mix_out(m, c0, chunks):
                    stream({(t, h): ("m", l, m, t, h) for t in range(T) for h in range(2)},
                           [("w" + m, l, u) for u in range(chunks // 2)], hTh[:, c0:c0 + chunks, :],
                           hTl[:, c0:c0 + chunks, :], chunks, side, pairs("yt", l, c0, c0 + chunks))

                for s in range(len(JOBS) + 2):
                    if s < len(JOBS):
                        m, t = JOBS[s]
                        nk = P * (t + 1)
                        per = W // nk
                        for i in range(t + 1):
                            b = begin(aux, ("lg", l, s, i))
                            for j in range(per // 2 if m != "b" else per):
                                if m == "b":
                                    h = i * per + j
                                    ins = pe.matmul(b[:, j * nk:(j + 1) * nk], qbT[0:96, h, t * P:(t + 1) * P],
                                                    kbT[0:96, h, 0:nk], start=True, stop=True)
                                else:
                                    pair = i * per // 2 + j
                                    q, k = (qaT, kaz) if m == "a" else (qcT, kcz[:, int(m[1])])
                                    blk = pair if m == "a" else 2 * int(m[1]) + pair
                                    ins = pe.matmul(b[:, 2 * j * nk:2 * (j + 1) * nk].rearrange("p (h k) -> p h k", k=nk),
                                                    q[:, blk, t * P:(t + 1) * P], k[:, :, 0:nk], start=True, stop=True)
                            ins.then_inc(aux_ready, 1)
                    if s < 6:
                        gate(6 + s)
                    if s == 6:
                        pe.wait_ge(*aux.taken(("pv", l, 3)))
                        transposes("yt", l, xn, (2, 3))
                    if s == 7:
                        mix_out("c", 4, 4)
                    if 1 <= s <= len(JOBS):
                        q, tq = s - 1, JOBS[s - 1][1]
                        pe.wait_ge(probs_ready, len(JOBS) * l + q + 1)
                        for i in range(tq + 1):
                            four(("pt", l, q, i), [logit[:, q % 2, h, i * P:(i + 1) * P] for h in range(4)])
                    if s == 9:
                        pe.wait_ge(*aux.taken(("pv", l, 5)))
                        transposes("yt", l, xn, (1,))
                    if s >= 2:
                        q = s - 2
                        m, t = JOBS[q]
                        pe.wait_ge(*aux.taken(("pt", l, q, t)))
                        b = begin(aux, ("pv", l, q))
                        for h in range(4):
                            for i in range(t + 1):
                                if m == "a":
                                    v = proj[:, i, COL["va"]:COL["va"] + 64]
                                elif m == "b":
                                    v = kvb[:, i, 128 * h + 64:128 * h + 128]
                                else:
                                    v = proj[:, i, COL["vc"] + 64 * int(m[1]):COL["vc"] + 64 * int(m[1]) + 64]
                                ins = pe.matmul(b[:, 64 * h:64 * h + 64], probT[:, q % 2, 4 * i + h, :], v,
                                                start=(i == 0), stop=(i == t))
                        ins.then_inc(aux_ready, 1)
                keep_warm(aux, ("yt", l, 0), 1)
                pe.wait_ge(*aux.taken(("pv", l, len(JOBS) - 1)))
                transposes("yt", l, xn, (0,))
                mix_out("b", 2, 2)
                mix_out("a", 0, 2)
                keep_warm(aux, ("mt", l, 0), 2)
                pe.wait_ge(merged_ready, 2 * (l + 1))
                transposes("mt", l, merged)
                stream({(t, h): ("o", l, t, h) for t in range(T) for h in range(2)},
                       [("wo", l, u) for u in range(KC // 2)], hTh, hTl, KC, side, pairs("mt", l))
                keep_warm(aux, ("f", l, 0), 6)
                pe.wait_ge(normed, 4 * l + 4)
                transposes("f", l, xn)
                if l == 0:
                    def hidden_transposes(j):
                        n = FF_GROUPS[j][1]
                        for t in range(T):
                            pe.wait_ge(*acc.taken(("h3", j, t)))
                            four(("ht", j, t), [ff_hidden[:, t, c * P:(c + 1) * P] for c in range(n // P)])

                    for j, (_, n) in enumerate(FF_GROUPS):
                        for kind, wn in (("h1", "w1"), ("h3", "w3")):
                            stream({(t, 0): (kind, j, t) for t in range(T)},
                                   [(wn, j, u) for u in range(2 if n > 256 else 1)], hTh, hTl, KC, lambda h, n=n: slice(0, n),
                                   pairs("f", 0) if (kind, j) == ("h1", 0) else {})
                            if kind == "h1" and j:
                                hidden_transposes(j - 1)

                    def last_hidden(u):
                        if u == 2:
                            hidden_transposes(len(FF_GROUPS) - 1)

                    stream({(t, h): ("y", t, h) for t in range(T) for h in range(2)},
                           [("w2", u) for u in range(FF_CHUNKS // 2)], ffTh, ffTl, FF_CHUNKS, side,
                           {4 * j: ("ht", j, 1) for j in range(len(FF_GROUPS))}, last_hidden)

            for t in range(T):
                b = begin(aux, ("router", t))
                for k in range(KC):
                    if t == 0 and k % 2 == 0:
                        pe.wait_ge(*aux.taken(("f", DEPTH - 1, k // 2)))
                    ins = pe.matmul(b[:, 0:N_EXP], h2T[:, k, t * P:(t + 1) * P], wr[:, k, :], start=(k == 0), stop=(k == KC - 1))
                ins.then_inc(aux_ready, 1)
            keep_warm(aux, ("slots",), 2)
            pe.wait_ge(chosen_ready, 1)
            b = begin(aux, ("slots",))
            pe.matmul(b[:, 0:8], lower[:, :], chosen[:, 0, :], start=True, stop=True)
            pe.matmul(b[:, 8:16], ones[:, :], chosen[:, 0, :], start=True, stop=False)
            pe.matmul(b[:, 8:16], lower[:, :], chosen[:, 1, :], start=False, stop=True)
            pe.matmul(b[:, 16:24], ones[:, :], chosen[:, 0, :], start=True, stop=False)
            pe.matmul(b[:, 16:24], ones[:, :], chosen[:, 1, :], start=False, stop=True).then_inc(aux_ready, 1)
            def gather(i, b):
                for c in range(2):
                    k = 2 * i + c
                    for t in range(T):
                        ins = pe.matmul(b[:, c * P:(c + 1) * P], xn[:, t, k * P:(k + 1) * P], pick[:, t, :],
                                        start=(t == 0), stop=(t == T - 1))
                ins.then_inc(aux_ready, 1)

            keep_warm(aux, ("x", 0), 2)
            pe.wait_ge(onehot_ready, 1)
            for i in range(4):
                gather(i, begin(aux, ("x", i)))
            keep_warm(acc, ("y0", 0), 3)
            for h in range(2):
                b = begin(acc, ("y0", h))
                pe.matmul(b[:, :], pickT[:, 0, :], xn[:, 0, h * W:(h + 1) * W], start=True, stop=True).then_inc(acc_ready, 1)
            pe.wait_ge(passes_ready, 1)
            pe.wait_ge(acc_taken["act"], acc.order.count("act") - 2)
            pe.wait_ge(acc_taken["dve"], acc.order.count("dve"))

            def combine(t, h, b):
                pe.matmul(b[:, :], pickT[:, t, :], ysb[:, h * W:(h + 1) * W], start=True, stop=True).then_inc(aux_ready, 1)

            passes = pe.value_load(n_pass[0:1, 0:1], min_val=1, max_val=2)
            with pe.Fori(0, passes) as ps:
                with pe.Fori(0, N_EXP) as e:
                    it = ps * N_EXP + e

                    def aux_fill(i):
                        pe.wait_ge(*e_free(AUXR, E_AUX, i, it))
                        return aux_bank[(AUX0 + i) % 4]

                    def acc_fill(i):
                        pe.wait_ge(*e_free(ACCR, E_ACC, i, it))
                        return acc_bank[(ACC0 + i) % 4]

                    pe.wait_ge(aux_taken["dve"], it * E_AUX.count("dve") + aux.order.count("dve"))

                    def expert_transposes(j):
                        pe.wait_ge(*e_taken(ACCR, E_ACC, 2 * j + 1, it))
                        b = aux_fill(HT[j])
                        for c in range(4):
                            ins = pe.transpose(b[:, c * P:(c + 1) * P], hidden[:, j % 2, c * P:(c + 1) * P], ident[:, :])
                        ins.then_inc(aux_ready, 1)

                    for j in range(E_GROUPS):
                        for side in range(2):
                            b = acc_fill(2 * j + side)
                            for k in range(KC):
                                u = 4 * j + 2 * side + k // 4
                                if k % 4 == 0:
                                    pe.wait_ge(low_split["dve"], it * E_UNITS + (LOW0 + u + 1))
                                wh, wl = e_parts(u, (4, W))
                                ins = three(b[:, :], xgTh[:, k, :], xgTl[:, k, :], wh[:, k % 4, :], wl[:, k % 4, :],
                                            k == 0, k == KC - 1)
                                if k == 3:
                                    ins.then_inc(unit_used, 1)
                            ins.then_inc(acc_ready, 1)
                            if side == 0 and j:
                                expert_transposes(j - 1)
                            if j == 1:
                                if side == 0:
                                    pe.wait_ge(acc_taken["act"], it * E_ACC.count("act") + acc.order.count("act"))
                                for h in range(2):
                                    combine(side, h, aux_fill(CB[2 * side + h]))
                            if j == 2 and side == 0:
                                b = aux_fill(PG)
                                for t in range(T):
                                    ins = pe.transpose(b[:, t * P:(t + 1) * P], pickg[:, t, :], ident[:, :])
                                ins.then_inc(aux_ready, 1)
                    pe.wait_ge(*e_taken(AUXR, E_AUX, HT[-2], it))
                    banks = [acc_fill(2 * E_GROUPS + h) for h in range(2)]
                    for c in range(E_CHUNKS):
                        u = 4 * E_GROUPS + c // 2
                        if c % 2 == 0:
                            pe.wait_ge(low_split["dve"], it * E_UNITS + (LOW0 + u + 1))
                        if c == 4 * (E_GROUPS - 1):
                            pe.wait_ge(*e_taken(AUXR, E_AUX, HT[-1], it))
                        wh, wl = e_parts(u, (2, D_MODEL))
                        for h in range(2):
                            m = slice(h * W, (h + 1) * W)
                            ins = three(banks[h][:, :], hidTh[:, c, :], hidTl[:, c, :], wh[:, c % 2, m], wl[:, c % 2, m],
                                        c == 0, c == E_CHUNKS - 1)
                            if c == E_CHUNKS - 1:
                                ins.then_inc(acc_ready, 1)
                        if c % 2 and c < E_CHUNKS - 1:
                            ins.then_inc(unit_used, 1)
                        if c == 3:
                            expert_transposes(E_GROUPS - 1)
                        if c == 2 * X_AFTER + 1:
                            pe.wait_ge(onehot_ready, it + 2)
                            for i in range(4):
                                gather(i, aux_fill(X0 + i))
            n_it = passes * N_EXP
            pe.wait_ge(acc_taken["act"], n_it * E_ACC.count("act") + acc.order.count("act"))
            for t in range(T):
                for h in range(2):
                    pe.wait_ge(*e_free(AUXR, E_AUX, 2 * t + h, n_it))
                    combine(t, h, aux_bank[(AUX0 + 2 * t + h) % 4])

        @block.sync
        def _(sp):
            def load_mla(l):
                sp.dma_start(uq[:, :, :], w["b_w_uq"][l].rearrange("(c p) n -> p c n", p=P)).then_inc(mla_loaded, 16)
                sp.dma_start(ukv[:, :], w["b_w_ukv"][l]).then_inc(mla_loaded, 16)

            for dst, src in rows_in:
                sp.dma_start(dst, src).then_inc(rows_loaded, 16)
            for t in range(T):
                sp.dma_start(x_sb[:, t, :], x_view[:, t, :]).then_inc(x_loaded[t], 16)
            for n, (name, src, shape) in enumerate(units):
                if n >= RAW:
                    sp.wait_ge(*low_done(n - RAW))
                if name == ("p", 0, 2, 0):
                    load_mla(0)
                if name == ("p", 1, 0, 0):
                    sp.wait_ge(aux_ready, aux.no(("ukv", 0, 1)))
                    load_mla(1)
                sp.dma_start(in_slot(raw, n % RAW, shape), src).then_inc(raw_loaded[n % RAW], 16)

            w1, w3 = (w[k][0].rearrange("e (c p) n -> e p c n", p=P) for k in ("moe_w1", "moe_w3"))
            w2 = w["moe_w2"][0].rearrange("e (c p) n -> e p c n", p=P)

            def expert_unit(u, e, it):
                sp.wait_ge(low_split["dve"], it * E_UNITS + (LOW0 + u + 1 - E_RAW))
                if u < 4 * E_GROUPS:
                    j, side, half = u // 4, u // 2 % 2, u % 2
                    src = (w1, w3)[side][bass.ds(e, 1), :, 4 * half:4 * half + 4, j * W:(j + 1) * W]
                    dst = in_slot(e_raw, u % E_RAW, (4, W))
                else:
                    c = 2 * (u - 4 * E_GROUPS)
                    src = w2[bass.ds(e, 1), :, c:c + 2, :]
                    dst = in_slot(e_raw, u % E_RAW, (2, D_MODEL))
                sp.dma_start(dst, src.rearrange("e p c n -> p (e c) n")).then_inc(e_raw_loaded[u % E_RAW], 16)

            sp.wait_ge(acc_ready, acc.no(("o", DEPTH - 1, 1, 1)))
            for u in range(E_RAW):
                expert_unit(u, 0, 0)
            sp.wait_ge(passes_ready, 1)
            more = sp.value_load(n_pass[0:1, 1:2], min_val=N_EXP - 1, max_val=2 * N_EXP - 1)
            with sp.Fori(0, more) as it:
                this, following = it & (N_EXP - 1), (it + 1) & (N_EXP - 1)
                for expert in (this, following):
                    sp.compute_val(expert * (D_MODEL * E_FF))
                    sp.compute_val(expert * (D_MODEL * E_FF) * 4)
                for u in range(E_RAW, E_UNITS):
                    expert_unit(u, this, it)
                for u in range(E_RAW):
                    expert_unit(u, following, it + 1)
            for u in range(E_RAW, E_UNITS):
                expert_unit(u, N_EXP - 1, more)
            n_it = more + 1
            done = len([r for r in E_AUX if r == "dve"])
            for t in range(T):
                sp.wait_ge(aux_taken["dve"], n_it * done + (aux.order.count("dve") + 2 * (t + 1)))
                sp.dma_start(out_view[:, t, :], x_sb[:, t, :]).then_inc(stored, 16)
            sp.wait_ge(stored, 16 * T)


_INS = ['x', 'positions', 'attn_norm_g', 'w_in', 'a_q_norm_g', 'a_k_norm_g', 'b_cq_norm_g', 'b_ckv_norm_g',
        'b_w_uq', 'b_w_ukv', 'b_qn_g', 'b_qr_g', 'b_kn_g', 'b_kr_g', 'c_q_norm_g', 'c_k_norm_g', 'c_sinks',
        'w_a_out', 'w_b_out', 'w_c_out', 'w_o', 'ffn_norm_g', 'ffn_w1', 'ffn_w3', 'ffn_w2',
        'router_w', 'moe_w1', 'moe_w3', 'moe_w2']


def kernel(**inputs):
    import numpy as _np
    import concourse.bacc as _bacc
    from concourse import mybir as _mybir
    from concourse.bass_utils import run_bass_kernel_spmd as _run

    nc = _bacc.Bacc("TRN2", target_bir_lowering=False, num_devices=1)
    arrays, args = {}, {}
    for name in _INS:
        a = _np.ascontiguousarray(inputs[name])
        arrays[f"in_{name}_dram"] = a
        args[name] = nc.dram_tensor(f"in_{name}_dram", a.shape, _mybir.dt.from_np(a.dtype), kind="ExternalInput").ap()
    out = nc.dram_tensor("out_0_dram", inputs["x"].shape, _mybir.dt.from_np(_np.dtype("float32")), kind="ExternalOutput").ap()
    hybrid_layers(nc, args, out)
    r = _run(nc, [arrays], core_ids=[0])
    return r.results[0]["out_0_dram"]
```
